# Optimizing a Trainium2 kernel written in Bass

```python
import math
import jax
import jax.numpy as jnp
from jax import lax
import numpy as np

D_MODEL = 1024
BATCH = 1
SEQ = 2048
DEPTH = 1
DEC_BATCH = 1
DEC_SEQ = 32
PAST_LEN = 128

CHUNK = 64
MIX_WIDTH = D_MODEL
DN_HEADS = 4
DN_KEY_DIM = 128
DN_VALUE_DIM = 128
CONV_W = 4
CONV_CH = DN_HEADS * (2 * DN_KEY_DIM + DN_VALUE_DIM)
DELTA_BLOCK = CHUNK
SB_HEADS = 8
SB_HEAD_DIM = 64
SB_QUERY_BLOCK = 128
N_GROUPS = 4
EXPERTS_PER_GROUP = 8
N_EXPERTS = N_GROUPS * EXPERTS_PER_GROUP
TOP_K = 2
D_EXPERT = D_MODEL // 2
MOE_BLOCK = 128
EPS = 1e-6

OFF_Q_A = 0
OFF_K_A = DN_HEADS * DN_KEY_DIM
OFF_V_A = 2 * DN_HEADS * DN_KEY_DIM
OFF_Z_A = CONV_CH
OFF_B_A = OFF_Z_A + DN_HEADS * DN_VALUE_DIM
OFF_G_A = OFF_B_A + DN_HEADS
OFF_Q_B = OFF_G_A + DN_HEADS
OFF_K_B = OFF_Q_B + SB_HEADS * SB_HEAD_DIM
OFF_V_B = OFF_K_B + SB_HEADS * SB_HEAD_DIM
IN_COLS = OFF_V_B + SB_HEADS * SB_HEAD_DIM
OUT_IN = DN_HEADS * DN_VALUE_DIM + SB_HEADS * SB_HEAD_DIM

kernel_name = 'hybrid_streaming_encoder_step'

def rms_norm(x, gain):
    xf = x.astype(jnp.float32)
    y = xf * lax.rsqrt(jnp.mean(xf * xf, axis=-1, keepdims=True) + EPS)
    return (y * gain.astype(jnp.float32)).astype(x.dtype)

def l2_normalize(x):
    xf = x.astype(jnp.float32)
    return xf * lax.rsqrt(jnp.sum(xf * xf, axis=-1, keepdims=True) + EPS)

def causal_conv(hist, w, t):
    out = hist[:, 0:t] * w[0]
    for i in range(1, CONV_W):
        out = out + hist[:, i:i + t] * w[i]
    return out

def gated_delta_rule(q, k, v, g, beta, s0):
    f32 = jnp.float32
    b, t, h, _ = q.shape
    dv = v.shape[-1]
    c = DELTA_BLOCK
    pad = (-t) % c
    n = (t + pad) // c

    def to_blocks(a):
        a = jnp.pad(a.astype(f32), [(0, 0), (0, pad)] + [(0, 0)] * (a.ndim - 2))
        a = a.reshape((b, n, c) + a.shape[2:])
        return jnp.moveaxis(a, 3, 1)

    qc, kc, vc, bc = to_blocks(q), to_blocks(k), to_blocks(v), to_blocks(beta)
    gc = lax.cumsum(to_blocks(g), axis=3)
    incl = jnp.tril(jnp.ones((c, c), bool))
    strict = jnp.tril(jnp.ones((c, c), bool), -1)
    decay = jnp.exp(jnp.where(incl, gc[..., :, None] - gc[..., None, :], -jnp.inf))
    kbeta = kc * bc[..., None]
    lower = jnp.where(strict, jnp.einsum('bhnid,bhnjd->bhnij', kbeta, kc) * decay, 0.0)
    rhs = jnp.concatenate([vc * bc[..., None], kbeta * jnp.exp(gc)[..., None]], axis=-1)
    sol = lax.linalg.triangular_solve(lower, rhs, left_side=True, lower=True, unit_diagonal=True)
    u, w = sol[..., :dv], sol[..., dv:]
    attn = jnp.where(incl, jnp.einsum('bhnid,bhnjd->bhnij', qc, kc) * decay, 0.0)
    q_dec = qc * jnp.exp(gc)[..., None]
    k_dec = kc * jnp.exp(gc[..., -1:] - gc)[..., None]
    a_blk = jnp.exp(gc[..., -1])

    def step(s, xs):
        q_i, k_i, u_i, w_i, at_i, a_i = xs
        v_new = u_i - jnp.einsum('bhck,bhkv->bhcv', w_i, s)
        o = jnp.einsum('bhck,bhkv->bhcv', q_i, s) + jnp.einsum('bhcj,bhjv->bhcv', at_i, v_new)
        s = s * a_i[..., None, None] + jnp.einsum('bhck,bhcv->bhkv', k_i, v_new)
        return s, o

    xs = (jnp.moveaxis(q_dec, 2, 0), jnp.moveaxis(k_dec, 2, 0), jnp.moveaxis(u, 2, 0),
          jnp.moveaxis(w, 2, 0), jnp.moveaxis(attn, 2, 0), jnp.moveaxis(a_blk, 2, 0))
    s_fin, o = lax.scan(step, s0.astype(f32), xs)
    o = o.transpose(1, 0, 3, 2, 4).reshape(b, n * c, h, dv)[:, :t]
    return o, s_fin

def sb_block(q, k, v, q_pos, k_pos):
    f32 = jnp.float32
    z = jnp.einsum('bqhd,bkhd->bhqk', q.astype(f32), k.astype(f32)) * (SB_HEAD_DIM ** -0.5)
    earlier = k_pos[None, :] < q_pos[:, None]
    log_keep = jnp.where(earlier, jax.nn.log_sigmoid(-z), 0.0)
    log_w = jax.nn.log_sigmoid(z) + lax.cumsum(log_keep, axis=3, reverse=True) - log_keep
    a = jnp.where(earlier, jnp.exp(log_w), 0.0)
    return jnp.einsum('bhqk,bkhd->bqhd', a, v.astype(f32))

def stick_breaking(q, k, v, q_pos, k_pos):
    b, t, h, d = q.shape
    if t % SB_QUERY_BLOCK != 0:
        return sb_block(q, k, v, q_pos, k_pos)
    n = t // SB_QUERY_BLOCK
    qs = q.reshape(b, n, SB_QUERY_BLOCK, h, d).transpose(1, 0, 2, 3, 4)
    ps = q_pos.reshape(n, SB_QUERY_BLOCK)
    out = lax.map(lambda a: sb_block(a[0], k, v, a[1], k_pos), (qs, ps))
    return out.transpose(1, 0, 2, 3, 4).reshape(b, t, h, d)

def hier_moe(h, p):
    f32 = jnp.float32
    b, t, d = h.shape
    n_tok = b * t
    m = n_tok * TOP_K
    x = h.reshape(n_tok, d)
    logit_g = (x @ p['w_router_group']).astype(f32) + p['b_router_group'].astype(f32)
    grp = jnp.argmax(logit_g, axis=-1)
    p_grp = jnp.take_along_axis(jax.nn.softmax(logit_g, axis=-1), grp[:, None], axis=1)[:, 0]
    logit_e = ((x @ p['w_router_expert']).astype(f32) + p['b_router_expert'].astype(f32)).reshape(
        n_tok, N_GROUPS, EXPERTS_PER_GROUP)
    logit_e = jnp.take_along_axis(logit_e, grp[:, None, None], axis=1)[:, 0]
    top_p, top_i = lax.top_k(jax.nn.softmax(logit_e, axis=-1), TOP_K)
    wts = (p_grp[:, None] * top_p / jnp.sum(top_p, axis=-1, keepdims=True)).reshape(m)
    eid = (grp[:, None] * EXPERTS_PER_GROUP + top_i).reshape(m)
    tok = jnp.arange(m, dtype=jnp.int32) // TOP_K
    order = jnp.argsort(eid)
    e_sorted = eid[order]
    counts = jnp.zeros((N_EXPERTS,), jnp.int32).at[eid].add(1)
    padded = (counts + MOE_BLOCK - 1) // MOE_BLOCK * MOE_BLOCK
    pad_end = jnp.cumsum(padded)
    pad_start = pad_end - padded
    start = jnp.cumsum(counts) - counts
    dest = pad_start[e_sorted] + jnp.arange(m, dtype=jnp.int32) - start[e_sorted]
    n_blocks = -(-m // MOE_BLOCK) + N_EXPERTS
    n_rows = n_blocks * MOE_BLOCK
    row_tok = jnp.full((n_rows,), n_tok, jnp.int32).at[dest].set(tok[order])
    row_w = jnp.zeros((n_rows,), f32).at[dest].set(wts[order])
    blk_e = jnp.minimum(jnp.searchsorted(pad_end, jnp.arange(n_blocks) * MOE_BLOCK, side='right'),
                        N_EXPERTS - 1)
    x_rows = jnp.concatenate([x, jnp.zeros((1, d), x.dtype)], axis=0)[row_tok].reshape(
        n_blocks, MOE_BLOCK, d)
    w_gate, w_up, w_down = p['w_gate'], p['w_up'], p['w_down']

    def expert_block(args):
        xb, e = args
        return (jax.nn.silu(xb @ w_gate[e]) * (xb @ w_up[e])) @ w_down[e]

    y_rows = lax.map(expert_block, (x_rows, blk_e)).reshape(n_rows, d)
    out = jnp.zeros((n_tok + 1, d), f32).at[row_tok].add(y_rows.astype(f32) * row_w[:, None])
    return out[:n_tok].reshape(b, t, d).astype(h.dtype)

def encoder_layer(x, c, conv_hist, s0, k_past, v_past, p):
    f32 = jnp.float32
    b, t, _ = x.shape
    past = 0 if k_past is None else k_past.shape[1]
    mod = jax.nn.silu(c) @ p['w_ada'] + p['b_ada']
    sh_m, sc_m, gt_m, sh_f, sc_f, gt_f = jnp.split(mod[:, None, :], 6, axis=-1)

    h = rms_norm(x, p['g_pre_mix']) * (1 + sc_m) + sh_m
    proj = h @ p['w_in']

    hist = jnp.concatenate([conv_hist.astype(proj.dtype), proj[..., :CONV_CH]], axis=1)
    conv = jax.nn.silu(causal_conv(hist, p['conv_w'], t))
    new_conv = hist[:, -(CONV_W - 1):]
    qa = l2_normalize(conv[..., OFF_Q_A:OFF_K_A].reshape(b, t, DN_HEADS, DN_KEY_DIM)) * (DN_KEY_DIM ** -0.5)
    ka = l2_normalize(conv[..., OFF_K_A:OFF_V_A].reshape(b, t, DN_HEADS, DN_KEY_DIM))
    va = conv[..., OFF_V_A:CONV_CH].reshape(b, t, DN_HEADS, DN_VALUE_DIM)
    za = proj[..., OFF_Z_A:OFF_B_A].reshape(b, t, DN_HEADS, DN_VALUE_DIM)
    beta = jax.nn.sigmoid(proj[..., OFF_B_A:OFF_G_A].astype(f32))
    g = -jnp.exp(p['a_log'].astype(f32)) * jax.nn.softplus(
        proj[..., OFF_G_A:OFF_Q_B].astype(f32) + p['dt_bias'].astype(f32))
    oa, s_new = gated_delta_rule(qa, ka, va, g, beta, s0)
    oa = rms_norm(oa, p['onorm_a']) * jax.nn.silu(za.astype(f32))

    qb = proj[..., OFF_Q_B:OFF_K_B].reshape(b, t, SB_HEADS, SB_HEAD_DIM)
    kb = proj[..., OFF_K_B:OFF_V_B].reshape(b, t, SB_HEADS, SB_HEAD_DIM)
    vb = proj[..., OFF_V_B:IN_COLS].reshape(b, t, SB_HEADS, SB_HEAD_DIM)
    if k_past is None:
        k_all, v_all = kb, vb
    else:
        k_all = jnp.concatenate([k_past.astype(kb.dtype), kb], axis=1)
        v_all = jnp.concatenate([v_past.astype(vb.dtype), vb], axis=1)
    ob = stick_breaking(qb, k_all, v_all, past + jnp.arange(t), jnp.arange(past + t))
    ob = rms_norm(ob, p['onorm_b'])

    merged = jnp.concatenate([oa.reshape(b, t, -1), ob.reshape(b, t, -1)], axis=-1).astype(x.dtype)
    x = x + gt_m * rms_norm(merged @ p['w_out'], p['g_post_mix'])

    h = rms_norm(x, p['g_pre_ffn']) * (1 + sc_f) + sh_f
    x = x + gt_f * rms_norm(hier_moe(h, p), p['g_post_ffn'])
    return x, kb, vb, s_new, new_conv

def setup_inputs(seed: int = 0) -> dict:
    key = jax.random.key(seed)
    ks = jax.random.split(key, 28)
    f32 = jnp.float32
    L, D = DEPTH, D_MODEL

    def normal(k, shape, scale):
        return jax.random.normal(k, shape, f32) * scale

    dt = jnp.exp(jax.random.uniform(ks[17], (L, DN_HEADS), f32, math.log(1e-3), math.log(1e-1)))
    return {
        'x_prompt': normal(ks[0], (BATCH, SEQ, D), 1.0),
        'x_sample': normal(ks[1], (DEC_BATCH, DEC_SEQ, D), 1.0),
        'c_prompt': normal(ks[2], (BATCH, D), 1.0),
        'c_sample': normal(ks[3], (DEC_BATCH, D), 1.0),
        'cache_k': normal(ks[4], (L, DEC_BATCH, PAST_LEN, SB_HEADS, SB_HEAD_DIM), 1.0),
        'cache_v': normal(ks[5], (L, DEC_BATCH, PAST_LEN, SB_HEADS, SB_HEAD_DIM), 1.0),
        'state_delta': normal(ks[6], (L, DEC_BATCH, DN_HEADS, DN_KEY_DIM, DN_VALUE_DIM), 0.5),
        'state_conv': normal(ks[7], (L, DEC_BATCH, CONV_W - 1, CONV_CH), 1.0),
        'w_ada': normal(ks[8], (L, D, 6 * D), 0.5 * D ** -0.5),
        'b_ada': normal(ks[9], (L, 6 * D), 0.01),
        'g_pre_mix': 1.0 + normal(ks[10], (L, D), 0.01),
        'g_post_mix': 1.0 + normal(ks[11], (L, D), 0.01),
        'g_pre_ffn': 1.0 + normal(ks[12], (L, D), 0.01),
        'g_post_ffn': 1.0 + normal(ks[13], (L, D), 0.01),
        'w_in': normal(ks[14], (L, D, IN_COLS), D ** -0.5),
        'conv_w': normal(ks[15], (L, CONV_W, CONV_CH), CONV_W ** -0.5),
        'a_log': jnp.log(jax.random.uniform(ks[16], (L, DN_HEADS), f32, 1.0, 16.0)),
        'dt_bias': dt + jnp.log(-jnp.expm1(-dt)),
        'onorm_a': 1.0 + normal(ks[18], (L, DN_VALUE_DIM), 0.01),
        'onorm_b': 1.0 + normal(ks[19], (L, SB_HEAD_DIM), 0.01),
        'w_out': normal(ks[20], (L, OUT_IN, D), OUT_IN ** -0.5),
        'w_router_group': normal(ks[21], (L, D, N_GROUPS), D ** -0.5),
        'b_router_group': normal(ks[22], (L, N_GROUPS), 0.01),
        'w_router_expert': normal(ks[23], (L, D, N_EXPERTS), D ** -0.5),
        'b_router_expert': normal(ks[24], (L, N_EXPERTS), 0.01),
        'w_gate': normal(ks[25], (L, N_EXPERTS, D, D_EXPERT), D ** -0.5),
        'w_up': normal(ks[26], (L, N_EXPERTS, D, D_EXPERT), D ** -0.5),
        'w_down': normal(ks[27], (L, N_EXPERTS, D_EXPERT, D), D_EXPERT ** -0.5),
    }

def reference(x_prompt, x_sample, c_prompt, c_sample, cache_k, cache_v, state_delta, state_conv,
              w_ada, b_ada, g_pre_mix, g_post_mix, g_pre_ffn, g_post_ffn, w_in, conv_w, a_log,
              dt_bias, onorm_a, onorm_b, w_out, w_router_group, b_router_group, w_router_expert,
              b_router_expert, w_gate, w_up, w_down):
    bp = x_prompt.shape[0]
    y_p, y_s = x_prompt, x_sample
    kp_l, vp_l, sp_l, cp_l, ks_l, vs_l, ss_l, cs_l = [], [], [], [], [], [], [], []
    for l in range(DEPTH):
        p = dict(w_ada=w_ada[l], b_ada=b_ada[l], g_pre_mix=g_pre_mix[l], g_post_mix=g_post_mix[l],
                 g_pre_ffn=g_pre_ffn[l], g_post_ffn=g_post_ffn[l], w_in=w_in[l], conv_w=conv_w[l],
                 a_log=a_log[l], dt_bias=dt_bias[l], onorm_a=onorm_a[l], onorm_b=onorm_b[l],
                 w_out=w_out[l], w_router_group=w_router_group[l], b_router_group=b_router_group[l],
                 w_router_expert=w_router_expert[l], b_router_expert=b_router_expert[l],
                 w_gate=w_gate[l], w_up=w_up[l], w_down=w_down[l])
        y_p, kp, vp, sp, cp = encoder_layer(
            y_p, c_prompt, jnp.zeros((bp, CONV_W - 1, CONV_CH), x_prompt.dtype),
            jnp.zeros((bp, DN_HEADS, DN_KEY_DIM, DN_VALUE_DIM), jnp.float32), None, None, p)
        y_s, k_s, v_s, s_s, c_s = encoder_layer(
            y_s, c_sample, state_conv[l], state_delta[l], cache_k[l], cache_v[l], p)
        kp_l.append(kp); vp_l.append(vp); sp_l.append(sp); cp_l.append(cp)
        ks_l.append(k_s); vs_l.append(v_s); ss_l.append(s_s); cs_l.append(c_s)
    return (y_p, y_s, jnp.stack(kp_l), jnp.stack(vp_l), jnp.stack(sp_l), jnp.stack(cp_l),
            jnp.stack(ks_l), jnp.stack(vs_l), jnp.stack(ss_l), jnp.stack(cs_l))


_drawn_inputs = setup_inputs


def setup_inputs(seed=0):
    import zlib

    import numpy as np

    out = dict(_drawn_inputs(seed))
    spreads = {}
    factors = {'g_pre_mix': 3.813,
     'g_post_mix': 3.282,
     'g_post_ffn': 8.0,
     'onorm_a': 3.587,
     'onorm_b': 3.077,
     'b_router_expert': 2.696}
    for name, (base, spread) in spreads.items():
        noise = np.random.default_rng([zlib.crc32(name.encode()), seed]).standard_normal(out[name].shape)
        drawn = base * np.exp(spread * noise) if base else spread * noise
        out[name] = jnp.asarray(drawn.astype(out[name].dtype))
    for name, factor in factors.items():
        out[name] = (out[name] * factor).astype(out[name].dtype)
    return out
```

```python
from contextlib import ExitStack

import concourse.bass as bass
from concourse import mybir

ALU = mybir.AluOpType
ACT = mybir.ActivationFunctionType
F32 = mybir.dt.float32
I32 = mybir.dt.int32
U32 = mybir.dt.uint32
AX = mybir.AxisListType.X

P = 128
EPS = 1e-6
CONV_W = 4
DN_HEADS = 4
DN_DIM = 128
SB_HEADS = 8
SB_DIM = 64


class Steps:

    def __init__(self, sem, eng, per):
        self.sem, self.eng, self.per, self.k, self.base = sem, eng, per, 0, 0

    def begin(self, turn):
        self.base, self.k = turn * self.per, 0

    def link(self, ins):
        self.k += 1
        assert self.k <= self.per, (self.sem, self.per)
        ins.then_inc(self.sem, 1)
        self.eng.wait_ge(self.sem, self.base + self.k)

    def end(self):
        assert self.k == self.per, (self.sem, self.k, self.per)


class Plan:
    pass


def build(nc, ins, outs):
    g = Plan()
    g.x = [ins["x_prompt"][0], ins["x_sample"][0]]
    g.SEQ, g.D = g.x[0].shape
    g.NEW = g.x[1].shape[0]
    g.KT = g.D // P
    g.TILES = g.SEQ // P
    g.CONV_CH = ins["conv_w"].shape[2]
    g.CT = g.CONV_CH // P
    g.IN_COLS = ins["w_in"].shape[2]
    g.ROWS = SB_HEADS * SB_DIM
    g.QKT = 2 * g.ROWS // P
    g.OFF_Z = g.CONV_CH
    g.OFF_B = g.OFF_Z + DN_HEADS * DN_DIM
    g.OFF_QB = g.OFF_B + 2 * DN_HEADS
    g.OFF_VB = g.OFF_QB + 2 * g.ROWS
    g.TOK = g.SEQ + g.NEW
    g.T17 = g.TILES + 1
    g.ins, g.outs, g.nc = ins, outs, nc
    with ExitStack() as life:
        g.sb = lambda name, shape, dt=F32, at=life: at.enter_context(nc.sbuf_tensor(name, shape, dt))
        g.psum = lambda name, shape, dt=F32, at=life: at.enter_context(nc.psum_tensor(name, shape, dt))
        g.sem = lambda name: life.enter_context(nc.semaphore(name))
        g.mod_d = nc.dram_tensor("mod_d", [2, 6 * g.D], F32, kind="Internal").ap()
        g.conv_d = nc.dram_tensor("conv_d", [g.CT, P, g.TOK], F32, kind="Internal").ap()
        g.qk_d = nc.dram_tensor("qk_d", [g.QKT, P, g.TOK], F32, kind="Internal").ap()
        g.z_d = nc.dram_tensor("z_d", [g.TOK, g.ROWS], F32, kind="Internal").ap()
        g.merged_d = nc.dram_tensor("merged_d", [g.TOK, DN_HEADS * DN_DIM + g.ROWS], F32, kind="Internal").ap()
        g.ident = g.sb("ident", [P, P])
        g.bg = g.sb("bg", [P, g.T17, 2 * DN_HEADS])
        g.modT = g.sb("modT", [P, 4 * g.KT])
        constants(nc, g)
        modulation(nc, g)
        projection(nc, g)
        g.ones = g.sb("ones", [P, P])
        g.half = g.sb("minus_half", [P, 2 * DN_HEADS])
        g.upto = g.sb("upto", [P, P])
        g.behind = g.sb("behind", [P, P])
        g.level = g.sb("level", [P, 8, P])
        g.GROUPS_E = g.ins["w_router_group"].shape[2]
        g.EXPERTS = g.ins["w_router_expert"].shape[2]
        g.BLOCKS = 2 * g.TOK // P + g.EXPERTS
        g.COLS = g.BLOCKS + 2
        g.x2_d = nc.dram_tensor("x2_d", [g.TOK, g.D], F32, kind="Internal").ap()
        g.h2_d = nc.dram_tensor("h2_d", [g.TOK + 1, g.D], F32, kind="Internal").ap()
        g.Y_BLOCKS = g.EXPERTS + -(-(g.BLOCKS - g.EXPERTS) // g.TILES) * g.TILES
        g.y_d = nc.dram_tensor("y_d", [g.Y_BLOCKS * P, g.D], F32, kind="Internal").ap()
        g.token_d = nc.dram_tensor("token_d", [P, g.COLS], I32, kind="Internal").ap()
        g.logits = g.sb("logits", [P, g.T17, g.GROUPS_E + g.EXPERTS])
        g.weight = g.sb("weight", [P, 2, g.T17])
        g.dest = g.sb("dest", [P, 2, g.T17], U32)
        g.slot = g.sb("slot", [P, 2, g.T17], U32)
        g.bounds = g.sb("bounds", [1, g.EXPERTS + 1], I32)
        masks(nc, g)
        delta(nc, g)
        with ExitStack() as until_mixed:
            R = g.EXPERTS + g.GROUPS_E
            g.w_out = g.sb("w_out", [P, g.KT, g.D], at=until_mixed)
            g.w_router = g.sb("w_router", [P, g.KT, R], at=until_mixed)
            g.b_router = g.sb("b_router", [P, R], at=until_mixed)
            g.post, g.scale, g.shift = ([g.sb(f"x_{n}{a}", [P, g.D], at=until_mixed) for a in range(2)] for n in ("post", "scale", "shift"))
            g.gains = g.sb("x_gains", [P, 2, g.D], at=until_mixed)
            g.s_w_mixed, g.s_rows_mixed = g.sem("x_w"), g.sem("x_rows")
            sticks(nc, g)
            mixed(nc, g)
        with ExitStack() as until_combine:
            F = ins["w_gate"].shape[3]
            g.expert_w = [g.sb("e_wg", [P, 2, g.KT, F], at=until_combine), g.sb("e_wu", [P, 2, g.KT, F], at=until_combine),
                          g.sb("e_wd", [P, 2, F // P, g.D], at=until_combine)]
            g.s_expert = [g.sem("e_wg0"), g.sem("e_wg1")], [g.sem("e_wd0"), g.sem("e_wd1")]
            routing(nc, g)
            experts(nc, g)
        combine(nc, g)


def constants(nc, g):
    s_cleared, s_ident = g.sem("s_cleared"), g.sem("s_ident")
    with nc.Block() as block:
        @block.gpsimd
        def _(pool):
            nc.gpsimd.memset(g.ident[:], 0.0).then_inc(s_cleared, 1)
            pool.wait_ge(s_cleared, 1)
            nc.gpsimd.affine_select(out=g.ident[:], in_=g.ident[:], compare_op=ALU.not_equal, fill=1.0,
                                    base=0, pattern=[[-1, P]], channel_multiplier=1).then_inc(s_ident, 1)
            nc.gpsimd.memset(g.bg[:], 0.0).then_inc(s_ident, 1)
            pool.wait_ge(s_ident, 2)


def masks(nc, g):
    s_set, s_tri = g.sem("k_set"), g.sem("k_tri")
    LEVELS = 7
    with nc.sbuf_tensor("row_no", [P, P], I32) as row_no, nc.sbuf_tensor("col_no", [P, P], I32) as col_no, \
            nc.sbuf_tensor("xor", [P, P], I32) as xor, nc.sbuf_tensor("xor_f", [P, P], F32) as xor_f, \
            nc.sbuf_tensor("below", [P, 2, P], F32) as below, nc.Block() as block:
        @block.vector
        def _(dve):
            link = Steps(g.sem("k_link"), dve, 2 + 3 * (LEVELS + 1))
            link.begin(0)
            dve.wait_ge(s_tri, 6)
            link.link(nc.vector.tensor_tensor(xor[:], row_no[:], col_no[:], ALU.bitwise_xor))
            link.link(nc.vector.tensor_copy(xor_f[:], xor[:]))
            for l in range(LEVELS + 1):
                low = 2 ** (l % LEVELS)
                link.link(nc.vector.tensor_scalar(g.level[:, l, :], xor_f[:], float(low), None, ALU.is_ge))
                link.link(nc.vector.scalar_tensor_tensor(out=g.level[:, l, :], in0=xor_f[:], scalar=float(2 * low), in1=g.level[:, l, :],
                                                         op0=ALU.is_lt, op1=ALU.mult))
                link.link(nc.vector.tensor_tensor(g.level[:, l, :], g.level[:, l, :], below[:, l // LEVELS, :], ALU.mult))

        @block.gpsimd
        def _(pool):
            nc.gpsimd.memset(g.half[:], -0.5).then_inc(s_set, 1)
            nc.gpsimd.memset(g.ones[:], 1.0).then_inc(s_set, 1)
            pool.wait_ge(s_set, 2)
            for out, sign, least in ((g.upto[:], -1, 0), (g.behind[:], 1, 1), (below[:, 0, :], 1, 1), (below[:, 1, :], -1, 1)):
                nc.gpsimd.affine_select(out=out, in_=g.ones[:], compare_op=ALU.is_ge, fill=0.0, base=-least,
                                        pattern=[[-sign, P]], channel_multiplier=sign).then_inc(s_tri, 1)
            nc.gpsimd.iota(row_no[:], pattern=[[0, P]], base=0, channel_multiplier=1).then_inc(s_tri, 1)
            nc.gpsimd.iota(col_no[:], pattern=[[1, P]], base=0, channel_multiplier=0).then_inc(s_tri, 1)


def modulation(nc, g):
    KT, D = g.KT, g.D
    WIDE = 512
    CHUNKS = 6 * D // WIDE
    w_ada = g.ins["w_ada"][0].rearrange("(k p) n -> p k n", p=P)
    s_c, s_w = g.sem("m_c"), [g.sem("m_w0"), g.sem("m_w1")]
    s_gain = g.sem("m_gain")
    s_silu, s_cT, s_cTs = g.sem("m_silu"), g.sem("m_cT"), g.sem("m_cTs")
    s_mm, s_add, s_row = g.sem("m_mm"), g.sem("m_add"), g.sem("m_row")
    s_tr, s_col = g.sem("m_tr"), g.sem("m_col")
    with ExitStack() as life:
        c_rows = g.sb("c_rows", [2, D], at=life)
        c_silu = g.sb("c_silu", [2, D], at=life)
        cT = g.sb("cT", [P, KT, 2], at=life)
        w = [g.sb(f"w_ada{b}", [P, KT, WIDE], at=life) for b in range(2)]
        bias = g.sb("b_ada2", [2, 6 * D], at=life)
        rows = g.sb("mod_rows", [2, 6 * D], at=life)
        gain_rows = g.sb("gain_rows", [KT, P], at=life)
        gain = g.sb("gain_cols", [P, KT], at=life)
        cols = g.sb("mod_cols", [P, 2 * KT, 2], at=life)
        p_c = g.psum("m_pc", [P, 512], at=life)
        p_mod = [g.psum(f"m_pm{b}", [2, WIDE], at=life) for b in range(2)]
        p_col = g.psum("m_pcol", [P, 512], at=life)
        with nc.Block() as block:
            @block.sync
            def _(sp):
                sp.dma_start(c_rows[0:1, :], g.ins["c_prompt"]).then_inc(s_c, 16)
                sp.dma_start(c_rows[1:2, :], g.ins["c_sample"]).then_inc(s_c, 16)
                for r in range(2):
                    sp.dma_start(bias[r:r + 1, :], g.ins["b_ada"]).then_inc(s_c, 16)
                sp.dma_start(gain_rows[:], g.ins["g_pre_mix"][0].rearrange("(k p) -> k p", p=P)).then_inc(s_gain, 16)
                for b in range(2):
                    sp.dma_start(w[b][:], w_ada[:, :, b * WIDE:(b + 1) * WIDE]).then_inc(s_w[b], 16)
                with sp.Fori(1, CHUNKS // 2) as i:
                    for b in range(2):
                        sp.wait_ge(s_mm, 2 * i - 1 + b)
                        sp.dma_start(w[b][:], w_ada[:, :, bass.ds(i * (2 * WIDE) + b * WIDE, WIDE)]).then_inc(s_w[b], 16)

            @block.scalar
            def _(act):
                act.wait_ge(s_c, 64)
                nc.scalar.activation(c_silu[:], c_rows[:], ACT.Silu).then_inc(s_silu, 1)
                act.wait_ge(s_add, CHUNKS)
                act.dma_start(g.mod_d, rows[:]).then_inc(s_row, 16)
                act.wait_ge(s_row, 16)

            @block.tensor
            def _(pe):
                pe.wait_ge(s_silu, 1)
                for k in range(KT):
                    last = nc.tensor.transpose(p_c[:, 2 * k:2 * k + 2], c_silu[:, k * P:(k + 1) * P], g.ident[0:2, 0:2])
                last.then_inc(s_cT, 1)
                pe.wait_ge(s_cTs, 1)

                def chunk(b):
                    for k in range(KT):
                        mm = nc.tensor.matmul(p_mod[b][:], cT[:, k, :], w[b][:, k, :], start=(k == 0), stop=(k == KT - 1))
                    mm.then_inc(s_mm, 1)

                for b in range(2):
                    pe.wait_ge(s_w[b], 16)
                    chunk(b)
                with pe.Fori(1, CHUNKS // 2) as i:
                    for b in range(2):
                        pe.wait_ge(s_w[b], 16 * i + 16)
                        pe.wait_ge(s_add, 2 * i - 1 + b)
                        chunk(b)
                pe.wait_ge(s_add, CHUNKS)
                for j in range(2 * KT):
                    nc.tensor.transpose(p_col[:, 2 * j:2 * j + 2], rows[:, j * P:(j + 1) * P], g.ident[0:2, 0:2])
                pe.wait_ge(s_gain, 16)
                nc.tensor.transpose(p_col[:, 4 * KT:5 * KT], gain_rows[:], g.ident[0:KT, 0:KT]).then_inc(s_tr, 1)

            @block.vector
            def _(dve):
                dve.wait_ge(s_cT, 1)
                nc.vector.tensor_copy(cT[:].rearrange("p k c -> p (k c)"), p_c[:, 0:2 * KT]).then_inc(s_cTs, 1)
                dve.wait_ge(s_c, 64)

                def add(b, at):
                    nc.vector.tensor_tensor(rows[:, at], p_mod[b][:], bias[:, at], ALU.add).then_inc(s_add, 1)

                with dve.Fori(0, CHUNKS // 2) as i:
                    for b in range(2):
                        dve.wait_ge(s_mm, 2 * i + 1 + b)
                        add(b, bass.ds(i * (2 * WIDE) + b * WIDE, WIDE))
                dve.wait_ge(s_tr, 1)
                nc.vector.tensor_copy(cols[:].rearrange("p k c -> p (k c)"), p_col[:, 0:4 * KT]).then_inc(s_col, 1)
                nc.vector.tensor_copy(gain[:], p_col[:, 4 * KT:5 * KT]).then_inc(s_col, 1)
                dve.wait_ge(s_col, 2)
                for grp in range(2):
                    at = grp * 2 * KT
                    nc.vector.scalar_tensor_tensor(out=g.modT[:, at:at + KT], in0=cols[:, KT:2 * KT, grp], scalar=1.0,
                                                   in1=gain[:], op0=ALU.add, op1=ALU.mult).then_inc(s_col, 1)
                    nc.vector.tensor_copy(g.modT[:, at + KT:at + 2 * KT], cols[:, 0:KT, grp]).then_inc(s_col, 1)
                dve.wait_ge(s_col, 6)


def projection(nc, g):
    KT, D, CT, QKT, NEW = g.KT, g.D, g.CT, g.QKT, g.NEW
    SLAB = 512
    TT = SLAB // P
    SLABS = g.SEQ // SLAB
    HIST = CONV_W - 1
    T_GROUPS = CT + QKT
    R_GROUPS = 2 * TT
    GROUPS = T_GROUPS + R_GROUPS
    BANKS = 3
    KTILES = QKT // 2
    w_in = g.ins["w_in"][0].rearrange("(k p) n -> p k n", p=P)
    s_w, s_small = g.sem("p_w"), g.sem("p_small")
    s_x, s_sq, s_std, s_xn = [g.sem(f"p_x{t}") for t in range(TT)], g.sem("p_sq"), g.sem("p_std"), g.sem("p_xn")
    s_xt, s_h, s_mm, s_ev = g.sem("p_xt"), g.sem("p_h"), g.sem("p_mm"), g.sem("p_ev")
    s_bgm, s_bg, s_link, s_silu = g.sem("p_bgm"), g.sem("p_bg"), g.sem("p_link"), g.sem("p_silu")
    s_kt, s_kr, s_carry, s_tail = g.sem("p_kt"), g.sem("p_kr"), g.sem("p_carry"), g.sem("p_tail")
    CHAIN = 1 + CONV_W * CT
    s_co, s_qo = [g.sem("p_co0"), g.sem("p_co1")], [g.sem(f"p_qo{b}") for b in range(4)]
    s_zo, s_vo, s_ko, s_to, s_trt, s_wc = g.sem("p_zo"), g.sem("p_vo"), g.sem("p_ko"), g.sem("p_to"), g.sem("p_trt"), g.sem("p_wc")
    with ExitStack() as life:
        w = g.sb("w_in", [P, KT, g.IN_COLS], at=life)
        x = g.sb("x_in", [P, TT, D], at=life)
        hT = g.sb("hT", [P, KT, SLAB], at=life)
        junk = g.sb("junk", [P, D], at=life)
        sq = g.sb("sq", [P, TT], at=life)
        std = g.sb("std", [P, TT], at=life)
        rstd = g.sb("rstd", [P, TT], at=life)
        raw = g.sb("raw", [P, CT, HIST + SLAB], at=life)
        acc = g.sb("conv_acc", [P, 2, SLAB], at=life)
        conv = g.sb("conv_out", [P, 2, SLAB], at=life)
        qk = g.sb("qk_out", [P, 4, SLAB], at=life)
        zv = g.sb("zv_out", [P, 4, g.ROWS], at=life)
        krow = g.sb("k_rows", [P, TT, g.ROWS], at=life)
        small = krow[0:HIST + CONV_W].rearrange("p t n -> p (t n)")[:, 0:g.CONV_CH]
        cw = g.sb("conv_cols", [P, CT, HIST + CONV_W], at=life)
        tail = g.sb("tail", [P, CT, 2 * HIST], at=life)
        tail_rows = x[0:2 * HIST].rearrange("p t n -> p (t n)")[:, 0:g.CONV_CH]
        eps = g.sb("eps_p", [P, 1], at=life)
        p_x = g.psum("p_px", [P, KT, P], at=life)
        p_mm = [g.psum(f"p_pm{b}", [P, 512], at=life) for b in range(BANKS)]
        p_bg = g.psum("p_pbg", [P, 512], at=life)
        p_kt = [g.psum(f"p_pk{b}", [P, TT, P], at=life) for b in range(2)]

        def slab_shape(turn):
            return (1, NEW, 1, NEW) if isinstance(turn, int) and turn == 0 else (0, P, TT, SLAB)

        def tokens(turn, n):
            return bass.ds(g.SEQ, n) if isinstance(turn, int) else bass.ds((turn - 1) * SLAB, n)

        def last_of(tiles, zi):
            return 1 + 2 * (TT - tiles) * zi

        def slabs(eng, body):
            body(0)
            with eng.Fori(1, SLABS + 1) as turn:
                body(turn)

        with nc.Block() as block:
            @block.sync
            def _(sp):
                sp.dma_start(small[0:HIST, :], g.ins["state_conv"][0, 0]).then_inc(s_small, 16)
                sp.dma_start(small[HIST:, :], g.ins["conv_w"][0]).then_inc(s_small, 16)

                def load_x(turn):
                    grp, rows, tiles, _ = slab_shape(turn)
                    for t in range(TT):
                        if not isinstance(turn, int):
                            sp.wait_ge(s_xt, turn * TT)
                        if t < tiles:
                            src = g.x[1] if grp else g.x[0][bass.ds((turn - 1) * SLAB + t * P, P), :]
                            sp.dma_start(x[0:rows, t, :], src).then_inc(s_x[t], 16)

                load_x(0)
                for k in range(KT):
                    sp.dma_start(w[:, k, :], w_in[:, k, :]).then_inc(s_w, 16)
                with sp.Fori(1, SLABS + 1) as turn:
                    load_x(turn)

            @block.scalar
            def _(act):
                def body(turn):
                    grp, rows, tiles, n = slab_shape(turn)
                    for t in range(tiles):
                        act.wait_ge(s_x[t], (turn + (t == 0)) * 16)
                        if t or not grp:
                            act.wait_ge(s_sq, turn * TT + t)
                        nc.scalar.activation(junk[0:rows, :], x[0:rows, t, :], ACT.Square,
                                             accum_out=sq[0:rows, t:t + 1]).then_inc(s_sq, TT // tiles)
                    if isinstance(turn, int):
                        act.wait_ge(s_wc, 2)
                    act.wait_ge(s_sq, (turn + 1) * TT)
                    if not isinstance(turn, int):
                        act.wait_ge(s_link, (turn - 1) * CHAIN + 1)
                    nc.scalar.activation(std[0:rows, 0:tiles], sq[0:rows, 0:tiles], ACT.Sqrt, bias=eps[0:rows, :],
                                         scale=1.0 / D).then_inc(s_std, 1)
                    for j in range(T_GROUPS):
                        act.wait_ge(s_mm, turn * GROUPS + j + 1)
                        bank = p_mm[j % BANKS]
                        if j < CT:
                            if j == 0:
                                act.wait_ge(s_carry, turn + 1)
                            nc.scalar.copy(raw[:, j, HIST:HIST + n], bank[:, 0:n]).then_inc(s_ev, 1)
                        else:
                            q = (j - CT) % 4
                            stores = 2 * turn + (j - CT) // 4
                            if not (isinstance(turn, int) and j - CT < 4):
                                act.wait_ge(s_qo[q], stores * 16)
                            if j - CT < 4 and not isinstance(turn, int):
                                act.wait_ge(s_kt, turn * KTILES)
                            nc.scalar.copy(qk[:, q, 0:n], bank[:, 0:n]).then_inc(s_ev, 1)
                            act.wait_ge(s_ev, turn * GROUPS + j + 1)
                            act.dma_start(g.qk_d[j - CT, :, tokens(turn, n)], qk[:, q, 0:n]).then_inc(s_qo[q], 16)
                    for t in range(TT):
                        for zi in range(2):
                            k = T_GROUPS + 2 * t + zi
                            done = s_vo if zi else s_zo
                            if t >= tiles:
                                continue
                            slot = 2 * (t % 2) + zi
                            act.wait_ge(s_mm, turn * GROUPS + k + 1)
                            if not grp:
                                act.wait_ge(done, (1 + (turn - 1) * TT + t) * 16)
                            nc.scalar.activation(zv[0:rows, slot, :], p_mm[k % BANKS][0:rows, :],
                                                 ACT.Copy if zi else ACT.Silu).then_inc(s_ev, last_of(tiles, zi))
                            if grp:
                                dst = g.outs["v_sample"] if zi else g.z_d[g.SEQ:g.TOK, :]
                            else:
                                dst = (g.outs["v_prompt"] if zi else g.z_d)[bass.ds((turn - 1) * SLAB + t * P, P), :]
                            act.wait_ge(s_ev, turn * GROUPS + T_GROUPS + 2 * t + zi + last_of(tiles, zi))
                            act.dma_start(dst, zv[0:rows, slot, :]).then_inc(done, 16)
                    for c in range(CT):
                        act.wait_ge(s_link, turn * CHAIN + 1 + CONV_W * (c + 1))
                        stored = turn * (CT // 2) + c // 2
                        if not isinstance(stored, int) or stored > 0:
                            act.wait_ge(s_co[c % 2], stored * 16)
                        nc.scalar.activation(conv[:, c % 2, 0:n], acc[:, c % 2, 0:n], ACT.Silu).then_inc(s_silu, 1)
                        act.wait_ge(s_silu, turn * CT + c + 1)
                        act.dma_start(g.conv_d[c, :, tokens(turn, n)], conv[:, c % 2, 0:n]).then_inc(s_co[c % 2], 16)
                    act.wait_ge(s_kr, (turn + 1) * KTILES)
                    if grp:
                        act.dma_start(g.outs["k_sample"], krow[0:rows, 0, :]).then_inc(s_ko, 16)
                    else:
                        act.dma_start(g.outs["k_prompt"][bass.ds((turn - 1) * SLAB, SLAB), :].rearrange("(t p) n -> p t n", p=P),
                                      krow[:]).then_inc(s_ko, 16)

                slabs(act, body)
                act.wait_ge(s_tail, 2 + CT // 4)
                act.dma_start(g.outs["conv_prompt"], tail_rows[0:HIST, :]).then_inc(s_to, 16)
                act.dma_start(g.outs["conv_sample"], tail_rows[HIST:, :]).then_inc(s_to, 16)
                turns = SLABS + 1
                act.wait_ge(s_to, 32)
                act.wait_ge(s_ko, turns * 16)
                act.wait_ge(s_zo, (1 + g.TILES) * 16)
                act.wait_ge(s_vo, (1 + g.TILES) * 16)
                for s in s_co:
                    act.wait_ge(s, turns * (CT // 2) * 16)
                for s in s_qo:
                    act.wait_ge(s, turns * (QKT // 4) * 16)

            @block.tensor
            def _(pe):
                pe.wait_ge(s_small, 32)
                for c in range(CT):
                    last = nc.tensor.transpose(p_kt[0][:].rearrange("p t n -> p (t n)")[:, 8 * c:8 * c + HIST + CONV_W],
                                               small[:, c * P:(c + 1) * P], g.ident[0:HIST + CONV_W, 0:HIST + CONV_W])
                last.then_inc(s_trt, 1)

                def body(turn):
                    grp, rows, tiles, n = slab_shape(turn)
                    for t in range(tiles):
                        pe.wait_ge(s_xn, turn * TT + t + 1)
                        before = turn * TT + t
                        if not isinstance(before, int) or before > 0:
                            pe.wait_ge(s_h, before)
                        for k in range(KT):
                            last = nc.tensor.transpose(p_x[:, k, 0:rows], x[0:rows, t, k * P:(k + 1) * P], g.ident[0:rows, 0:rows])
                        last.then_inc(s_xt, TT // tiles)
                    pe.wait_ge(s_h, (turn + 1) * TT)
                    if isinstance(turn, int):
                        pe.wait_ge(s_w, 16 * KT)

                    def bank_free(k):
                        free = turn * GROUPS + k + 1 - BANKS
                        if not isinstance(free, int) or free > 0:
                            pe.wait_ge(s_ev, free)

                    for j in range(T_GROUPS):
                        col = j * P if j < CT else g.OFF_QB + (j - CT) * P
                        bank_free(j)
                        for k in range(KT):
                            mm = nc.tensor.matmul(p_mm[j % BANKS][:, 0:n], w[:, k, col:col + P], hT[:, k, 0:n],
                                                  start=(k == 0), stop=(k == KT - 1))
                        mm.then_inc(s_mm, 1)
                    for t in range(TT):
                        for zi in range(2):
                            k2 = T_GROUPS + 2 * t + zi
                            if t >= tiles:
                                continue
                            col = g.OFF_VB if zi else g.OFF_Z
                            bank_free(k2)
                            for k in range(KT):
                                mm = nc.tensor.matmul(p_mm[k2 % BANKS][0:rows, :], hT[:, k, t * P:t * P + rows],
                                                      w[:, k, col:col + g.ROWS], start=(k == 0), stop=(k == KT - 1))
                            mm.then_inc(s_mm, last_of(tiles, zi))
                    if not isinstance(turn, int):
                        pe.wait_ge(s_bg, turn)
                    for t in range(tiles):
                        for k in range(KT):
                            mm = nc.tensor.matmul(p_bg[0:rows, 8 * t:8 * t + 8], hT[:, k, t * P:t * P + rows],
                                                  w[:, k, g.OFF_B:g.OFF_QB], start=(k == 0), stop=(k == KT - 1))
                    mm.then_inc(s_bgm, 1)
                    for c in range(KTILES):
                        pe.wait_ge(s_ev, turn * GROUPS + CT + KTILES + c + 1)
                        free = turn * KTILES + c - 1
                        if c < 1 or c < 2:
                            if isinstance(turn, int):
                                pe.wait_ge(s_wc, 2)
                        if not isinstance(free, int) or free > 0:
                            pe.wait_ge(s_kr, free)
                        for t in range(tiles):
                            tr = nc.tensor.transpose(p_kt[c % 2][0:rows, t, :], qk[:, c, t * P:t * P + rows], g.ident[:])
                        tr.then_inc(s_kt, 1)

                slabs(pe, body)
                pe.wait_ge(s_tail, 2)
                pe.wait_ge(s_ev, (SLABS + 1) * GROUPS)
                for c in range(CT):
                    last = nc.tensor.transpose(p_mm[c // 4][0:2 * HIST, (c % 4) * P:(c % 4 + 1) * P], tail[:, c, :], g.ident[:])
                last.then_inc(s_trt, 1)

            @block.vector
            def _(dve):
                link = Steps(s_link, dve, CHAIN)
                nc.vector.memset(eps[:], EPS).then_inc(s_wc, 1)
                dve.wait_ge(s_trt, 1)
                nc.vector.tensor_copy(cw[:], p_kt[0][:].rearrange("p t n -> p (t n)")[:, 0:8 * CT]
                                      .rearrange("p (c e) -> p c e", e=8)[:, :, 0:HIST + CONV_W]).then_inc(s_wc, 1)
                dve.wait_ge(s_wc, 2)
                nc.vector.tensor_copy(raw[:, :, 0:HIST], cw[:, :, 0:HIST]).then_inc(s_carry, 1)

                def body(turn):
                    grp, rows, tiles, n = slab_shape(turn)
                    link.begin(turn)
                    dve.wait_ge(s_std, turn + 1)
                    rec = nc.vector.reciprocal(rstd[0:rows, 0:tiles], std[0:rows, 0:tiles])
                    link.link(rec)
                    for t in range(tiles):
                        nc.vector.tensor_scalar(x[0:rows, t, :], x[0:rows, t, :], rstd[0:rows, t:t + 1], None,
                                                ALU.mult).then_inc(s_xn, TT // tiles)
                    if not isinstance(turn, int):
                        dve.wait_ge(s_bgm, turn)
                    for t in range(tiles):
                        dve.wait_ge(s_xt, turn * TT + t + 1)
                        for k in range(KT):
                            at = grp * 2 * KT + k
                            last = nc.vector.tensor_scalar(hT[:, k, t * P:t * P + rows], p_x[:, k, 0:rows],
                                                           g.modT[:, at:at + 1], g.modT[:, at + KT:at + KT + 1],
                                                           ALU.mult, ALU.add)
                        last.then_inc(s_h, TT // tiles)
                    for c in range(CT):
                        dve.wait_ge(s_ev, turn * GROUPS + c + 1)
                        used = turn * CT + c - 1
                        if not isinstance(used, int) or used > 0:
                            dve.wait_ge(s_silu, used)
                        a = acc[:, c % 2, 0:n]
                        link.link(nc.vector.tensor_scalar(a, raw[:, c, 0:n], cw[:, c, HIST:HIST + 1], None, ALU.mult))
                        for i in range(1, CONV_W):
                            step = nc.vector.scalar_tensor_tensor(out=a, in0=raw[:, c, i:i + n], scalar=cw[:, c, HIST + i:HIST + i + 1],
                                                                  in1=a, op0=ALU.mult, op1=ALU.add)
                            link.link(step)
                    if isinstance(turn, int):
                        nc.vector.tensor_copy(tail[:, :, HIST:2 * HIST], raw[:, :, n:n + HIST]).then_inc(s_tail, 1)
                        nc.vector.memset(raw[:, :, 0:HIST], 0.0).then_inc(s_carry, 1)
                    else:
                        nc.vector.tensor_copy(raw[:, :, 0:HIST], raw[:, :, n:n + HIST]).then_inc(s_carry, 1)
                    dve.wait_ge(s_bgm, turn + 1)
                    first = g.TILES if isinstance(turn, int) else (turn - 1) * TT
                    nc.vector.tensor_copy(g.bg[0:rows, bass.ds(first, tiles), :],
                                          p_bg[0:rows, 0:8 * tiles].rearrange("p (t c) -> p t c", c=8)).then_inc(s_bg, 1)
                    for c in range(KTILES):
                        dve.wait_ge(s_kt, turn * KTILES + c + 1)
                        if c == 0 and not isinstance(turn, int):
                            dve.wait_ge(s_ko, turn * 16)
                        nc.vector.tensor_copy(krow[0:rows, 0:tiles, c * P:(c + 1) * P], p_kt[c % 2][0:rows, 0:tiles, :]).then_inc(s_kr, 1)
                    link.end()

                slabs(dve, body)
                dve.wait_ge(s_carry, SLABS + 2)
                nc.vector.tensor_copy(tail[:, :, 0:HIST], raw[:, :, 0:HIST]).then_inc(s_tail, 1)
                dve.wait_ge(s_trt, 2)
                for b in range(CT // 4):
                    nc.vector.tensor_copy(tail_rows[:, b * 512:(b + 1) * 512], p_mm[b][0:2 * HIST, :]).then_inc(s_tail, 1)


class Line:

    def __init__(self, sem, steps):
        self.sem, self.steps, self.at = sem, list(steps), 0

    def __call__(self, turn, step):
        return turn * len(self.steps) + self.steps.index(step) + 1

    def did(self, step):
        assert self.steps[self.at % len(self.steps)] == step, (step, self.steps[self.at % len(self.steps)])
        self.at += 1
        return 1


def wide(ap, *shape):
    if len(ap.shape) == 3:
        return ap.to_broadcast(list(shape))
    axis = 2 if ap.shape[1] == shape[1] and ap.shape[1] != shape[2] else 1
    return ap.unsqueeze(axis).to_broadcast(list(shape))


def delta(nc, g):
    H, DD, NEW = DN_HEADS, DN_DIM, g.NEW
    LEVELS = 7
    s_in, s_z, s_par, s_s0 = g.sem("d_in"), g.sem("d_z"), g.sem("d_par"), g.sem("d_s0")
    s_out, s_sout, s_pre, s_exp = g.sem("d_out"), g.sem("d_sout"), g.sem("d_pre"), g.sem("d_exp")
    halves = [(l, h) for l in range(1, LEVELS) for h in range(2)]
    by_pe = Line(g.sem("d_pe"), ["rows", "sums", "decay", "knT", "kbT", "qnT", "qdT", "kk", "kq", "L"]
                 + [f"{a}{l}{h}" for l in range(1, LEVELS) for a in ("LT", "TLT") for h in range(2)]
                 + ["u", "wT", "wS", "qS", "aV", "kV"])
    by_act = Line(g.sem("d_act"), ["squares", "e_rows", "e_all", "decay", "knT", "kbT", "qnT", "qdT", "wT", "o_sq"])
    by_dve = Line(g.sem("d_dve"), ["bg", "sum_sq", "q_sq", "k_sq", "kn", "qn", "vb", "LT", "AT", "B0", "T0"]
                  + [f"{a}{l}{h}" for l in range(1, LEVELS) for a in ("m", "T") for h in range(2)]
                  + ["v_new", "state", "o_sum", "o_eps", "o_n", "o_g", "o_z"])
    by_pool = Line(g.sem("d_pool"), ["g_mask", "r", "kb", "qd", "kbe", "kd", "D", "B0T", "T0T", "S_dec", "o_r"])
    with ExitStack() as life:
        ct = g.sb("d_ct", [P, 3 * H, P], at=life)
        zt = g.sb("d_zt", [P, H, DD], at=life)
        par = g.sb("d_param", [P, 2, H], at=life)
        gain = g.sb("d_gain", [P, DD], at=life)
        sp_in = g.sb("d_sp", [P, g.T17, H], at=life)
        sp_abs = g.sb("d_spabs", [P, g.T17, H], at=life)
        bgt = g.sb("d_bg", [P, 2 * H], at=life)
        sq = g.sb("d_sq", [P, 2 * H, DD], at=life)
        ss = g.sb("d_ss", [P, 2 * H], at=life)
        ssn = g.sb("d_ssn", [P, 2 * H], at=life)
        r = g.sb("d_r", [P, 2 * H], at=life)
        e_rows = g.sb("d_er", [P, 2, H], at=life)
        e_all = g.sb("d_ea", [P, H], at=life)
        gm = g.sb("d_gm", [P, H, P], at=life)
        dec = g.sb("d_dec", [P, H, P], at=life)
        dm = g.sb("d_dm", [P, H, P], at=life)
        kn, qn, vb, kb, qd, kbe, kd = (g.sb("d_" + n, [P, H, DD], at=life) for n in ("kn", "qn", "vb", "kb", "qd", "kbe", "kd"))
        knT, kbT, qnT, qdT, wT = (g.sb("d_" + n, [P, H, P], at=life) for n in ("knT", "kbT", "qnT", "qdT", "wT"))
        LT, AT, T, TT, B, BT = (g.sb("d_" + n, [P, H, P], at=life) for n in ("LT", "AT", "T", "TT", "B", "BT"))
        M = g.sb("d_m", [P, H, P], at=life)
        vn = g.sb("d_vn", [P, H, DD], at=life)
        S = g.sb("d_S", [P, H, DD], at=life)
        osq = g.sb("d_osq", [P, H, DD], at=life)
        oss = g.sb("d_oss", [P, H], at=life)
        osn = g.sb("d_osn", [P, H], at=life)
        orr = g.sb("d_orr", [P, H], at=life)
        o = g.sb("d_o", [P, H, DD], at=life)
        og = g.sb("d_og", [P, H, DD], at=life)
        oz = g.sb("d_oz", [P, H, DD], at=life)
        zero = g.sb("d_zero", [P, g.D], at=life)
        s_zero, s_zeros = g.sem("d_zero_set"), g.sem("d_zeros")
        FILL = -(-(g.BLOCKS - g.EXPERTS) // g.TILES)
        X = [g.psum(f"d_x{i}", [P, H, P], at=life) for i in range(4)]
        P1 = [g.psum(f"d_p1{i}", [P, H, P], at=life) for i in range(2)]
        P2 = [g.psum(f"d_p2{i}", [P, 2, 2, P], at=life) for i in range(2)]

        def turns(eng, body):
            body(0)
            with eng.Fori(1, g.TILES + 1) as turn:
                body(turn)

        def shape(turn):
            first = isinstance(turn, int)
            n = NEW if first else P
            return not first, n, (g.TILES if first else turn - 1), (slice(g.SEQ, g.TOK) if first else bass.ds((turn - 1) * P, P))

        with nc.Block() as block:
            @block.sync
            def _(sp):
                for i, name in enumerate(["a_log", "dt_bias"]):
                    sp.dma_start(par[:, i, :], g.ins[name][0].partition_broadcast(P)).then_inc(s_par, 16)
                sp.dma_start(gain[:], g.ins["onorm_a"][0].partition_broadcast(P)).then_inc(s_par, 16)
                sp.dma_start(S[:], g.ins["state_delta"][0, 0].rearrange("h k v -> k h v")).then_inc(s_s0, 16)

                def body(turn):
                    later, n, tile, at = shape(turn)
                    if later:
                        sp.wait_ge(by_pe.sem, by_pe(turn - 1, "rows"))
                    sp.dma_start(ct[:, :, 0:n], g.conv_d[:, :, at].rearrange("c p t -> p c t")).then_inc(s_in, 16)
                    if later:
                        sp.wait_ge(by_dve.sem, by_dve(turn - 1, "o_z"))
                    sp.dma_start(zt[0:n].rearrange("p h d -> p (h d)"), g.z_d[at, :]).then_inc(s_z, 16)
                    if later:
                        sp.dma_start(g.y_d[bass.ds((turn - 1) * FILL * P + g.EXPERTS * P, FILL * P), :].rearrange("(b p) d -> p b d", p=P),
                                     zero[:].unsqueeze(1).to_broadcast([P, FILL, g.D])).then_inc(s_zeros, 16)

                body(0)
                sp.wait_ge(s_zero, 1)
                sp.dma_start(g.h2_d[g.TOK:g.TOK + 1, :], zero[0:1]).then_inc(s_zeros, 16)
                with sp.Fori(1, g.TILES + 1) as turn:
                    body(turn)
                sp.wait_ge(s_zeros, (1 + g.TILES) * 16)

            @block.scalar
            def _(act):
                act.wait_ge(s_pre, 1)
                nc.scalar.activation(sp_abs[:], sp_abs[:], ACT.Exp, scale=-1.0).then_inc(s_exp, 1)
                nc.scalar.activation(g.bg[:, :, 0:H], g.bg[:, :, 0:H], ACT.Exp, scale=-1.0).then_inc(s_exp, 1)
                act.wait_ge(s_par, 48)
                nc.scalar.activation(par[:, 0, :], par[:, 0, :], ACT.Exp).then_inc(s_exp, 1)
                act.wait_ge(s_exp, 3)
                nc.scalar.activation(sp_abs[:], sp_abs[:], ACT.Ln, bias=1.0).then_inc(s_exp, 1)

                def body(turn):
                    later, n, tile, at = shape(turn)
                    act.wait_ge(by_pe.sem, by_pe(turn, "rows"))
                    if later:
                        act.wait_ge(by_dve.sem, by_dve(turn - 1, "sum_sq"))
                        act.wait_ge(by_act.sem, by_act(turn - 1, "squares"))
                    nc.scalar.activation(sq[0:n, 0:H], X[0][0:n], ACT.Square)
                    nc.scalar.activation(sq[0:n, H:2 * H], X[1][0:n], ACT.Square).then_inc(by_act.sem, by_act.did("squares"))
                    act.wait_ge(by_pe.sem, by_pe(turn, "sums"))
                    if later:
                        act.wait_ge(by_pool.sem, by_pool(turn - 1, "S_dec"))
                        act.wait_ge(by_act.sem, by_act(turn - 1, "e_all"))
                    sums = X[3][:].rearrange("p h d -> p (h d)")
                    nc.scalar.activation(e_rows[0:n].rearrange("p a h -> p (a h)"), sums[0:n, 0:2 * H], ACT.Exp).then_inc(by_act.sem, by_act.did("e_rows"))
                    nc.scalar.activation(e_all[:], sums[:, 2 * H:3 * H], ACT.Exp).then_inc(by_act.sem, by_act.did("e_all"))
                    act.wait_ge(by_pe.sem, by_pe(turn, "decay"))
                    if later:
                        act.wait_ge(by_pool.sem, by_pool(turn - 1, "D"))
                        act.wait_ge(by_act.sem, by_act(turn - 1, "decay"))
                    nc.scalar.activation(dec[0:n, :, 0:n], P2[0][:].rearrange("p a b n -> p (a b) n")[0:n, :, 0:n], ACT.Exp).then_inc(by_act.sem, by_act.did("decay"))
                    for name, src, dst, reader in (("knT", P1[0][:], knT, "kq"), ("kbT", P1[1][:], kbT, "kk"),
                                                   ("qnT", P2[0][:].rearrange("p a b n -> p (a b) n"), qnT, "kq"),
                                                   ("qdT", P2[1][:].rearrange("p a b n -> p (a b) n"), qdT, "qS")):
                        act.wait_ge(by_pe.sem, by_pe(turn, name))
                        if later:
                            act.wait_ge(by_pe.sem, by_pe(turn - 1, reader))
                            act.wait_ge(by_act.sem, by_act(turn - 1, name))
                        nc.scalar.copy(dst[:, :, 0:n], src[:, :, 0:n]).then_inc(by_act.sem, by_act.did(name))
                    act.wait_ge(by_pe.sem, by_pe(turn, "wT"))
                    if later:
                        act.wait_ge(by_pe.sem, by_pe(turn - 1, "wS"))
                        act.wait_ge(by_act.sem, by_act(turn - 1, "wT"))
                    nc.scalar.mul(wT[:, :, 0:n], X[1][:, :, 0:n], -1.0).then_inc(by_act.sem, by_act.did("wT"))
                    act.wait_ge(by_pe.sem, by_pe(turn, "aV"))
                    if later:
                        act.wait_ge(by_dve.sem, by_dve(turn - 1, "o_sum"))
                        act.wait_ge(by_act.sem, by_act(turn - 1, "o_sq"))
                    nc.scalar.activation(osq[0:n], X[2][0:n], ACT.Square).then_inc(by_act.sem, by_act.did("o_sq"))
                    act.wait_ge(by_dve.sem, by_dve(turn, "o_z"))
                    act.dma_start(g.merged_d[at, 0:H * DD], oz[0:n].rearrange("p h d -> p (h d)")).then_inc(s_out, 16)

                body(0)
                act.dma_start(g.outs["delta_sample"].rearrange("h k v -> k h v"), S[:]).then_inc(s_sout, 16)
                with act.Fori(1, g.TILES + 1) as turn:
                    body(turn)
                act.dma_start(g.outs["delta_prompt"].rearrange("h k v -> k h v"), S[:]).then_inc(s_sout, 16)
                act.wait_ge(s_sout, 32)
                act.wait_ge(s_out, g.T17 * 16)

            @block.tensor
            def _(pe):
                def body(turn):
                    later, n, tile, at = shape(turn)
                    one = g.ident[0:n, 0:n]
                    pe.wait_ge(s_in, (turn + 1) * 16)
                    if later:
                        pe.wait_ge(by_dve.sem, by_dve(turn - 1, "o_n"))
                        pe.wait_ge(by_act.sem, by_act(turn - 1, "o_sq"))
                    for j in range(3 * H):
                        tr = nc.tensor.transpose(X[j // H][0:n, j % H, :], ct[:, j, 0:n], g.ident[:])
                    tr.then_inc(by_pe.sem, by_pe.did("rows"))
                    pe.wait_ge(by_dve.sem, by_dve(turn, "bg"))
                    sums = X[3][:].rearrange("p h d -> p (h d)")
                    gt = bgt[0:n, H:2 * H]
                    nc.tensor.matmul(sums[0:n, 0:H], g.upto[0:n, 0:n], gt, start=True, stop=True)
                    nc.tensor.matmul(sums[0:n, H:2 * H], g.behind[0:n, 0:n], gt, start=True, stop=True)
                    nc.tensor.matmul(sums[:, 2 * H:3 * H], g.ones[0:n, :], gt, start=True, stop=True).then_inc(by_pe.sem, by_pe.did("sums"))
                    pe.wait_ge(by_pool.sem, by_pool(turn, "g_mask"))
                    for h in range(H):
                        mm = nc.tensor.matmul(P2[0][0:n, h // 2, h % 2, 0:n], gm[0:n, h, 0:n], g.upto[0:n, 0:n], start=True, stop=True)
                    mm.then_inc(by_pe.sem, by_pe.did("decay"))
                    pe.wait_ge(by_dve.sem, by_dve(turn, "kn"))
                    for h in range(H):
                        tr = nc.tensor.transpose(P1[0][:, h, 0:n], kn[0:n, h, :], one)
                    tr.then_inc(by_pe.sem, by_pe.did("knT"))
                    pe.wait_ge(by_pool.sem, by_pool(turn, "kb"))
                    for h in range(H):
                        tr = nc.tensor.transpose(P1[1][:, h, 0:n], kb[0:n, h, :], one)
                    tr.then_inc(by_pe.sem, by_pe.did("kbT"))
                    pe.wait_ge(by_dve.sem, by_dve(turn, "qn"))
                    pe.wait_ge(by_act.sem, by_act(turn, "decay"))
                    for h in range(H):
                        tr = nc.tensor.transpose(P2[0][:, h // 2, h % 2, 0:n], qn[0:n, h, :], one)
                    tr.then_inc(by_pe.sem, by_pe.did("qnT"))
                    pe.wait_ge(by_pool.sem, by_pool(turn, "qd"))
                    for h in range(H):
                        tr = nc.tensor.transpose(P2[1][:, h // 2, h % 2, 0:n], qd[0:n, h, :], one)
                    tr.then_inc(by_pe.sem, by_pe.did("qdT"))
                    pe.wait_ge(by_act.sem, by_act(turn, "kbT"))
                    for h in range(H):
                        mm = nc.tensor.matmul(X[0][0:n, h, 0:n], knT[:, h, 0:n], kbT[:, h, 0:n], start=True, stop=True)
                    mm.then_inc(by_pe.sem, by_pe.did("kk"))
                    pe.wait_ge(by_act.sem, by_act(turn, "qnT"))
                    for h in range(H):
                        mm = nc.tensor.matmul(X[1][0:n, h, 0:n], knT[:, h, 0:n], qnT[:, h, 0:n], start=True, stop=True)
                    mm.then_inc(by_pe.sem, by_pe.did("kq"))
                    pe.wait_ge(by_dve.sem, by_dve(turn, "LT"))
                    for h in range(H):
                        tr = nc.tensor.transpose(X[2][0:n, h, 0:n], LT[0:n, h, 0:n], one)
                    tr.then_inc(by_pe.sem, by_pe.did("L"))
                    for l in range(1, LEVELS):
                        for half in range(2):
                            if l == 1:
                                pe.wait_ge(by_dve.sem, by_dve(turn, "T0"))
                                pe.wait_ge(by_pool.sem, by_pool(turn, "T0T"))
                            else:
                                pe.wait_ge(by_dve.sem, by_dve(turn, f"T{l - 1}{half}"))
                            for h in (2 * half, 2 * half + 1):
                                mm = nc.tensor.matmul(P1[half][0:n, h, 0:n], LT[0:n, h, 0:n], T[0:n, h, 0:n], start=True, stop=True)
                            mm.then_inc(by_pe.sem, by_pe.did(f"LT{l}{half}"))
                        for half in range(2):
                            pe.wait_ge(by_dve.sem, by_dve(turn, f"m{l}{half}"))
                            if l == 1 and half == 1:
                                pe.wait_ge(by_act.sem, by_act(turn, "qdT"))
                            for h in (2 * half, 2 * half + 1):
                                if l < LEVELS - 1:
                                    nc.tensor.matmul(P2[half][0:n, 0, h % 2, 0:n], TT[0:n, h, 0:n], M[0:n, h, 0:n], start=True, stop=True)
                                mm = nc.tensor.matmul(P2[half][0:n, 1, h % 2, 0:n], M[0:n, h, 0:n], TT[0:n, h, 0:n], start=True, stop=True)
                            mm.then_inc(by_pe.sem, by_pe.did(f"TLT{l}{half}"))
                    pe.wait_ge(by_dve.sem, by_dve(turn, f"T{LEVELS - 1}1"))
                    for h in range(H):
                        mm = nc.tensor.matmul(X[0][0:n, h, :], TT[0:n, h, 0:n], vb[0:n, h, :], start=(h == 0), stop=False, skip_group_check=True)
                    mm.then_inc(by_pe.sem, by_pe.did("u"))
                    pe.wait_ge(by_pool.sem, by_pool(turn, "kbe"))
                    for h in range(H):
                        mm = nc.tensor.matmul(X[1][:, h, 0:n], kbe[0:n, h, :], TT[0:n, h, 0:n], start=True, stop=True)
                    mm.then_inc(by_pe.sem, by_pe.did("wT"))
                    pe.wait_ge(by_act.sem, by_act(turn, "wT"))
                    if later:
                        pe.wait_ge(by_dve.sem, by_dve(turn, "bg"))
                    else:
                        pe.wait_ge(s_s0, 16)
                    for h in range(H):
                        mm = nc.tensor.matmul(X[0][0:n, h, :], wT[:, h, 0:n], S[:, h, :], start=False, stop=True, skip_group_check=True)
                    mm.then_inc(by_pe.sem, by_pe.did("wS"))
                    for h in range(H):
                        mm = nc.tensor.matmul(X[2][0:n, h, :], qdT[:, h, 0:n], S[:, h, :], start=(h == 0), stop=False, skip_group_check=True)
                    mm.then_inc(by_pe.sem, by_pe.did("qS"))
                    pe.wait_ge(by_dve.sem, by_dve(turn, "v_new"))
                    for h in range(H):
                        mm = nc.tensor.matmul(X[2][0:n, h, :], AT[0:n, h, 0:n], vn[0:n, h, :], start=False, stop=True, skip_group_check=True)
                    mm.then_inc(by_pe.sem, by_pe.did("aV"))
                    for h in range(H):
                        mm = nc.tensor.matmul(X[3][:, h, :], kd[0:n, h, :], vn[0:n, h, :], start=True, stop=True)
                    mm.then_inc(by_pe.sem, by_pe.did("kV"))

                turns(pe, body)

            @block.vector
            def _(dve):
                link = Steps(g.sem("d_link"), dve, 9)
                link.begin(0)
                nc.vector.memset(zero[:], 0.0).then_inc(s_zero, 1)
                dve.wait_ge(s_par, 48)
                link.link(nc.vector.tensor_copy(sp_in[:], g.bg[:, :, H:2 * H]))
                link.link(nc.vector.tensor_tensor(sp_in[:], sp_in[:], wide(par[:, 1, :], P, g.T17, H), ALU.add))
                nc.vector.scalar_tensor_tensor(out=sp_abs[:], in0=sp_in[:], scalar=-1.0, in1=sp_in[:], op0=ALU.mult,
                                               op1=ALU.max).then_inc(s_pre, 1)
                dve.wait_ge(s_exp, 4)
                link.link(nc.vector.scalar_tensor_tensor(out=sp_in[:], in0=sp_in[:], scalar=0.0, in1=sp_abs[:], op0=ALU.max, op1=ALU.add))
                link.link(nc.vector.tensor_tensor(sp_in[:], sp_in[:], wide(par[:, 0, :], P, g.T17, H), ALU.mult))
                link.link(nc.vector.tensor_scalar(g.bg[:, :, H:2 * H], sp_in[:], -1.0, None, ALU.mult))
                link.link(nc.vector.tensor_scalar(g.bg[:, :, 0:H], g.bg[:, :, 0:H], 1.0, None, ALU.add))
                link.link(nc.vector.reciprocal(g.bg[:, :, 0:H], g.bg[:, :, 0:H]))

                def body(turn):
                    later, n, tile, at = shape(turn)
                    V = nc.vector

                    def did(name):
                        return by_dve.sem, by_dve.did(name)

                    def heads(a):
                        return wide(a, n, H, DD)

                    if later:
                        dve.wait_ge(by_dve.sem, by_dve(turn - 1, "o_z"))
                        dve.wait_ge(by_pe.sem, by_pe(turn - 1, "sums"))
                        dve.wait_ge(by_pool.sem, by_pool(turn - 1, "kb"))
                    V.tensor_copy(bgt[0:n], g.bg[0:n, bass.ds(tile, 1), :].rearrange("p a c -> p (a c)")).then_inc(*did("bg"))
                    dve.wait_ge(by_act.sem, by_act(turn, "squares"))
                    V.tensor_reduce(ss[0:n], sq[0:n], AX, ALU.add).then_inc(*did("sum_sq"))
                    dve.wait_ge(by_dve.sem, by_dve(turn, "sum_sq"))
                    if later:
                        dve.wait_ge(by_pool.sem, by_pool(turn - 1, "r"))
                    V.tensor_scalar(ssn[0:n, 0:H], ss[0:n, 0:H], EPS, float(DD), ALU.add, ALU.mult).then_inc(*did("q_sq"))
                    V.tensor_scalar(ssn[0:n, H:2 * H], ss[0:n, H:2 * H], EPS, None, ALU.add).then_inc(*did("k_sq"))
                    dve.wait_ge(by_pool.sem, by_pool(turn, "r"))
                    if later:
                        dve.wait_ge(by_pool.sem, by_pool(turn - 1, "kd"))
                        dve.wait_ge(by_pe.sem, by_pe(turn - 1, "kV"))
                    V.tensor_tensor(kn[0:n], X[1][0:n], heads(r[0:n, H:2 * H]), ALU.mult).then_inc(*did("kn"))
                    V.tensor_tensor(qn[0:n], X[0][0:n], heads(r[0:n, 0:H]), ALU.mult).then_inc(*did("qn"))
                    dve.wait_ge(by_dve.sem, by_dve(turn, "bg"))
                    V.tensor_tensor(vb[0:n], X[2][0:n], heads(bgt[0:n, 0:H]), ALU.mult).then_inc(*did("vb"))
                    dve.wait_ge(by_pe.sem, by_pe(turn, "kk"))
                    dve.wait_ge(by_pool.sem, by_pool(turn, "D"))
                    V.tensor_tensor(LT[0:n, :, 0:n], X[0][0:n, :, 0:n], dm[0:n, :, 0:n], ALU.mult).then_inc(*did("LT"))
                    dve.wait_ge(by_pe.sem, by_pe(turn, "kq"))
                    V.tensor_tensor(AT[0:n, :, 0:n], X[1][0:n, :, 0:n], dm[0:n, :, 0:n], ALU.mult).then_inc(*did("AT"))
                    dve.wait_ge(by_pe.sem, by_pe(turn, "L"))
                    V.tensor_tensor(B[0:n, :, 0:n], X[2][0:n, :, 0:n], g.level[0:n, 0:1, 0:n].to_broadcast([n, H, n]), ALU.mult).then_inc(*did("B0"))
                    dve.wait_ge(by_dve.sem, by_dve(turn, "B0"))
                    V.tensor_tensor(T[0:n, :, 0:n], g.ident[0:n, 0:n].unsqueeze(1).to_broadcast([n, H, n]), B[0:n, :, 0:n], ALU.subtract).then_inc(*did("T0"))
                    for l in range(1, LEVELS):
                        for half in range(2):
                            hh = slice(2 * half, 2 * half + 2)
                            dve.wait_ge(by_pe.sem, by_pe(turn, f"LT{l}{half}"))
                            if l == 1:
                                dve.wait_ge(by_pool.sem, by_pool(turn, "T0T"))
                            V.tensor_tensor(M[0:n, hh, 0:n], P1[half][0:n, hh, 0:n], g.level[0:n, l:l + 1, 0:n].to_broadcast([n, 2, n]),
                                            ALU.mult).then_inc(*did(f"m{l}{half}"))
                        for half in range(2):
                            hh = slice(2 * half, 2 * half + 2)
                            dve.wait_ge(by_pe.sem, by_pe(turn, f"TLT{l}{half}"))
                            if l < LEVELS - 1:
                                V.tensor_tensor(T[0:n, hh, 0:n], T[0:n, hh, 0:n], P2[half][0:n, 0, :, 0:n], ALU.subtract)
                            V.tensor_tensor(TT[0:n, hh, 0:n], TT[0:n, hh, 0:n], P2[half][0:n, 1, :, 0:n], ALU.subtract).then_inc(*did(f"T{l}{half}"))
                    dve.wait_ge(by_pe.sem, by_pe(turn, "wS"))
                    V.tensor_copy(vn[0:n], X[0][0:n]).then_inc(*did("v_new"))
                    dve.wait_ge(by_pe.sem, by_pe(turn, "kV"))
                    dve.wait_ge(by_pool.sem, by_pool(turn, "S_dec"))
                    state = V.tensor_tensor(S[:], S[:], X[3][:], ALU.add).then_inc(*did("state"))
                    dve.wait_ge(by_act.sem, by_act(turn, "o_sq"))
                    V.tensor_reduce(oss[0:n], osq[0:n], AX, ALU.add).then_inc(*did("o_sum"))
                    dve.wait_ge(by_dve.sem, by_dve(turn, "o_sum"))
                    V.tensor_scalar(osn[0:n], oss[0:n], 1.0 / DD, EPS, ALU.mult, ALU.add).then_inc(*did("o_eps"))
                    dve.wait_ge(by_pool.sem, by_pool(turn, "o_r"))
                    V.tensor_tensor(o[0:n], X[2][0:n], heads(orr[0:n]), ALU.mult).then_inc(*did("o_n"))
                    dve.wait_ge(by_dve.sem, by_dve(turn, "o_n"))
                    V.tensor_tensor(og[0:n], o[0:n], gain[0:n].unsqueeze(1).to_broadcast([n, H, DD]), ALU.mult).then_inc(*did("o_g"))
                    dve.wait_ge(by_dve.sem, by_dve(turn, "o_g"))
                    dve.wait_ge(s_z, (turn + 1) * 16)
                    if later:
                        dve.wait_ge(s_out, turn * 16)
                    V.tensor_tensor(oz[0:n], og[0:n], zt[0:n], ALU.mult).then_inc(*did("o_z"))

                body(0)
                dve.wait_ge(s_sout, 16)
                link.link(nc.vector.memset(S[:], 0.0))
                link.link(nc.vector.memset(oss[:], 0.0))
                with dve.Fori(1, g.TILES + 1) as turn:
                    body(turn)

            @block.gpsimd
            def _(pool):
                G = nc.gpsimd

                def body(turn):
                    later, n, tile, at = shape(turn)

                    def did(name):
                        return by_pool.sem, by_pool.did(name)

                    def heads(a):
                        return wide(a, n, H, DD)

                    pool.wait_ge(by_dve.sem, by_dve(turn, "bg"))
                    if later:
                        pool.wait_ge(by_pe.sem, by_pe(turn - 1, "decay"))
                        pool.wait_ge(by_pool.sem, by_pool(turn - 1, "g_mask"))
                    G.tensor_tensor(gm[0:n, :, 0:n], g.behind[0:n, 0:n].unsqueeze(1).to_broadcast([n, H, n]),
                                    bgt[0:n, H:2 * H].unsqueeze(2).to_broadcast([n, H, n]), ALU.mult).then_inc(*did("g_mask"))
                    pool.wait_ge(by_dve.sem, by_dve(turn, "k_sq"))
                    if later:
                        pool.wait_ge(by_dve.sem, by_dve(turn - 1, "qn"))
                    G.tensor_tensor(r[0:n], ssn[0:n], g.half[0:n, 0:2 * H], ALU.pow).then_inc(*did("r"))
                    pool.wait_ge(by_dve.sem, by_dve(turn, "kn"))
                    if later:
                        pool.wait_ge(by_pe.sem, by_pe(turn - 1, "kV"))
                    G.tensor_tensor(kb[0:n], kn[0:n], heads(bgt[0:n, 0:H]), ALU.mult).then_inc(*did("kb"))
                    pool.wait_ge(by_dve.sem, by_dve(turn, "qn"))
                    pool.wait_ge(by_act.sem, by_act(turn, "e_all"))
                    G.tensor_tensor(qd[0:n], qn[0:n], heads(e_rows[0:n, 0, :]), ALU.mult).then_inc(*did("qd"))
                    pool.wait_ge(by_pool.sem, by_pool(turn, "kb"))
                    G.tensor_tensor(kbe[0:n], kb[0:n], heads(e_rows[0:n, 0, :]), ALU.mult).then_inc(*did("kbe"))
                    G.tensor_tensor(kd[0:n], kn[0:n], heads(e_rows[0:n, 1, :]), ALU.mult).then_inc(*did("kd"))
                    pool.wait_ge(by_act.sem, by_act(turn, "decay"))
                    if later:
                        pool.wait_ge(by_dve.sem, by_dve(turn - 1, "AT"))
                    G.tensor_tensor(dm[0:n, :, 0:n], dec[0:n, :, 0:n], g.upto[0:n, 0:n].unsqueeze(1).to_broadcast([n, H, n]), ALU.mult).then_inc(*did("D"))
                    pool.wait_ge(by_dve.sem, by_dve(turn, "LT"))
                    G.tensor_tensor(BT[0:n, :, 0:n], LT[0:n, :, 0:n], g.level[0:n, LEVELS:LEVELS + 1, 0:n].to_broadcast([n, H, n]), ALU.mult).then_inc(*did("B0T"))
                    pool.wait_ge(by_pool.sem, by_pool(turn, "B0T"))
                    G.tensor_tensor(TT[0:n, :, 0:n], g.ident[0:n, 0:n].unsqueeze(1).to_broadcast([n, H, n]), BT[0:n, :, 0:n], ALU.subtract).then_inc(*did("T0T"))
                    pool.wait_ge(by_pe.sem, by_pe(turn, "qS"))
                    G.tensor_tensor(S[:], S[:], e_all[:].unsqueeze(2).to_broadcast([P, H, DD]), ALU.mult).then_inc(*did("S_dec"))
                    pool.wait_ge(by_dve.sem, by_dve(turn, "o_eps"))
                    G.tensor_tensor(orr[0:n], osn[0:n], g.half[0:n, 0:H], ALU.pow).then_inc(*did("o_r"))

                turns(pool, body)


def sticks(nc, g):
    H, DD, NEW = SB_HEADS, SB_DIM, g.NEW
    HS = H // 2
    PAIRS = g.QKT // 2
    NEW_BLOCK, PAST_BLOCK = g.TILES, g.TILES + 1
    BLOCKS = g.TILES + 2
    SCALE = float(DD) ** -0.5
    MASKED = -1e30
    s_kv, s_new, s_past, s_gain = g.sem("a_kv"), g.sem("a_new"), g.sem("a_past"), g.sem("a_gain")
    s_zero, s_mask, s_turned, s_ready = g.sem("a_zero"), g.sem("a_mask"), g.sem("a_turned"), g.sem("a_ready")
    s_q, s_qz = g.sem("a_q"), g.sem("a_qz")
    pair = lambda name: [g.sem(f"a_{name}{a}") for a in range(2)]
    s_z, s_zm, s_keep, s_beta, s_scan, s_carry, s_a, s_t, s_ev, s_v = (
        pair(n) for n in ("z", "zm", "keep", "beta", "scan", "carry", "a", "t", "ev", "v"))
    end_act = Line(g.sem("a_eact"), ["o_sq"])
    end_dve = Line(g.sem("a_edve"), ["o_sum", "o_eps", "o_n", "o_g"])
    end_pool = Line(g.sem("a_epool"), ["o_r"])
    s_out = g.sem("a_out")
    with ExitStack() as life:
        KT = g.sb("a_KT", [P, PAIRS, BLOCKS * P], at=life)
        V = g.sb("a_V", [P, BLOCKS, H * DD], at=life)
        past = g.sb("a_past", [P, H * DD], at=life)
        gain = g.sb("a_gainb", [P, DD], at=life)
        mask = g.sb("a_maskb", [P, P], at=life)
        q_in = g.sb("a_qin", [P, PAIRS, P], at=life)
        QZ = g.sb("a_QZ", [P, H, P], at=life)
        zm = [g.sb(f"a_zm{a}", [P, HS, P], at=life) for a in range(2)]
        keep = [g.sb(f"a_keep{a}", [P, HS, P + 1], at=life) for a in range(2)]
        beta = [g.sb(f"a_beta{a}", [P, HS, P], at=life) for a in range(2)]
        carry = [g.sb(f"a_carry{a}", [P, HS, P + 1], at=life) for a in range(2)]
        prod = [g.sb(f"a_prod{a}", [P, HS, P + 1], at=life) for a in range(2)]
        A = [g.sb(f"a_A{a}", [P, HS, P], at=life) for a in range(2)]
        AT = [g.sb(f"a_AT{a}", [P, HS, P], at=life) for a in range(2)]
        osq = g.sb("a_osq", [P, H, DD], at=life)
        oss, osn, orr = (g.sb("a_" + n, [P, H], at=life) for n in ("oss", "osn", "orr"))
        o = g.sb("a_o", [P, H, DD], at=life)
        og = g.sb("a_og", [P, H, DD], at=life)
        Z = [g.psum(f"a_z{a}", [P, HS, P], at=life) for a in range(2)]
        TR = [g.psum(f"a_tr{a}", [P, HS, P], at=life) for a in range(2)]
        acc = g.psum("a_acc", [P, H, DD], at=life)
        p_past = g.psum("a_pp", [P, PAIRS, P], at=life)

        def shape(turn):
            if isinstance(turn, int) and turn == 0:
                return NEW, slice(g.SEQ, g.TOK), 0, 1, lambda i: (NEW_BLOCK, PAST_BLOCK)[i]
            q = turn - 1
            return P, bass.ds(q * P, P), 2 + q * (q + 1) // 2, q, lambda i: q - i

        STEPS = 2 + g.TILES * (g.TILES + 1) // 2

        def first_of_all(turn):
            return isinstance(turn, int) and turn == 0

        def turns(eng, body):
            for turn in range(3):
                body(turn)
            with eng.Fori(3, g.TILES + 1) as turn:
                body(turn)

        def after(eng, sem, count):
            if not isinstance(count, int) or count > 0:
                eng.wait_ge(sem, count)

        def later_steps(eng, first, last, body):
            if isinstance(last, int):
                for i in range(first, last + 1):
                    body(i)
            else:
                with eng.Fori(first, last + 1) as i:
                    body(i)

        def flat(t, n):
            return t[0:n].rearrange("p h k -> p (h k)")[:, ::-1]

        with nc.Block() as block:
            @block.sync
            def _(sp):
                sp.dma_start(past[:], g.ins["cache_k"][0, 0].rearrange("t h d -> t (h d)")).then_inc(s_past, 16)
                sp.dma_start(gain[:], g.ins["onorm_b"][0].partition_broadcast(P)).then_inc(s_gain, 16)
                sp.wait_ge(s_zero, 2)
                sp.dma_start(KT[:, :, NEW_BLOCK * P:NEW_BLOCK * P + NEW], g.qk_d[PAIRS:, :, g.SEQ:g.TOK].rearrange("c p t -> p c t")).then_inc(s_new, 16)
                sp.dma_start(V[0:NEW, NEW_BLOCK, :], g.outs["v_sample"]).then_inc(s_new, 16)
                sp.dma_start(V[:, PAST_BLOCK, :], g.ins["cache_v"][0, 0].rearrange("t h d -> t (h d)")).then_inc(s_new, 16)

                def body(turn):
                    n, at, g0, last, block_of = shape(turn)
                    if not first_of_all(turn):
                        sp.wait_ge(s_qz, 2 * turn)
                    sp.dma_start(q_in[:, :, 0:n], g.qk_d[0:PAIRS, :, at].rearrange("c p t -> p c t")).then_inc(s_q, 16)
                    if isinstance(turn, int) and turn == 0:
                        sp.dma_start(KT[:, :, 0:g.SEQ], g.qk_d[PAIRS:, :, 0:g.SEQ].rearrange("c p t -> p c t")).then_inc(s_kv, 16)
                        sp.dma_start(V[:, 0:g.TILES, :], g.outs["v_prompt"].rearrange("(b p) n -> p b n", p=P)).then_inc(s_kv, 16)
                        return
                    store(turn - 1, NEW if isinstance(turn, int) and turn == 1 else P,
                          slice(g.SEQ, g.TOK) if isinstance(turn, int) and turn == 1 else bass.ds((turn - 2) * P, P))

                def store(turn, n, at):
                    sp.wait_ge(end_dve.sem, end_dve(turn, "o_g"))
                    sp.dma_start(g.merged_d[at, DN_HEADS * DN_DIM:], og[0:n].rearrange("p h d -> p (h d)")).then_inc(s_out, 16)

                turns(sp, body)
                D = g.D
                for a in range(2):
                    for tile, row in ((g.post[a], 2), (g.scale[a], 4), (g.shift[a], 3)):
                        sp.dma_start(tile[:], g.mod_d[a, row * D:(row + 1) * D].partition_broadcast(P)).then_inc(g.s_rows_mixed, 16)
                for i, name in enumerate(["g_post_mix", "g_pre_ffn"]):
                    sp.dma_start(g.gains[:, i, :], g.ins[name][0].partition_broadcast(P)).then_inc(g.s_rows_mixed, 16)
                GE = g.GROUPS_E
                for name, cols in (("group", slice(0, GE)), ("expert", slice(GE, None))):
                    sp.dma_start(g.b_router[:, cols], g.ins[f"b_router_{name}"][0].partition_broadcast(P)).then_inc(g.s_rows_mixed, 16)
                    sp.dma_start(g.w_router[:, :, cols], g.ins[f"w_router_{name}"][0].rearrange("(k p) n -> p k n", p=P)).then_inc(g.s_w_mixed, 16)
                sp.dma_start(g.w_out[:], g.ins["w_out"][0].rearrange("(k p) n -> p k n", p=P)).then_inc(g.s_w_mixed, 16)
                store(g.TILES, P, slice(g.SEQ - P, g.SEQ))
                sp.wait_ge(s_out, g.T17 * 16)

            @block.tensor
            def _(pe):
                pe.wait_ge(s_past, 16)
                for j in range(PAIRS):
                    tr = nc.tensor.transpose(p_past[:, j, :], past[:, j * P:(j + 1) * P], g.ident[:])
                tr.then_inc(s_turned, 1)
                pe.wait_ge(s_ready, 1)
                pe.wait_ge(s_new, 48)

                def body(turn):
                    n, at, g0, last, block_of = shape(turn)

                    def block(i):
                        b = block_of(i)
                        return b if isinstance(b, int) else nc.s_assert_within(
                            b, 0, g.TILES - 1, skip_runtime_bounds_check_because="the walk ends at block 0")

                    def score(i, a):
                        after(pe, s_beta[a], g0 + i)
                        for h in range(HS):
                            head = a * HS + h
                            mm = nc.tensor.matmul(Z[a][0:n, h, :], QZ[:, head, 0:n], KT[:, head // 2, bass.ds(block(i) * P, P)],
                                                  start=True, stop=True)
                        mm.then_inc(s_z[a], 1)

                    def turn_over(i, a):
                        pe.wait_ge(s_a[a], g0 + i + 1)
                        after(pe, s_ev[a], g0 + i)
                        for h in range(HS):
                            tr = nc.tensor.transpose(TR[a][:, h, 0:n], A[a][0:n, h, :], g.ident[0:n, 0:n])
                        tr.then_inc(s_t[a], 1)

                    def weigh(i, a, first=False):
                        pe.wait_ge(s_ev[a], g0 + i + 1)
                        if first and not first_of_all(turn):
                            pe.wait_ge(end_dve.sem, end_dve(turn - 1, "o_n"))
                            pe.wait_ge(end_act.sem, end_act(turn - 1, "o_sq"))
                        for h in range(HS):
                            head = a * HS + h
                            mm = nc.tensor.matmul(acc[0:n, head, :], AT[a][:, h, 0:n],
                                                  V[:, bass.ds(block(i), 1), head * DD:(head + 1) * DD].rearrange("p a n -> p (a n)"),
                                                  start=(first and h == 0), stop=True, skip_group_check=True)
                        mm.then_inc(s_v[a], 1)

                    pe.wait_ge(s_qz, 2 * (turn + 1))
                    if isinstance(turn, int) and turn == 1:
                        pe.wait_ge(s_kv, 32)
                    score(0, 0)
                    score(0, 1)
                    if isinstance(last, int) and last == 0:
                        turn_over(0, 0)
                        turn_over(0, 1)
                        weigh(0, 0, True)
                        weigh(0, 1)
                        return
                    score(1, 0)
                    turn_over(0, 0)
                    score(1, 1)
                    turn_over(0, 1)
                    weigh(0, 0, True)

                    def step(i):
                        score(i, 0)
                        turn_over(i - 1, 0)
                        weigh(i - 2, 1)
                        score(i, 1)
                        turn_over(i - 1, 1)
                        weigh(i - 1, 0)

                    later_steps(pe, 2, last, step)
                    turn_over(last, 0)
                    weigh(last - 1, 1)
                    turn_over(last, 1)
                    weigh(last, 0)
                    weigh(last, 1)

                turns(pe, body)

            @block.scalar
            def _(act):
                act.wait_ge(s_turned, 1)
                nc.scalar.copy(KT[:, :, PAST_BLOCK * P:(PAST_BLOCK + 1) * P], p_past[:]).then_inc(s_ready, 1)

                def body(turn):
                    n, at, g0, last, block_of = shape(turn)

                    def squash(i, a, diagonal=False):
                        G = g0 + i
                        if diagonal:
                            act.wait_ge(s_zm[a], turn + 1)
                        else:
                            act.wait_ge(s_z[a], G + 1)
                        src = zm[a] if diagonal else Z[a]
                        after(act, s_scan[a], G)
                        after(act, s_keep[a], G)
                        nc.scalar.activation(keep[a][0:n, :, 0:P], src[0:n], ACT.Sigmoid, scale=-SCALE).then_inc(s_keep[a], 1)
                        after(act, s_a[a], G)
                        after(act, s_beta[a], G)
                        nc.scalar.activation(beta[a][0:n], src[0:n], ACT.Sigmoid, scale=SCALE).then_inc(s_beta[a], 1)

                    def take(i):
                        act.wait_ge(s_t[0], g0 + i + 1)
                        after(act, s_v[0], g0 + i)
                        nc.scalar.copy(AT[0][:, :, 0:n], TR[0][:, :, 0:n]).then_inc(s_ev[0], 1)

                    squash(0, 0, True)
                    squash(0, 1, True)
                    if not first_of_all(turn):
                        finish(turn - 1, NEW if isinstance(turn, int) and turn == 1 else P, g0)

                    def step(i):
                        squash(i, 0)
                        take(i - 1)
                        squash(i, 1)

                    later_steps(act, 1, last, step)
                    take(last)

                def finish(turn, n, steps):
                    act.wait_ge(s_v[1], steps)
                    if not first_of_all(turn):
                        act.wait_ge(end_dve.sem, end_dve(turn - 1, "o_sum"))
                        act.wait_ge(end_act.sem, end_act(turn - 1, "o_sq"))
                    nc.scalar.activation(osq[0:n], acc[0:n], ACT.Square).then_inc(end_act.sem, end_act.did("o_sq"))

                turns(act, body)
                finish(g.TILES, P, STEPS)

            @block.vector
            def _(dve):
                link = Steps(g.sem("a_link"), dve, 1 + 6)
                link.begin(0)
                link.link(nc.vector.tensor_scalar(mask[:], g.upto[:], MASKED, None, ALU.mult))
                for a in range(2):
                    link.link(nc.vector.memset(keep[a][:, :, P:P + 1], 0.0))
                    link.link(nc.vector.memset(carry[a][:], 0.0))
                link.link(nc.vector.memset(osq[:], 0.0))
                link.link(nc.vector.memset(oss[:], 0.0))
                dve.wait_ge(s_gain, 16)

                def body(turn):
                    n, at, g0, last, block_of = shape(turn)

                    def walk(i, a):
                        G = g0 + i
                        dve.wait_ge(s_keep[a], G + 1)
                        after(dve, s_carry[a], G + turn + 1)
                        after(dve, s_a[a], G)
                        nc.vector.tensor_tensor_scan(flat(prod[a], n), flat(keep[a], n), flat(carry[a], n), 0.0,
                                                     ALU.mult, ALU.add).then_inc(s_scan[a], 1)
                        dve.wait_ge(s_scan[a], G + 1)
                        nc.vector.tensor_copy(carry[a][0:n, :, P:P + 1], prod[a][0:n, :, 0:1]).then_inc(s_carry[a], 1)

                    def take(i):
                        dve.wait_ge(s_t[1], g0 + i + 1)
                        after(dve, s_v[1], g0 + i)
                        nc.vector.tensor_copy(AT[1][:, :, 0:n], TR[1][:, :, 0:n]).then_inc(s_ev[1], 1)

                    for a in range(2):
                        after(dve, s_carry[a], g0 + turn)
                        nc.vector.memset(carry[a][:, :, P:P + 1], 1.0).then_inc(s_carry[a], 1)
                        dve.wait_ge(s_z[a], g0 + 1)
                        after(dve, s_beta[a], g0)
                        nc.vector.tensor_tensor(zm[a][0:n], Z[a][0:n], mask[0:n].unsqueeze(1).to_broadcast([n, HS, P]),
                                                ALU.add).then_inc(s_zm[a], 1)
                    walk(0, 0)
                    walk(0, 1)
                    if not first_of_all(turn):
                        finish(turn - 1, NEW if isinstance(turn, int) and turn == 1 else P)

                    def step(i):
                        walk(i, 0)
                        take(i - 1)
                        walk(i, 1)

                    later_steps(dve, 1, last, step)
                    take(last)

                def finish(turn, n):
                    V3 = nc.vector
                    dve.wait_ge(end_act.sem, end_act(turn, "o_sq"))
                    V3.tensor_reduce(oss[0:n], osq[0:n], AX, ALU.add).then_inc(end_dve.sem, end_dve.did("o_sum"))
                    dve.wait_ge(end_dve.sem, end_dve(turn, "o_sum"))
                    V3.tensor_scalar(osn[0:n], oss[0:n], 1.0 / DD, EPS, ALU.mult, ALU.add).then_inc(end_dve.sem, end_dve.did("o_eps"))
                    dve.wait_ge(end_pool.sem, end_pool(turn, "o_r"))
                    V3.tensor_tensor(o[0:n], acc[0:n], orr[0:n].unsqueeze(2).to_broadcast([n, H, DD]), ALU.mult).then_inc(end_dve.sem, end_dve.did("o_n"))
                    dve.wait_ge(end_dve.sem, end_dve(turn, "o_n"))
                    if not first_of_all(turn):
                        dve.wait_ge(s_out, turn * 16)
                    V3.tensor_tensor(og[0:n], o[0:n], gain[0:n].unsqueeze(1).to_broadcast([n, H, DD]), ALU.mult).then_inc(end_dve.sem, end_dve.did("o_g"))

                turns(dve, body)
                finish(g.TILES, P)

            @block.gpsimd
            def _(pool):
                G_ = nc.gpsimd
                G_.memset(KT[:, :, NEW_BLOCK * P:(NEW_BLOCK + 1) * P], 0.0).then_inc(s_zero, 1)
                G_.memset(V[:, NEW_BLOCK, :], 0.0).then_inc(s_zero, 1)
                G_.memset(QZ[:], 0.0).then_inc(s_mask, 1)
                pool.wait_ge(s_mask, 1)

                def body(turn):
                    n, at, g0, last, block_of = shape(turn)
                    pool.wait_ge(s_q, (turn + 1) * 16)
                    after(pool, s_z[1], g0)
                    spread = QZ[:].rearrange("p (c e) n -> p c e n", e=2)
                    after(pool, s_a[1], g0)
                    for e in range(2):
                        half = slice(e * DD, (e + 1) * DD)
                        G_.tensor_tensor(spread[half, :, e, 0:n], q_in[half, :, 0:n],
                                         g.ones[half, 0:n].unsqueeze(1).to_broadcast([DD, PAIRS, n]), ALU.mult).then_inc(s_qz, 1)
                        pool.wait_ge(s_qz, 2 * turn + e + 1)

                    def weights(i, a):
                        G = g0 + i
                        pool.wait_ge(s_scan[a], G + 1)
                        pool.wait_ge(s_beta[a], G + 1)
                        after(pool, s_t[a], G)
                        G_.tensor_tensor(A[a][0:n], prod[a][0:n, :, 1:P + 1], beta[a][0:n], ALU.mult).then_inc(s_a[a], 1)

                    def step(i):
                        weights(i, 0)
                        weights(i, 1)

                    step(0)
                    if not first_of_all(turn):
                        finish(turn - 1, NEW if isinstance(turn, int) and turn == 1 else P)
                    later_steps(pool, 1, last, step)

                def finish(turn, n):
                    pool.wait_ge(end_dve.sem, end_dve(turn, "o_eps"))
                    G_.tensor_tensor(orr[0:n], osn[0:n], g.half[0:n, 0:H], ALU.pow).then_inc(end_pool.sem, end_pool.did("o_r"))
                    if first_of_all(turn):
                        pool.wait_ge(end_pool.sem, end_pool(turn, "o_r"))

                turns(pool, body)
                finish(g.TILES, P)


def mixed(nc, g):
    D, KT, NEW, T17 = g.D, g.KT, g.NEW, g.T17
    R = g.EXPERTS + g.GROUPS_E
    s_w, s_rows = g.s_w_mixed, g.s_rows_mixed
    s_m, s_x, s_x2, s_h2, s_link = (g.sem("x_" + n) for n in ("m", "x", "x2", "h2", "link"))
    pe_a, pe_b = Line(g.sem("x_pea"), ["mT", "out"]), Line(g.sem("x_peb"), ["hT", "router"])
    act_a, act_b = Line(g.sem("x_acta"), ["mT", "out"]), Line(g.sem("x_actb"), ["sq", "sq2", "hT"])
    dve_b = Line(g.sem("x_dveb"), ["s1", "post", "x2", "s2", "h1", "h2", "logits"])
    pool_b = Line(g.sem("x_poolb"), ["r", "r2"])
    with ExitStack() as life:
        w, wr, br, post, scale, shift, gains = g.w_out, g.w_router, g.b_router, g.post, g.scale, g.shift, g.gains
        m = g.sb("x_m", [P, D], at=life)
        mT = g.sb("x_mT", [P, KT, P], at=life)
        osb = g.sb("x_o", [P, D], at=life)
        x = g.sb("x_x", [P, D], at=life)
        junk = g.sb("x_junk", [P, D], at=life)
        po = g.sb("x_po", [P, D], at=life)
        x2 = g.sb("x_x2", [P, D], at=life)
        hn = g.sb("x_hn", [P, D], at=life)
        h = g.sb("x_h", [P, D], at=life)
        hT = g.sb("x_hT", [P, KT, P], at=life)
        ss, sn, r = (g.sb("x_" + n, [P, 2], at=life) for n in ("ss", "sn", "r"))
        p_m = g.psum("x_pm", [P, KT, P], at=life)
        p_o = g.psum("x_po_", [P, D], at=life)
        p_h = g.psum("x_ph", [P, KT, P], at=life)
        p_r = g.psum("x_pr", [P, 512], at=life)

        def group_of(turn):
            return (1, NEW, slice(g.SEQ, g.TOK), g.TILES) if isinstance(turn, int) and turn == 0 else \
                (0, P, slice(g.SEQ - P, g.SEQ) if isinstance(turn, int) and turn == g.TILES else bass.ds((turn - 1) * P, P),
                 turn - 1)

        def turns(eng, start, finish):
            start(0)
            start(1)
            finish(0)
            with eng.Fori(2, g.TILES + 1) as turn:
                start(turn)
                finish(turn - 1)
            finish(g.TILES)

        def later(turn, n=0):
            return not isinstance(turn, int) or turn > n

        with nc.Block() as block:
            @block.sync
            def _(sp):
                def load(turn):
                    grp, n, at, tile = group_of(turn)
                    if later(turn):
                        sp.wait_ge(pe_a.sem, pe_a(turn - 1, "mT"))
                    sp.dma_start(m[0:n], g.merged_d[at, :]).then_inc(s_m, 16)
                    if later(turn):
                        sp.wait_ge(dve_b.sem, dve_b(turn - 1, "x2"))
                    sp.dma_start(x[0:n], g.x[1] if grp else g.x[0][at, :]).then_inc(s_x, 16)

                load(0)
                with sp.Fori(1, g.TILES + 1) as turn:
                    load(turn)

            @block.tensor
            def _(pe):
                def start(turn):
                    grp, n, at, tile = group_of(turn)
                    pe.wait_ge(s_m, (turn + 1) * 16)
                    if later(turn):
                        pe.wait_ge(act_a.sem, act_a(turn - 1, "mT"))
                    for k in range(KT):
                        tr = nc.tensor.transpose(p_m[:, k, 0:n], m[0:n, k * P:(k + 1) * P], g.ident[0:n, 0:n])
                    tr.then_inc(pe_a.sem, pe_a.did("mT"))
                    if not later(turn):
                        pe.wait_ge(s_w, 48)
                    pe.wait_ge(act_a.sem, act_a(turn, "mT"))
                    for c in range(D // 512):
                        for k in range(KT):
                            mm = nc.tensor.matmul(p_o[0:n, c * 512:(c + 1) * 512], mT[:, k, 0:n], w[:, k, c * 512:(c + 1) * 512],
                                                  start=(k == 0), stop=(k == KT - 1))
                    mm.then_inc(pe_a.sem, pe_a.did("out"))

                def finish(turn):
                    grp, n, at, tile = group_of(turn)
                    pe.wait_ge(dve_b.sem, dve_b(turn, "h2"))
                    if later(turn):
                        pe.wait_ge(act_b.sem, act_b(turn - 1, "hT"))
                    for k in range(KT):
                        tr = nc.tensor.transpose(p_h[:, k, 0:n], h[0:n, k * P:(k + 1) * P], g.ident[0:n, 0:n])
                    tr.then_inc(pe_b.sem, pe_b.did("hT"))
                    pe.wait_ge(act_b.sem, act_b(turn, "hT"))
                    if later(turn):
                        pe.wait_ge(dve_b.sem, dve_b(turn - 1, "logits"))
                    for k in range(KT):
                        mm = nc.tensor.matmul(p_r[0:n, 0:R], hT[:, k, 0:n], wr[:, k, :], start=(k == 0), stop=(k == KT - 1))
                    mm.then_inc(pe_b.sem, pe_b.did("router"))

                turns(pe, start, finish)

            @block.scalar
            def _(act):
                def start(turn):
                    grp, n, at, tile = group_of(turn)
                    act.wait_ge(pe_a.sem, pe_a(turn, "mT"))
                    if later(turn):
                        act.wait_ge(pe_a.sem, pe_a(turn - 1, "out"))
                        act.wait_ge(act_a.sem, act_a(turn - 1, "mT"))
                    nc.scalar.copy(mT[:, :, 0:n], p_m[:, :, 0:n]).then_inc(act_a.sem, act_a.did("mT"))
                    if later(turn):
                        chain(turn - 1)
                    act.wait_ge(pe_a.sem, pe_a(turn, "out"))
                    if later(turn):
                        act.wait_ge(dve_b.sem, dve_b(turn - 1, "post"))
                    nc.scalar.copy(osb[0:n], p_o[0:n]).then_inc(act_a.sem, act_a.did("out"))

                def chain(turn):
                    grp, n, at, tile = group_of(turn)
                    act.wait_ge(act_a.sem, act_a(turn, "out"))
                    if later(turn):
                        act.wait_ge(dve_b.sem, dve_b(turn - 1, "h1"))
                        act.wait_ge(act_b.sem, act_b(turn - 1, "sq2"))
                    nc.scalar.activation(junk[0:n], osb[0:n], ACT.Square, accum_out=ss[0:n, 0:1]).then_inc(act_b.sem, act_b.did("sq"))
                    act.wait_ge(dve_b.sem, dve_b(turn, "x2"))
                    act.wait_ge(act_b.sem, act_b(turn, "sq"))
                    nc.scalar.activation(junk[0:n], x2[0:n], ACT.Square, accum_out=ss[0:n, 1:2]).then_inc(act_b.sem, act_b.did("sq2"))
                    act.dma_start(g.x2_d[at, :], x2[0:n]).then_inc(s_x2, 16)

                def finish(turn):
                    grp, n, at, tile = group_of(turn)
                    act.wait_ge(pe_b.sem, pe_b(turn, "hT"))
                    if later(turn):
                        act.wait_ge(pe_b.sem, pe_b(turn - 1, "router"))
                        act.wait_ge(act_b.sem, act_b(turn - 1, "hT"))
                    nc.scalar.copy(hT[:, :, 0:n], p_h[:, :, 0:n]).then_inc(act_b.sem, act_b.did("hT"))
                    act.wait_ge(dve_b.sem, dve_b(turn, "h2"))
                    act.dma_start(g.h2_d[at, :], h[0:n]).then_inc(s_h2, 16)

                start(0)
                start(1)
                finish(0)
                with act.Fori(2, g.TILES + 1) as turn:
                    start(turn)
                    finish(turn - 1)
                chain(g.TILES)
                finish(g.TILES)
                act.wait_ge(s_x2, T17 * 16)
                act.wait_ge(s_h2, T17 * 16)

            @block.vector
            def _(dve):
                V = nc.vector
                link = Steps(s_link, dve, 5)
                link.begin(0)
                dve.wait_ge(s_rows, 160)
                for a in range(2):
                    link.link(V.tensor_tensor(post[a][:], post[a][:], gains[:, 0, :], ALU.mult))
                    link.link(V.scalar_tensor_tensor(out=scale[a][:], in0=scale[a][:], scalar=1.0, in1=gains[:, 1, :], op0=ALU.add, op1=ALU.mult))
                link.link(V.memset(g.logits[:], 0.0))

                def chain(turn):
                    grp, n, at, tile = group_of(turn)

                    def did(name):
                        return dve_b.sem, dve_b.did(name)

                    def after(name, t=turn):
                        dve.wait_ge(dve_b.sem, dve_b(t, name))

                    dve.wait_ge(act_b.sem, act_b(turn, "sq"))
                    if later(turn):
                        dve.wait_ge(pool_b.sem, pool_b(turn - 1, "r2"))
                    V.tensor_scalar(sn[0:n, 0:1], ss[0:n, 0:1], 1.0 / D, EPS, ALU.mult, ALU.add).then_inc(*did("s1"))
                    dve.wait_ge(pool_b.sem, pool_b(turn, "r"))
                    V.scalar_tensor_tensor(out=po[0:n], in0=osb[0:n], scalar=r[0:n, 0:1], in1=post[grp][0:n], op0=ALU.mult, op1=ALU.mult).then_inc(*did("post"))
                    after("post")
                    dve.wait_ge(s_x, (turn + 1) * 16)
                    if later(turn):
                        dve.wait_ge(s_x2, turn * 16)
                    V.tensor_tensor(x2[0:n], po[0:n], x[0:n], ALU.add).then_inc(*did("x2"))
                    dve.wait_ge(act_b.sem, act_b(turn, "sq2"))
                    V.tensor_scalar(sn[0:n, 1:2], ss[0:n, 1:2], 1.0 / D, EPS, ALU.mult, ALU.add).then_inc(*did("s2"))
                    dve.wait_ge(pool_b.sem, pool_b(turn, "r2"))
                    V.scalar_tensor_tensor(out=hn[0:n], in0=x2[0:n], scalar=r[0:n, 1:2], in1=scale[grp][0:n], op0=ALU.mult, op1=ALU.mult).then_inc(*did("h1"))
                    after("h1")
                    if later(turn):
                        dve.wait_ge(s_h2, turn * 16)
                        dve.wait_ge(pe_b.sem, pe_b(turn - 1, "hT"))
                    V.tensor_tensor(h[0:n], hn[0:n], shift[grp][0:n], ALU.add).then_inc(*did("h2"))
                    dve.wait_ge(pe_b.sem, pe_b(turn, "router"))
                    V.tensor_tensor(g.logits[0:n, bass.ds(tile, 1), :].rearrange("p a c -> p (a c)"), p_r[0:n, 0:R], br[0:n], ALU.add).then_inc(*did("logits"))

                chain(0)
                with dve.Fori(1, g.TILES + 1) as turn:
                    chain(turn)

            @block.gpsimd
            def _(pool):
                def body(turn):
                    grp, n, at, tile = group_of(turn)
                    pool.wait_ge(dve_b.sem, dve_b(turn, "s1"))
                    if later(turn):
                        pool.wait_ge(dve_b.sem, dve_b(turn - 1, "h1"))
                    nc.gpsimd.tensor_tensor(r[0:n, 0:1], sn[0:n, 0:1], g.half[0:n, 0:1], ALU.pow).then_inc(pool_b.sem, pool_b.did("r"))
                    pool.wait_ge(dve_b.sem, dve_b(turn, "s2"))
                    nc.gpsimd.tensor_tensor(r[0:n, 1:2], sn[0:n, 1:2], g.half[0:n, 0:1], ALU.pow).then_inc(pool_b.sem, pool_b.did("r2"))
                    if not later(turn):
                        pool.wait_ge(pool_b.sem, pool_b(turn, "r2"))

                body(0)
                with pool.Fori(1, g.TILES + 1) as turn:
                    body(turn)


def routing(nc, g):
    T17, E, GE, NEW = g.T17, g.EXPERTS, g.GROUPS_E, g.NEW
    PER = E // GE
    BIG = 1e30
    FAR = 1e6
    MOST = g.TOK // P + 1
    s_dve, s_act, s_pool, s_pe = (g.sem("r_" + n) for n in ("dve", "act", "pool", "pe"))
    s_fill, s_sc = g.sem("r_fill"), g.sem("r_sc")
    with ExitStack() as life:
        def t(name, shape, dt=F32):
            return g.sb("r_" + name, shape, dt, at=life)

        iota_g, iota_e, iota_b = t("ig", [P, GE]), t("ie", [P, E]), t("ib", [P, MOST])
        token = t("token", [P, T17], I32)
        fill = t("fill", [P, g.COLS], I32)
        valid = t("valid", [P, T17])
        gmax, gi, sg, pg = t("gmax", [P, T17]), t("gi", [P, T17]), t("sg", [P, T17]), t("pg", [P, T17])
        dg, eg, cg, ohg = (t(n, [P, T17, GE]) for n in ("dg", "eg", "cg", "ohg"))
        le, c1, c2, eq = (t(n, [P, T17, E]) for n in ("le", "c1", "c2", "eq"))
        oh = [t(f"oh{i}", [P, T17, E]) for i in range(2)]
        m1, m2, e1, e2, dm, em, den = (t(n, [P, T17]) for n in ("m1", "m2", "e1", "e2", "dm", "em", "den"))
        chosen = t("chosen", [P, T17, E])
        before = t("before", [P, T17 + 1, E])
        counts, blocks, ends, starts = (t(n, [P, E]) for n in ("counts", "blocks", "ends", "starts"))
        over = t("over", [P, E, MOST])
        place = t("place", [P, T17, E])
        sel = t("sel", [P, T17, E])
        destf = t("destf", [P, 2, T17])
        tab, tab2 = t("tab", [P, 2, T17], U32), t("tab2", [P, 2, T17], U32)
        p_rank = g.psum("r_rank", [P, 512], at=life)
        p_rank2 = g.psum("r_rank2", [P, 512], at=life)
        p_cnt = g.psum("r_cnt", [P, 512], at=life)

        def over_last(a, n):
            return a.unsqueeze(2).to_broadcast([P, a.shape[1], n])

        def over_tiles(a):
            return a.unsqueeze(1).to_broadcast([P, T17, a.shape[1]])

        mark = {}
        with nc.Block() as block:
            @block.sync
            def _(sp):
                load_expert(g, sp, 0, 0)
                load_expert(g, sp, 1, 1)

            @block.vector
            def _(dve):
                V = nc.vector
                link = Steps(s_dve, dve, 10 ** 6)
                link.begin(0)
                L = link.link
                dve.wait_ge(s_pool, 6)
                lg = g.logits[:, :, 0:GE]
                L(V.tensor_reduce(gmax[:], lg, AX, ALU.max))
                L(V.tensor_tensor(dg[:], lg, over_last(gmax[:], GE), ALU.subtract))
                mark['group'] = link.k
                L(V.tensor_scalar(cg[:], dg[:], 0.0, -FAR, ALU.is_equal, ALU.mult))
                L(V.tensor_tensor(cg[:], cg[:], over_tiles(iota_g[:]), ALU.add))
                L(V.tensor_reduce(gi[:], cg[:], AX, ALU.min))
                L(V.tensor_tensor(ohg[:], cg[:], over_last(gi[:], GE), ALU.is_equal))
                L(V.tensor_scalar(cg[:], ohg[:], -1.0, BIG, ALU.add, ALU.mult))
                L(V.tensor_tensor(le[:].rearrange("p t (g e) -> p t g e", g=GE), g.logits[:, :, GE:].rearrange("p t (g e) -> p t g e", g=GE),
                                  cg[:].unsqueeze(3).to_broadcast([P, T17, GE, PER]), ALU.add))
                for i, (top, idx) in enumerate(((m1, e1), (m2, e2))):
                    L(V.tensor_reduce(top[:], le[:], AX, ALU.max))
                    L(V.tensor_tensor(eq[:], le[:], over_last(top[:], E), ALU.is_equal))
                    L(V.tensor_scalar(c1[:], eq[:], -FAR, None, ALU.mult))
                    L(V.tensor_tensor(c1[:], c1[:], over_tiles(iota_e[:]), ALU.add))
                    L(V.tensor_reduce(idx[:], c1[:], AX, ALU.min))
                    L(V.tensor_tensor(oh[i][:], c1[:], over_last(idx[:], E), ALU.is_equal))
                    if i == 0:
                        L(V.scalar_tensor_tensor(out=le[:].rearrange("p t e -> p (t e)"), in0=oh[0][:].rearrange("p t e -> p (t e)"), scalar=-2 * BIG,
                                                 in1=le[:].rearrange("p t e -> p (t e)"), op0=ALU.mult, op1=ALU.add))
                L(V.tensor_tensor(dm[:], m2[:], m1[:], ALU.subtract))
                mark['pair'] = link.k
                L(V.tensor_tensor(chosen[:], oh[0][:], oh[1][:], ALU.add))
                L(V.tensor_tensor(chosen[:], chosen[:], over_last(valid[:], E), ALU.mult))
                L(V.memset(before[:, 0, :], 0.0))
                for tile in range(T17):
                    L(V.tensor_tensor(before[:, tile + 1, :], before[:, tile, :], chosen[:, tile, :], ALU.add))
                mark['chosen'] = link.k
                dve.wait_ge(s_act, 2)
                L(V.tensor_reduce(sg[:], eg[:], AX, ALU.add))
                L(V.reciprocal(pg[:], sg[:]))
                L(V.tensor_scalar(den[:], em[:], 1.0, None, ALU.add))
                L(V.reciprocal(den[:], den[:]))
                L(V.tensor_tensor(g.weight[:, 0, :], den[:], pg[:], ALU.mult))
                L(V.tensor_tensor(g.weight[:, 1, :], g.weight[:, 0, :], em[:], ALU.mult))
                dve.wait_ge(s_pe, 1)
                L(V.tensor_copy(counts[:], p_cnt[:, 0:E]))
                L(V.tensor_tensor(over[:], over_last(counts[:], MOST), iota_b[:].unsqueeze(1).to_broadcast([P, E, MOST]), ALU.is_gt))
                L(V.tensor_reduce(blocks[:], over[:], AX, ALU.add))
                L(V.tensor_scalar(blocks[:], blocks[:], 1.0, None, ALU.max))
                L(V.tensor_tensor_scan(ends[:], g.ones[:, 0:E], blocks[:], 0.0, ALU.mult, ALU.add))
                L(V.tensor_tensor(starts[:], ends[:], blocks[:], ALU.subtract))
                L(V.memset(g.bounds[:], 0.0))
                L(V.tensor_copy(g.bounds[:, 1:E + 1], ends[0:1, :]))
                L(V.tensor_scalar(starts[:], starts[:], float(P), -1.0, ALU.mult, ALU.add))
                L(V.tensor_tensor(place[:, 0:16, :], p_rank[:].rearrange("p (t e) -> p t e", e=E), starts[:].unsqueeze(1).to_broadcast([P, 16, E]), ALU.add))
                L(V.tensor_tensor(place[:, 16, :], p_rank2[:, 0:E], starts[:], ALU.add))
                for i in range(2):
                    L(V.tensor_tensor(sel[:], oh[i][:], place[:], ALU.mult))
                    L(V.tensor_reduce(destf[:, i, :], sel[:], AX, ALU.add))
                L(V.tensor_copy(g.dest[:], destf[:]))
                L(V.tensor_single_scalar(tab[:], g.dest[:], P - 1, ALU.bitwise_and))
                L(V.tensor_single_scalar(tab2[:], g.dest[:], 7, ALU.logical_shift_right))
                L(V.tensor_scalar(tab[:], tab[:], float(g.COLS), None, ALU.mult))
                L(V.tensor_tensor(g.slot[:], tab[:], tab2[:], ALU.add))
                mark['places'] = link.k

            @block.gpsimd
            def _(pool):
                G = nc.gpsimd
                G.iota(iota_g[:], pattern=[[1, GE]], base=0, channel_multiplier=0, allow_small_or_imprecise_dtypes=True).then_inc(s_pool, 1)
                G.iota(iota_e[:], pattern=[[1, E]], base=0, channel_multiplier=0, allow_small_or_imprecise_dtypes=True).then_inc(s_pool, 1)
                G.iota(iota_b[:], pattern=[[P, MOST]], base=0, channel_multiplier=0, allow_small_or_imprecise_dtypes=True).then_inc(s_pool, 1)
                G.iota(token[:], pattern=[[P, T17]], base=0, channel_multiplier=1).then_inc(s_pool, 1)
                G.iota(fill[:], pattern=[[0, g.COLS]], base=g.TOK, channel_multiplier=0).then_inc(s_pool, 1)
                G.affine_select(out=valid[:], in_=g.ones[:, 0:T17], compare_op=ALU.is_gt, fill=0.0, base=g.TOK,
                                pattern=[[-P, T17]], channel_multiplier=-1).then_inc(s_pool, 1)
                pool.wait_ge(s_pool, 6)
                pool.dma_start(g.token_d, fill[:]).then_inc(s_fill, 16)
                pool.wait_ge(s_fill, 16)
                pool.wait_ge(s_dve, mark['places'])
                table = g.token_d.rearrange("p (b o) -> (p b) o", o=1)
                for tile in range(T17):
                    n = NEW if tile == g.TILES else P
                    for i in range(2):
                        G.indirect_dma_start(out=table, out_offset=bass.IndirectOffsetOnAxis(ap=g.slot[0:n, i, tile:tile + 1], axis=0),
                                             in_=token[0:n, tile:tile + 1], in_offset=None).then_inc(s_sc, 16)
                pool.wait_ge(s_sc, 32 * T17)

            @block.scalar
            def _(act):
                act.wait_ge(s_dve, mark['group'])
                nc.scalar.activation(eg[:], dg[:], ACT.Exp).then_inc(s_act, 1)
                act.wait_ge(s_dve, mark['pair'])
                nc.scalar.activation(em[:], dm[:], ACT.Exp).then_inc(s_act, 1)

            @block.tensor
            def _(pe):
                pe.wait_ge(s_dve, mark['chosen'])
                for out, a, b in ((p_rank, 0, 16), (p_rank2, 16, T17)):
                    n = (b - a) * E
                    nc.tensor.matmul(out[:, 0:n], g.upto[:], chosen[:, a:b, :].rearrange("p t e -> p (t e)"), start=True, stop=False)
                    nc.tensor.matmul(out[:, 0:n], g.ones[:], before[:, a:b, :].rearrange("p t e -> p (t e)"), start=False, stop=True)
                nc.tensor.matmul(p_cnt[:, 0:E], g.ones[:], before[:, T17, :], start=True, stop=True).then_inc(s_pe, 1)


def load_expert(g, sp, e, buf):
    wg, wu, wd = g.expert_w
    s_wg, s_wd = g.s_expert
    for w, src in ((wg, "w_gate"), (wu, "w_up")):
        sp.dma_start(w[:, buf], g.ins[src][0, bass.ds(e, 1)].rearrange("a (k p) f -> p (a k) f", p=P)).then_inc(s_wg[buf], 16)
    sp.dma_start(wd[:, buf], g.ins["w_down"][0, bass.ds(e, 1)].rearrange("a (k p) d -> p (a k) d", p=P)).then_inc(s_wd[buf], 16)


def experts(nc, g):
    D, KT, E = g.D, g.KT, g.EXPERTS
    F = g.ins["w_gate"].shape[3]
    FT = F // P
    s_wg, s_wd = g.s_expert
    s_tab, s_stored = g.sem("e_tab"), g.sem("e_stored")
    s_idx, s_started, s_x, s_y = g.sem("e_idx"), g.sem("e_started"), g.sem("e_x"), g.sem("e_y")
    s_xt, s_gate, s_up, s_ht, s_down = [g.sem("e_xt0"), g.sem("e_xt1")], *(g.sem("e_" + n) for n in ("gate", "up", "ht", "down"))
    s_silu, s_h, s_hTs, s_xe0, s_xe1, s_ye0, s_ye1 = (g.sem("e_" + n) for n in ("silu", "h", "hTs", "xe0", "xe1", "ye0", "ye1"))
    HALF = KT // 2
    with ExitStack() as life:
        wg, wu, wd = g.expert_w
        table = g.sb("e_table", [P, g.COLS], I32, at=life)
        idx = g.sb("e_idx_", [P, 1], U32, at=life)
        x = g.sb("e_x_", [P, D], at=life)
        xT = g.sb("e_xT", [P, KT, P], at=life)
        sg = g.sb("e_sg", [P, F], at=life)
        h = g.sb("e_h_", [P, F], at=life)
        hT = g.sb("e_hT", [P, FT, P], at=life)
        y = g.sb("e_y_", [P, D], at=life)
        p_x = [g.psum(f"e_px{i}", [P, HALF, P], at=life) for i in range(2)]
        p_g = g.psum("e_pg", [P, F], at=life)
        p_u = g.psum("e_pu", [P, F], at=life)
        p_h = g.psum("e_ph", [P, FT, P], at=life)
        p_y = [g.psum(f"e_py{i}", [P, D // 2], at=life) for i in range(2)]

        def bound(eng, e):
            return eng.value_load(g.bounds[0:1, bass.ds(e, 1)], min_val=0, max_val=g.BLOCKS)

        def blocks_of(eng, e, body):
            first, last = bound(eng, e), bound(eng, e + 1)
            with eng.Fori(first, last) as b:
                body(b)

        with nc.Block() as block:
            @block.sync
            def _(sp):
                sp.dma_start(table[:], g.token_d).then_inc(s_tab, 16)

                with sp.Fori(1, E // 2) as pair:
                    for buf in range(2):
                        sp.wait_ge(s_down, bound(sp, pair * 2 + buf - 1))
                        load_expert(g, sp, pair * 2 + buf, buf)

            @block.gpsimd
            def _(pool):
                with pool.Fori(0, bound(pool, E) + 1) as b:
                    pool.wait_ge(s_idx, b + 1)
                    pool.sem_inc(s_started, 1)
                    nc.gpsimd.indirect_dma_start(out=x[:], out_offset=None, in_=g.h2_d,
                                                 in_offset=bass.IndirectOffsetOnAxis(ap=idx[:], axis=0)).then_inc(s_x, 16)

            @block.tensor
            def _(pe):
                def turn_rows(b, half):
                    if half == 0:
                        pe.wait_ge(s_x, b * 16 + 16)
                    for k in range(half * HALF, (half + 1) * HALF):
                        tr = nc.tensor.transpose(p_x[half][:, k % HALF, :], x[:, k * P:(k + 1) * P], g.ident[:])
                    tr.then_inc(s_xt[half], 1)

                turn_rows(0, 0)
                turn_rows(0, 1)

                def multiply(pair, buf, b):
                    pe.wait_ge(s_wg[buf], pair * 32 + 32)
                    pe.wait_ge(s_xe0, b + 1)
                    pe.wait_ge(s_xe1, b + 1)
                    for out, w, done in ((p_g, wg, s_gate), (p_u, wu, s_up)):
                        for k in range(KT):
                            mm = nc.tensor.matmul(out[:], xT[:, k, :], w[:, buf, k, :], start=(k == 0), stop=(k == KT - 1))
                        mm.then_inc(done, 1)
                    turn_rows(b + 1, 0)
                    pe.wait_ge(s_h, b + 1)
                    for f in range(FT):
                        tr = nc.tensor.transpose(p_h[:, f, :], h[:, f * P:(f + 1) * P], g.ident[:])
                    tr.then_inc(s_ht, 1)
                    turn_rows(b + 1, 1)
                    pe.wait_ge(s_wd[buf], pair * 16 + 16)
                    pe.wait_ge(s_hTs, b + 1)
                    for c in range(2):
                        for f in range(FT):
                            mm = nc.tensor.matmul(p_y[c][:], hT[:, f, :], wd[:, buf, f, c * (D // 2):(c + 1) * (D // 2)],
                                                  start=(f == 0), stop=(f == FT - 1))
                    mm.then_inc(s_down, 1)

                with pe.Fori(0, E // 2) as pair:
                    for buf in range(2):
                        blocks_of(pe, pair * 2 + buf, lambda b: multiply(pair, buf, b))

            @block.scalar
            def _(act):
                def take_x(b):
                    act.wait_ge(s_xt[0], b + 1)
                    nc.scalar.copy(xT[:, 0:HALF, :], p_x[0][:]).then_inc(s_xe0, 1)

                take_x(0)

                def body(b):
                    act.wait_ge(s_gate, b + 1)
                    nc.scalar.activation(sg[:], p_g[:], ACT.Silu).then_inc(s_silu, 1)
                    act.wait_ge(s_up, b + 1)
                    take_x(b + 1)
                    act.wait_ge(s_ht, b + 1)
                    nc.scalar.copy(hT[:], p_h[:]).then_inc(s_hTs, 1)
                    if not isinstance(b, int):
                        act.wait_ge(s_y, b * 16)
                    act.wait_ge(s_down, b + 1)
                    nc.scalar.copy(y[:, 0:D // 2], p_y[0][:]).then_inc(s_ye0, 1)
                    act.wait_ge(s_ye0, b + 1)
                    act.wait_ge(s_ye1, b + 1)
                    act.dma_start(g.y_d[bass.ds(b * P, P), :], y[:]).then_inc(s_y, 16)

                body(0)
                with act.Fori(1, bound(act, E)) as b:
                    body(b)
                act.wait_ge(s_y, bound(act, E) * 16)
                act.sem_inc(s_stored, 1)

            @block.vector
            def _(dve):
                def take_x(b):
                    dve.wait_ge(s_xt[1], b + 1)
                    nc.vector.tensor_copy(xT[:, HALF:, :], p_x[1][:]).then_inc(s_xe1, 1)

                def name_rows(b):
                    nc.vector.tensor_scalar(idx[:], table[:, bass.ds(b, 1)], 0.0, None, ALU.add).then_inc(s_idx, 1)

                dve.wait_ge(s_tab, 16)
                name_rows(0)
                take_x(0)
                dve.wait_ge(s_idx, 1)
                name_rows(1)

                def body(b):
                    dve.wait_ge(s_silu, b + 1)
                    dve.wait_ge(s_up, b + 1)
                    nc.vector.tensor_tensor(h[:], sg[:], p_u[:], ALU.mult).then_inc(s_h, 1)
                    take_x(b + 1)
                    dve.wait_ge(s_idx, b + 2)
                    name_rows(b + 2)
                    if not isinstance(b, int):
                        dve.wait_ge(s_y, b * 16)
                    dve.wait_ge(s_down, b + 1)
                    nc.vector.tensor_copy(y[:, D // 2:], p_y[1][:]).then_inc(s_ye1, 1)

                body(0)
                with dve.Fori(1, bound(dve, E)) as b:
                    body(b)


def combine(nc, g):
    D, NEW = g.D, g.NEW
    GT = 5
    s_rows, s_idx, s_started, s_y0, s_y1, s_x2, s_out, s_link = (g.sem("o_" + n) for n in
                                                               ("rows", "idx", "started", "y0", "y1", "x2", "out", "link"))
    by_dve = Line(g.sem("o_dve"), ["w0", "w1", "mean", "gated", "out"])
    s_sq, s_r = g.sem("o_sq"), g.sem("o_r")
    with ExitStack() as life:
        post = [g.sb(f"o_post{a}", [P, D], at=life) for a in range(2)]
        gain = g.sb("o_gain", [P, D], at=life)
        idx = [g.sb(f"o_idx{i}", [P, 1], U32, at=life) for i in range(2)]
        rows = [g.sb(f"o_row{i}", [P, D], at=life) for i in range(2)]
        t0, t1, junk, gated, x2, out = (g.sb("o_" + n, [P, D], at=life) for n in ("t0", "t1", "junk", "gated", "x2_", "out_"))
        ss, sn, r = (g.sb("o_" + n, [P, 1], at=life) for n in ("ss", "sn", "rr"))

        def shape(turn):
            first = isinstance(turn, int)
            return not first, (NEW if first else P), (g.TILES if first else turn - 1),                 (slice(g.SEQ, g.TOK) if first else bass.ds((turn - 1) * P, P))

        def turns(eng, body):
            body(0)
            with eng.Fori(1, g.TILES + 1) as turn:
                body(turn)

        with nc.Block() as block:
            @block.sync
            def _(sp):
                for a in range(2):
                    sp.dma_start(post[a][:], g.mod_d[a, GT * D:(GT + 1) * D].partition_broadcast(P)).then_inc(s_rows, 16)
                sp.dma_start(gain[:], g.ins["g_post_ffn"][0].partition_broadcast(P)).then_inc(s_rows, 16)

                def body(turn):
                    later, n, tile, at = shape(turn)
                    if later:
                        sp.wait_ge(by_dve.sem, by_dve(turn - 1, "out"))
                    sp.dma_start(x2[0:n], g.x2_d[at, :]).then_inc(s_x2, 16)

                turns(sp, body)

            @block.gpsimd
            def _(pool):
                def body(turn):
                    later, n, tile, at = shape(turn)
                    pool.wait_ge(s_idx, 2 * turn + 2)
                    pool.sem_inc(s_started, 1)
                    for i, done in enumerate((s_y0, s_y1)):
                        nc.gpsimd.indirect_dma_start(out=rows[i][0:n], out_offset=None, in_=g.y_d,
                                                     in_offset=bass.IndirectOffsetOnAxis(ap=idx[i][0:n], axis=0)).then_inc(done, 16)
                    pool.wait_ge(by_dve.sem, by_dve(turn, "mean"))
                    nc.gpsimd.tensor_tensor(r[0:n], sn[0:n], g.half[0:n, 0:1], ALU.pow).then_inc(s_r, 1)
                    if not later:
                        pool.wait_ge(s_r, 1)

                turns(pool, body)

            @block.scalar
            def _(act):
                def body(turn):
                    later, n, tile, at = shape(turn)
                    act.wait_ge(by_dve.sem, by_dve(turn, "w1"))
                    if later:
                        act.wait_ge(s_sq, turn)
                    nc.scalar.activation(junk[0:n], t1[0:n], ACT.Square, accum_out=ss[0:n]).then_inc(s_sq, 1)
                    act.wait_ge(by_dve.sem, by_dve(turn, "out"))
                    act.dma_start(g.outs["y_prompt"][at, :] if later else g.outs["y_sample"], out[0:n]).then_inc(s_out, 16)

                turns(act, body)
                act.wait_ge(s_out, g.T17 * 16)

            @block.vector
            def _(dve):
                V = nc.vector
                link = Steps(s_link, dve, 2)
                link.begin(0)
                dve.wait_ge(s_rows, 48)
                for a in range(2):
                    link.link(V.tensor_tensor(post[a][:], post[a][:], gain[:], ALU.mult))

                def name_rows(turn):
                    tile = g.TILES if isinstance(turn, int) and turn == 0 else (turn - 1)
                    for i in range(2):
                        V.tensor_scalar(idx[i][:], g.dest[:, i, bass.ds(tile, 1)], 0.0, None, ALU.add).then_inc(s_idx, 1)

                def body(turn):
                    later, n, tile, at = shape(turn)
                    grp = 0 if later else 1

                    def did(name):
                        return by_dve.sem, by_dve.did(name)

                    dve.wait_ge(s_y0, (turn + 1) * 16)
                    V.tensor_scalar(t0[0:n], rows[0][0:n], g.weight[0:n, 0, bass.ds(tile, 1)], None, ALU.mult).then_inc(*did("w0"))
                    dve.wait_ge(s_y1, (turn + 1) * 16)
                    dve.wait_ge(by_dve.sem, by_dve(turn, "w0"))
                    V.scalar_tensor_tensor(out=t1[0:n], in0=rows[1][0:n], scalar=g.weight[0:n, 1, bass.ds(tile, 1)], in1=t0[0:n],
                                           op0=ALU.mult, op1=ALU.add).then_inc(*did("w1"))
                    dve.wait_ge(by_dve.sem, by_dve(turn, "w1"))
                    dve.wait_ge(s_idx, 2 * turn + 2)
                    name_rows(turn + 1)
                    dve.wait_ge(s_sq, turn + 1)
                    V.tensor_scalar(sn[0:n], ss[0:n], 1.0 / D, EPS, ALU.mult, ALU.add).then_inc(*did("mean"))
                    dve.wait_ge(s_r, turn + 1)
                    V.scalar_tensor_tensor(out=gated[0:n], in0=t1[0:n], scalar=r[0:n, 0:1], in1=post[grp][0:n],
                                           op0=ALU.mult, op1=ALU.mult).then_inc(*did("gated"))
                    dve.wait_ge(by_dve.sem, by_dve(turn, "gated"))
                    dve.wait_ge(s_x2, (turn + 1) * 16)
                    if later:
                        dve.wait_ge(s_out, turn * 16)
                    V.tensor_tensor(out[0:n], gated[0:n], x2[0:n], ALU.add).then_inc(*did("out"))

                name_rows(0)
                turns(dve, body)


_OUTS = [("y_prompt", (1, 2048, 1024)), ("y_sample", (1, 32, 1024)),
         ("k_prompt", (1, 1, 2048, 8, 64)), ("v_prompt", (1, 1, 2048, 8, 64)),
         ("delta_prompt", (1, 1, 4, 128, 128)), ("conv_prompt", (1, 1, 3, 1536)),
         ("k_sample", (1, 1, 32, 8, 64)), ("v_sample", (1, 1, 32, 8, 64)),
         ("delta_sample", (1, 1, 4, 128, 128)), ("conv_sample", (1, 1, 3, 1536))]


def _flat(name, ap):
    if name[0] == "y":
        return ap.rearrange("a t d -> (a t) d")
    if name[0] in "kv":
        return ap.rearrange("l b t h d -> (l b t) (h d)")
    if name[0] == "d":
        return ap.rearrange("l b h k v -> (l b h) k v")
    return ap.rearrange("l b t c -> (l b t) c")


def kernel(**inputs):
    import numpy as _np
    import concourse.bacc as _bacc
    from concourse import mybir as _mybir
    from concourse.bass_utils import run_bass_kernel_spmd as _run

    nc = _bacc.Bacc("TRN2", target_bir_lowering=False, num_devices=1)
    arrays, ins, outs = {}, {}, {}
    for name, value in inputs.items():
        a = _np.ascontiguousarray(value)
        arrays[f"in_{name}"] = a
        ins[name] = nc.dram_tensor(f"in_{name}", a.shape, _mybir.dt.from_np(a.dtype), kind="ExternalInput").ap()
    for name, shape in _OUTS:
        outs[name] = _flat(name, nc.dram_tensor(f"out_{name}", shape, _mybir.dt.float32, kind="ExternalOutput").ap())
    build(nc, ins, outs)
    r = _run(nc, [arrays], core_ids=[0])
    return tuple(r.results[0][f"out_{name}"] for name, _ in _OUTS)
```

```python
from contextlib import ExitStack

import concourse.bass as bass
from concourse import mybir

ALU = mybir.AluOpType
ACT = mybir.ActivationFunctionType
F32 = mybir.dt.float32
I32 = mybir.dt.int32
U32 = mybir.dt.uint32
AX = mybir.AxisListType.X

P = 128
EPS = 1e-6
CONV_W = 4
DN_HEADS = 4
DN_DIM = 128
SB_HEADS = 8
SB_DIM = 64


class Steps:

    def __init__(self, sem, eng, per):
        self.sem, self.eng, self.per, self.k, self.base = sem, eng, per, 0, 0

    def begin(self, turn, done=0):
        self.base, self.k = turn * self.per, done

    def link(self, ins):
        self.k += 1
        assert self.k <= self.per, (self.sem, self.per)
        ins.then_inc(self.sem, 1)
        self.eng.wait_ge(self.sem, self.base + self.k)

    def end(self):
        assert self.k == self.per, (self.sem, self.k, self.per)


class Plan:
    pass


def build(nc, ins, outs):
    g = Plan()
    g.x = [ins["x_prompt"][0], ins["x_sample"][0]]
    g.SEQ, g.D = g.x[0].shape
    g.NEW = g.x[1].shape[0]
    g.KT = g.D // P
    g.TILES = g.SEQ // P
    g.CONV_CH = ins["conv_w"].shape[2]
    g.CT = g.CONV_CH // P
    g.IN_COLS = ins["w_in"].shape[2]
    g.ROWS = SB_HEADS * SB_DIM
    g.QKT = 2 * g.ROWS // P
    g.OFF_Z = g.CONV_CH
    g.OFF_B = g.OFF_Z + DN_HEADS * DN_DIM
    g.OFF_QB = g.OFF_B + 2 * DN_HEADS
    g.OFF_VB = g.OFF_QB + 2 * g.ROWS
    g.TOK = g.SEQ + g.NEW
    g.T17 = g.TILES + 1
    g.ins, g.outs, g.nc = ins, outs, nc
    with ExitStack() as life:
        g.sb = lambda name, shape, dt=F32, at=life: at.enter_context(nc.sbuf_tensor(name, shape, dt))
        g.psum = lambda name, shape, dt=F32, at=life: at.enter_context(nc.psum_tensor(name, shape, dt))
        g.sem = lambda name: life.enter_context(nc.semaphore(name))
        g.mod_d = nc.dram_tensor("mod_d", [2, 6 * g.D], F32, kind="Internal").ap()
        g.conv_d = nc.dram_tensor("conv_d", [g.CT, P, g.TOK], F32, kind="Internal").ap()
        g.qk_d = nc.dram_tensor("qk_d", [g.QKT, P, g.TOK], F32, kind="Internal").ap()
        g.z_d = nc.dram_tensor("z_d", [g.TOK, g.ROWS], F32, kind="Internal").ap()
        g.merged_d = nc.dram_tensor("merged_d", [g.TOK, DN_HEADS * DN_DIM + g.ROWS], F32, kind="Internal").ap()
        g.ident = g.sb("ident", [P, P])
        g.bg = g.sb("bg", [P, g.T17, 2 * DN_HEADS])
        g.modT = g.sb("modT", [P, 4 * g.KT])
        constants(nc, g)
        with ExitStack() as until_projected:
            g.w_in = g.sb("w_in", [P, g.KT, g.IN_COLS], at=until_projected)
            g.s_w_in = g.sem("p_w")
            modulation(nc, g)
            projection(nc, g)
        g.ones = g.sb("ones", [P, P])
        g.half = g.sb("minus_half", [P, 2 * DN_HEADS])
        g.upto = g.sb("upto", [P, P])
        g.behind = g.sb("behind", [P, P])
        g.level = g.sb("level", [P, 8, P])
        g.GROUPS_E = g.ins["w_router_group"].shape[2]
        g.EXPERTS = g.ins["w_router_expert"].shape[2]
        g.BLOCKS = 2 * g.TOK // P + g.EXPERTS
        g.COLS = g.BLOCKS + 2
        g.x2_d = nc.dram_tensor("x2_d", [g.TOK, g.D], F32, kind="Internal").ap()
        g.h2_d = nc.dram_tensor("h2_d", [g.TOK + 1, g.D], F32, kind="Internal").ap()
        g.Y_BLOCKS = g.EXPERTS + -(-(g.BLOCKS - g.EXPERTS) // g.TILES) * g.TILES
        g.y_d = nc.dram_tensor("y_d", [g.Y_BLOCKS * P, g.D], F32, kind="Internal").ap()
        g.token_d = nc.dram_tensor("token_d", [P, g.COLS], I32, kind="Internal").ap()
        g.logits = g.sb("logits", [P, g.T17, g.GROUPS_E + g.EXPERTS])
        g.weight = g.sb("weight", [P, 2, g.T17])
        g.dest = g.sb("dest", [P, 2, g.T17], U32)
        g.slot = g.sb("slot", [P, 2, g.T17], U32)
        g.bounds = g.sb("bounds", [1, g.EXPERTS + 1], I32)
        masks(nc, g)
        delta(nc, g)
        with ExitStack() as until_mixed:
            R = g.EXPERTS + g.GROUPS_E
            g.w_out = g.sb("w_out", [P, g.KT, g.D], at=until_mixed)
            g.w_router = g.sb("w_router", [P, g.KT, R], at=until_mixed)
            g.b_router = g.sb("b_router", [P, R], at=until_mixed)
            g.post, g.scale, g.shift = ([g.sb(f"x_{n}{a}", [P, g.D], at=until_mixed) for a in range(2)] for n in ("post", "scale", "shift"))
            g.gains = g.sb("x_gains", [P, 2, g.D], at=until_mixed)
            g.s_w_mixed, g.s_rows_mixed = g.sem("x_w"), g.sem("x_rows")
            sticks(nc, g)
            mixed(nc, g)
        with ExitStack() as until_combine:
            F = ins["w_gate"].shape[3]
            g.expert_w = [g.sb("e_wg", [P, 2, g.KT, F], at=until_combine), g.sb("e_wu", [P, 2, g.KT, F], at=until_combine),
                          g.sb("e_wd", [P, 2, F // P, g.D], at=until_combine)]
            g.s_expert = [g.sem("e_wg0"), g.sem("e_wg1")], [g.sem("e_wd0"), g.sem("e_wd1")]
            routing(nc, g)
            experts(nc, g)
        combine(nc, g)


def constants(nc, g):
    s_cleared, s_ident = g.sem("s_cleared"), g.sem("s_ident")
    with nc.Block() as block:
        @block.gpsimd
        def _(pool):
            nc.gpsimd.memset(g.ident[:], 0.0).then_inc(s_cleared, 1)
            pool.wait_ge(s_cleared, 1)
            nc.gpsimd.affine_select(out=g.ident[:], in_=g.ident[:], compare_op=ALU.not_equal, fill=1.0,
                                    base=0, pattern=[[-1, P]], channel_multiplier=1).then_inc(s_ident, 1)
            nc.gpsimd.memset(g.bg[:], 0.0).then_inc(s_ident, 1)
            pool.wait_ge(s_ident, 2)


def masks(nc, g):
    s_set, s_tri = g.sem("k_set"), g.sem("k_tri")
    LEVELS = 7
    with nc.sbuf_tensor("row_no", [P, P], I32) as row_no, nc.sbuf_tensor("col_no", [P, P], I32) as col_no, \
            nc.sbuf_tensor("xor", [P, P], I32) as xor, nc.sbuf_tensor("xor_f", [P, P], F32) as xor_f, \
            nc.sbuf_tensor("below", [P, 2, P], F32) as below, nc.Block() as block:
        @block.vector
        def _(dve):
            link = Steps(g.sem("k_link"), dve, 2 + 3 * (LEVELS + 1))
            link.begin(0)
            dve.wait_ge(s_tri, 6)
            link.link(nc.vector.tensor_tensor(xor[:], row_no[:], col_no[:], ALU.bitwise_xor))
            link.link(nc.vector.tensor_copy(xor_f[:], xor[:]))
            for l in range(LEVELS + 1):
                low = 2 ** (l % LEVELS)
                link.link(nc.vector.tensor_scalar(g.level[:, l, :], xor_f[:], float(low), None, ALU.is_ge))
                link.link(nc.vector.scalar_tensor_tensor(out=g.level[:, l, :], in0=xor_f[:], scalar=float(2 * low), in1=g.level[:, l, :],
                                                         op0=ALU.is_lt, op1=ALU.mult))
                link.link(nc.vector.tensor_tensor(g.level[:, l, :], g.level[:, l, :], below[:, l // LEVELS, :], ALU.mult))

        @block.gpsimd
        def _(pool):
            nc.gpsimd.memset(g.half[:], -0.5).then_inc(s_set, 1)
            nc.gpsimd.memset(g.ones[:], 1.0).then_inc(s_set, 1)
            pool.wait_ge(s_set, 2)
            for out, sign, least in ((g.upto[:], -1, 0), (g.behind[:], 1, 1), (below[:, 0, :], 1, 1), (below[:, 1, :], -1, 1)):
                nc.gpsimd.affine_select(out=out, in_=g.ones[:], compare_op=ALU.is_ge, fill=0.0, base=-least,
                                        pattern=[[-sign, P]], channel_multiplier=sign).then_inc(s_tri, 1)
            nc.gpsimd.iota(row_no[:], pattern=[[0, P]], base=0, channel_multiplier=1).then_inc(s_tri, 1)
            nc.gpsimd.iota(col_no[:], pattern=[[1, P]], base=0, channel_multiplier=0).then_inc(s_tri, 1)


def modulation(nc, g):
    KT, D = g.KT, g.D
    WIDE = 512
    CHUNKS = 6 * D // WIDE
    w_ada = g.ins["w_ada"][0].rearrange("(k p) n -> p k n", p=P)
    s_c, s_w = g.sem("m_c"), [g.sem("m_w0"), g.sem("m_w1")]
    s_gain = g.sem("m_gain")
    s_silu, s_cT, s_cTs = g.sem("m_silu"), g.sem("m_cT"), g.sem("m_cTs")
    s_mm, s_add, s_row = g.sem("m_mm"), g.sem("m_add"), g.sem("m_row")
    s_tr, s_col = g.sem("m_tr"), g.sem("m_col")
    with ExitStack() as life:
        c_rows = g.sb("c_rows", [2, D], at=life)
        c_silu = g.sb("c_silu", [2, D], at=life)
        cT = g.sb("cT", [P, KT, 2], at=life)
        w = [g.sb(f"w_ada{b}", [P, KT, WIDE], at=life) for b in range(2)]
        rows = bias = g.sb("mod_rows", [2, 6 * D], at=life)
        gain_rows = g.sb("gain_rows", [KT, P], at=life)
        gain = g.sb("gain_cols", [P, KT], at=life)
        cols = g.sb("mod_cols", [P, 2 * KT, 2], at=life)
        p_c = g.psum("m_pc", [P, 512], at=life)
        p_mod = [g.psum(f"m_pm{b}", [2, WIDE], at=life) for b in range(2)]
        p_col = g.psum("m_pcol", [P, 512], at=life)
        with nc.Block() as block:
            @block.sync
            def _(sp):
                sp.dma_start(c_rows[0:1, :], g.ins["c_prompt"]).then_inc(s_c, 16)
                sp.dma_start(c_rows[1:2, :], g.ins["c_sample"]).then_inc(s_c, 16)
                for r in range(2):
                    sp.dma_start(bias[r:r + 1, :], g.ins["b_ada"]).then_inc(s_c, 16)
                sp.dma_start(gain_rows[:], g.ins["g_pre_mix"][0].rearrange("(k p) -> k p", p=P)).then_inc(s_gain, 16)
                for b in range(2):
                    sp.dma_start(w[b][:], w_ada[:, :, b * WIDE:(b + 1) * WIDE]).then_inc(s_w[b], 16)
                with sp.Fori(1, CHUNKS // 2) as i:
                    for b in range(2):
                        sp.wait_ge(s_mm, 2 * i - 1 + b)
                        sp.dma_start(w[b][:], w_ada[:, :, bass.ds(i * (2 * WIDE) + b * WIDE, WIDE)]).then_inc(s_w[b], 16)

            @block.scalar
            def _(act):
                w_in = g.ins["w_in"][0].rearrange("(k p) n -> p k n", p=P)
                for k in range(KT):
                    act.dma_start(g.w_in[:, k, :], w_in[:, k, :]).then_inc(g.s_w_in, 16)
                act.wait_ge(s_c, 64)
                nc.scalar.activation(c_silu[:], c_rows[:], ACT.Silu).then_inc(s_silu, 1)
                act.wait_ge(s_add, CHUNKS)
                act.dma_start(g.mod_d, rows[:]).then_inc(s_row, 16)
                act.wait_ge(s_row, 16)

            @block.tensor
            def _(pe):
                pe.wait_ge(s_silu, 1)
                for k in range(KT):
                    last = nc.tensor.transpose(p_c[:, 2 * k:2 * k + 2], c_silu[:, k * P:(k + 1) * P], g.ident[0:2, 0:2])
                last.then_inc(s_cT, 1)
                pe.wait_ge(s_cTs, 1)

                def chunk(b):
                    for k in range(KT):
                        mm = nc.tensor.matmul(p_mod[b][:], cT[:, k, :], w[b][:, k, :], start=(k == 0), stop=(k == KT - 1))
                    mm.then_inc(s_mm, 1)

                for b in range(2):
                    pe.wait_ge(s_w[b], 16)
                    chunk(b)
                with pe.Fori(1, CHUNKS // 2) as i:
                    for b in range(2):
                        pe.wait_ge(s_w[b], 16 * i + 16)
                        pe.wait_ge(s_add, 2 * i - 1 + b)
                        chunk(b)
                pe.wait_ge(s_add, CHUNKS)
                for j in range(2 * KT):
                    nc.tensor.transpose(p_col[:, 2 * j:2 * j + 2], rows[:, j * P:(j + 1) * P], g.ident[0:2, 0:2])
                pe.wait_ge(s_gain, 16)
                nc.tensor.transpose(p_col[:, 4 * KT:5 * KT], gain_rows[:], g.ident[0:KT, 0:KT]).then_inc(s_tr, 1)

            @block.vector
            def _(dve):
                dve.wait_ge(s_cT, 1)
                nc.vector.tensor_copy(cT[:].rearrange("p k c -> p (k c)"), p_c[:, 0:2 * KT]).then_inc(s_cTs, 1)
                dve.wait_ge(s_c, 64)

                def add(b, at):
                    nc.vector.tensor_tensor(rows[:, at], p_mod[b][:], bias[:, at], ALU.add).then_inc(s_add, 1)

                with dve.Fori(0, CHUNKS // 2) as i:
                    for b in range(2):
                        dve.wait_ge(s_mm, 2 * i + 1 + b)
                        add(b, bass.ds(i * (2 * WIDE) + b * WIDE, WIDE))
                dve.wait_ge(s_tr, 1)
                nc.vector.tensor_copy(cols[:].rearrange("p k c -> p (k c)"), p_col[:, 0:4 * KT]).then_inc(s_col, 1)
                nc.vector.tensor_copy(gain[:], p_col[:, 4 * KT:5 * KT]).then_inc(s_col, 1)
                dve.wait_ge(s_col, 2)
                for grp in range(2):
                    at = grp * 2 * KT
                    nc.vector.scalar_tensor_tensor(out=g.modT[:, at:at + KT], in0=cols[:, KT:2 * KT, grp], scalar=1.0,
                                                   in1=gain[:], op0=ALU.add, op1=ALU.mult).then_inc(s_col, 1)
                    nc.vector.tensor_copy(g.modT[:, at + KT:at + 2 * KT], cols[:, 0:KT, grp]).then_inc(s_col, 1)
                dve.wait_ge(s_col, 6)


def projection(nc, g):
    KT, D, CT, QKT, NEW = g.KT, g.D, g.CT, g.QKT, g.NEW
    SLAB = 512
    TT = SLAB // P
    SLABS = g.SEQ // SLAB
    HIST = CONV_W - 1
    T_GROUPS = CT + QKT
    R_GROUPS = 2 * TT
    GROUPS = T_GROUPS + R_GROUPS
    BANKS = 3
    KTILES = QKT // 2
    s_w, s_small = g.s_w_in, g.sem("p_small")
    s_x, s_sq, s_std, s_xn = [g.sem(f"p_x{t}") for t in range(TT)], g.sem("p_sq"), g.sem("p_std"), g.sem("p_xn")
    s_xt, s_h, s_h2, s_mm, s_ev = g.sem("p_xt"), g.sem("p_h"), g.sem("p_h2"), g.sem("p_mm"), g.sem("p_ev")
    s_bgm, s_bg, s_link, s_silu = g.sem("p_bgm"), g.sem("p_bg"), g.sem("p_link"), g.sem("p_silu")
    s_kt, s_kr, s_carry, s_tail = g.sem("p_kt"), g.sem("p_kr"), g.sem("p_carry"), g.sem("p_tail")
    CHAIN = 1 + CONV_W * CT
    s_co, s_qo = [g.sem("p_co0"), g.sem("p_co1")], [g.sem(f"p_qo{b}") for b in range(4)]
    s_zo, s_vo, s_ko, s_to, s_trt, s_wc = g.sem("p_zo"), g.sem("p_vo"), g.sem("p_ko"), g.sem("p_to"), g.sem("p_trt"), g.sem("p_wc")
    with ExitStack() as life:
        w = g.w_in
        x = g.sb("x_in", [P, TT, D], at=life)
        hT = g.sb("hT", [P, KT, SLAB], at=life)
        junk = g.sb("junk", [P, D], at=life)
        sq = g.sb("sq", [P, TT], at=life)
        std = g.sb("std", [P, TT], at=life)
        rstd = g.sb("rstd", [P, TT], at=life)
        raw = g.sb("raw", [P, CT, HIST + SLAB], at=life)
        acc = g.sb("conv_acc", [P, 2, SLAB], at=life)
        conv = g.sb("conv_out", [P, 2, SLAB], at=life)
        qk = g.sb("qk_out", [P, 4, SLAB], at=life)
        zv = g.sb("zv_out", [P, 4, g.ROWS], at=life)
        krow = g.sb("k_rows", [P, TT, g.ROWS], at=life)
        small = krow[0:HIST + CONV_W].rearrange("p t n -> p (t n)")[:, 0:g.CONV_CH]
        cw = g.sb("conv_cols", [P, CT, HIST + CONV_W], at=life)
        tail = g.sb("tail", [P, CT, 2 * HIST], at=life)
        tail_rows = x[0:2 * HIST].rearrange("p t n -> p (t n)")[:, 0:g.CONV_CH]
        eps = g.sb("eps_p", [P, 1], at=life)
        p_x = g.psum("p_px", [P, KT, P], at=life)
        p_mm = [g.psum(f"p_pm{b}", [P, 512], at=life) for b in range(BANKS)]
        p_bg = g.psum("p_pbg", [P, 512], at=life)
        p_kt = [g.psum(f"p_pk{b}", [P, TT, P], at=life) for b in range(2)]

        def first(turn):
            return isinstance(turn, int) and turn == 0

        def slab_shape(turn):
            return (1, NEW, 1, NEW) if first(turn) else (0, P, TT, SLAB)

        def tokens(turn, n):
            return bass.ds(g.SEQ, n) if first(turn) else bass.ds((turn - 1) * SLAB, n)

        def last_of(tiles, zi):
            return 1 + 2 * (TT - tiles) * zi

        def slabs(body, prepare, eng):
            prepare(0)
            body(0, lambda: prepare(1))
            with eng.Fori(1, SLABS) as turn:
                body(turn, lambda: prepare(turn + 1))
            body(SLABS, lambda: None)

        with nc.Block() as block:
            @block.sync
            def _(sp):
                sp.dma_start(small[0:HIST, :], g.ins["state_conv"][0, 0]).then_inc(s_small, 16)
                sp.dma_start(small[HIST:, :], g.ins["conv_w"][0]).then_inc(s_small, 16)

                def load_x(turn):
                    grp, rows, tiles, _ = slab_shape(turn)
                    for t in range(TT):
                        if not first(turn):
                            sp.wait_ge(s_xt, turn * TT)
                        if t < tiles:
                            src = g.x[1] if grp else g.x[0][bass.ds((turn - 1) * SLAB + t * P, P), :]
                            sp.dma_start(x[0:rows, t, :], src).then_inc(s_x[t], 16)

                load_x(0)
                with sp.Fori(1, SLABS + 1) as turn:
                    load_x(turn)

            @block.scalar
            def _(act):
                def prepare(turn):
                    grp, rows, tiles, n = slab_shape(turn)
                    for t in range(tiles):
                        act.wait_ge(s_x[t], (turn + (t == 0)) * 16)
                        if t or not grp:
                            act.wait_ge(s_sq, turn * TT + t)
                        nc.scalar.activation(junk[0:rows, :], x[0:rows, t, :], ACT.Square,
                                             accum_out=sq[0:rows, t:t + 1]).then_inc(s_sq, TT // tiles)
                    if first(turn):
                        act.wait_ge(s_wc, 2)
                    act.wait_ge(s_sq, (turn + 1) * TT)
                    if not first(turn):
                        act.wait_ge(s_link, (turn - 1) * CHAIN + 1)
                    nc.scalar.activation(std[0:rows, 0:tiles], sq[0:rows, 0:tiles], ACT.Sqrt, bias=eps[0:rows, :],
                                         scale=1.0 / D).then_inc(s_std, 1)

                def convolved(turn, n, c):
                    act.wait_ge(s_link, turn * CHAIN + 1 + CONV_W * (c + 1))
                    stored = turn * (CT // 2) + c // 2
                    if not isinstance(stored, int) or stored > 0:
                        act.wait_ge(s_co[c % 2], stored * 16)
                    nc.scalar.activation(conv[:, c % 2, 0:n], acc[:, c % 2, 0:n], ACT.Silu).then_inc(s_silu, 1)
                    act.wait_ge(s_silu, turn * CT + c + 1)
                    act.dma_start(g.conv_d[c, :, tokens(turn, n)], conv[:, c % 2, 0:n]).then_inc(s_co[c % 2], 16)

                def body(turn, prepare_next):
                    grp, rows, tiles, n = slab_shape(turn)
                    if not first(turn):
                        act.wait_ge(s_bgm, turn)
                    for t in range(tiles):
                        act.wait_ge(s_xt, turn * TT + t + 1)
                        for k in range(KT // 2, KT):
                            at = grp * 2 * KT + k
                            last = nc.scalar.activation(hT[:, k, t * P:t * P + rows], p_x[:, k, 0:rows], ACT.Identity,
                                                        bias=g.modT[:, at + KT:at + KT + 1], scale=g.modT[:, at:at + 1])
                        last.then_inc(s_h2, TT // tiles)
                    for j in range(T_GROUPS):
                        act.wait_ge(s_mm, turn * GROUPS + j + 1)
                        bank = p_mm[j % BANKS]
                        if j < CT:
                            if j == 0:
                                act.wait_ge(s_carry, turn + 1)
                            nc.scalar.copy(raw[:, j, HIST:HIST + n], bank[:, 0:n]).then_inc(s_ev, 1)
                        else:
                            q = (j - CT) % 4
                            stores = 2 * turn + (j - CT) // 4
                            if not (first(turn) and j - CT < 4):
                                act.wait_ge(s_qo[q], stores * 16)
                            if j - CT < 4 and not first(turn):
                                act.wait_ge(s_kt, turn * KTILES)
                            nc.scalar.copy(qk[:, q, 0:n], bank[:, 0:n]).then_inc(s_ev, 1)
                            act.wait_ge(s_ev, turn * GROUPS + j + 1)
                            act.dma_start(g.qk_d[j - CT, :, tokens(turn, n)], qk[:, q, 0:n]).then_inc(s_qo[q], 16)
                        if 0 < j <= CT:
                            convolved(turn, n, j - 1)
                    prepare_next()
                    for t in range(TT):
                        for zi in range(2):
                            k = T_GROUPS + 2 * t + zi
                            done = s_vo if zi else s_zo
                            if t >= tiles:
                                continue
                            slot = 2 * (t % 2) + zi
                            act.wait_ge(s_mm, turn * GROUPS + k + 1)
                            if not grp:
                                act.wait_ge(done, (1 + (turn - 1) * TT + t) * 16)
                            nc.scalar.activation(zv[0:rows, slot, :], p_mm[k % BANKS][0:rows, :],
                                                 ACT.Copy if zi else ACT.Silu).then_inc(s_ev, last_of(tiles, zi))
                            if grp:
                                dst = g.outs["v_sample"] if zi else g.z_d[g.SEQ:g.TOK, :]
                            else:
                                dst = (g.outs["v_prompt"] if zi else g.z_d)[bass.ds((turn - 1) * SLAB + t * P, P), :]
                            act.wait_ge(s_ev, turn * GROUPS + T_GROUPS + 2 * t + zi + last_of(tiles, zi))
                            act.dma_start(dst, zv[0:rows, slot, :]).then_inc(done, 16)
                    act.wait_ge(s_kr, (turn + 1) * KTILES)
                    if grp:
                        act.dma_start(g.outs["k_sample"], krow[0:rows, 0, :]).then_inc(s_ko, 16)
                    else:
                        act.dma_start(g.outs["k_prompt"][bass.ds((turn - 1) * SLAB, SLAB), :].rearrange("(t p) n -> p t n", p=P),
                                      krow[:]).then_inc(s_ko, 16)

                slabs(body, prepare, act)
                act.wait_ge(s_tail, 2 + CT // 4)
                act.dma_start(g.outs["conv_prompt"], tail_rows[0:HIST, :]).then_inc(s_to, 16)
                act.dma_start(g.outs["conv_sample"], tail_rows[HIST:, :]).then_inc(s_to, 16)
                turns = SLABS + 1
                act.wait_ge(s_to, 32)
                act.wait_ge(s_ko, turns * 16)
                act.wait_ge(s_zo, (1 + g.TILES) * 16)
                act.wait_ge(s_vo, (1 + g.TILES) * 16)
                for s in s_co:
                    act.wait_ge(s, turns * (CT // 2) * 16)
                for s in s_qo:
                    act.wait_ge(s, turns * (QKT // 4) * 16)

            @block.tensor
            def _(pe):
                pe.wait_ge(s_small, 32)
                for c in range(CT):
                    last = nc.tensor.transpose(p_kt[0][:].rearrange("p t n -> p (t n)")[:, 8 * c:8 * c + HIST + CONV_W],
                                               small[:, c * P:(c + 1) * P], g.ident[0:HIST + CONV_W, 0:HIST + CONV_W])
                last.then_inc(s_trt, 1)

                def body(turn, _):
                    grp, rows, tiles, n = slab_shape(turn)
                    for t in range(tiles):
                        pe.wait_ge(s_xn, turn * TT + t + 1)
                        before = turn * TT + t
                        if not isinstance(before, int) or before > 0:
                            pe.wait_ge(s_h, before)
                            pe.wait_ge(s_h2, before)
                        for k in range(KT):
                            last = nc.tensor.transpose(p_x[:, k, 0:rows], x[0:rows, t, k * P:(k + 1) * P], g.ident[0:rows, 0:rows])
                        last.then_inc(s_xt, TT // tiles)
                    pe.wait_ge(s_h, (turn + 1) * TT)
                    pe.wait_ge(s_h2, (turn + 1) * TT)
                    if first(turn):
                        pe.wait_ge(s_w, 16 * KT)

                    def bank_free(k):
                        free = turn * GROUPS + k + 1 - BANKS
                        if not isinstance(free, int) or free > 0:
                            pe.wait_ge(s_ev, free)

                    for j in range(T_GROUPS):
                        col = j * P if j < CT else g.OFF_QB + (j - CT) * P
                        bank_free(j)
                        for k in range(KT):
                            mm = nc.tensor.matmul(p_mm[j % BANKS][:, 0:n], w[:, k, col:col + P], hT[:, k, 0:n],
                                                  start=(k == 0), stop=(k == KT - 1))
                        mm.then_inc(s_mm, 1)
                    for t in range(TT):
                        for zi in range(2):
                            k2 = T_GROUPS + 2 * t + zi
                            if t >= tiles:
                                continue
                            col = g.OFF_VB if zi else g.OFF_Z
                            bank_free(k2)
                            for k in range(KT):
                                mm = nc.tensor.matmul(p_mm[k2 % BANKS][0:rows, :], hT[:, k, t * P:t * P + rows],
                                                      w[:, k, col:col + g.ROWS], start=(k == 0), stop=(k == KT - 1))
                            mm.then_inc(s_mm, last_of(tiles, zi))
                        if t == 0:
                            keys_to_rows(turn, rows, tiles)
                    if not first(turn):
                        pe.wait_ge(s_bg, turn)
                    for t in range(tiles):
                        for k in range(KT):
                            mm = nc.tensor.matmul(p_bg[0:rows, 8 * t:8 * t + 8], hT[:, k, t * P:t * P + rows],
                                                  w[:, k, g.OFF_B:g.OFF_QB], start=(k == 0), stop=(k == KT - 1))
                    mm.then_inc(s_bgm, 1)

                def keys_to_rows(turn, rows, tiles):
                    for c in range(KTILES):
                        pe.wait_ge(s_ev, turn * GROUPS + CT + KTILES + c + 1)
                        free = turn * KTILES + c - 1
                        if c < 1 or c < 2:
                            if first(turn):
                                pe.wait_ge(s_wc, 2)
                        if not isinstance(free, int) or free > 0:
                            pe.wait_ge(s_kr, free)
                        for t in range(tiles):
                            tr = nc.tensor.transpose(p_kt[c % 2][0:rows, t, :], qk[:, c, t * P:t * P + rows], g.ident[:])
                        tr.then_inc(s_kt, 1)

                slabs(body, lambda turn: None, pe)
                pe.wait_ge(s_tail, 2)
                pe.wait_ge(s_ev, (SLABS + 1) * GROUPS)
                for c in range(CT):
                    last = nc.tensor.transpose(p_mm[c // 4][0:2 * HIST, (c % 4) * P:(c % 4 + 1) * P], tail[:, c, :], g.ident[:])
                last.then_inc(s_trt, 1)

            @block.vector
            def _(dve):
                link = Steps(s_link, dve, CHAIN)
                nc.vector.memset(eps[:], EPS).then_inc(s_wc, 1)
                dve.wait_ge(s_trt, 1)
                nc.vector.tensor_copy(cw[:], p_kt[0][:].rearrange("p t n -> p (t n)")[:, 0:8 * CT]
                                      .rearrange("p (c e) -> p c e", e=8)[:, :, 0:HIST + CONV_W]).then_inc(s_wc, 1)
                dve.wait_ge(s_wc, 2)
                nc.vector.tensor_copy(raw[:, :, 0:HIST], cw[:, :, 0:HIST]).then_inc(s_carry, 1)

                def prepare(turn):
                    grp, rows, tiles, n = slab_shape(turn)
                    link.begin(turn)
                    dve.wait_ge(s_std, turn + 1)
                    rec = nc.vector.reciprocal(rstd[0:rows, 0:tiles], std[0:rows, 0:tiles])
                    link.link(rec)
                    for t in range(tiles):
                        nc.vector.tensor_scalar(x[0:rows, t, :], x[0:rows, t, :], rstd[0:rows, t:t + 1], None,
                                                ALU.mult).then_inc(s_xn, TT // tiles)

                def body(turn, prepare_next):
                    grp, rows, tiles, n = slab_shape(turn)
                    link.begin(turn, 1)
                    if not first(turn):
                        dve.wait_ge(s_bgm, turn)
                    for t in range(tiles):
                        dve.wait_ge(s_xt, turn * TT + t + 1)
                        for k in range(KT // 2):
                            at = grp * 2 * KT + k
                            last = nc.vector.tensor_scalar(hT[:, k, t * P:t * P + rows], p_x[:, k, 0:rows],
                                                           g.modT[:, at:at + 1], g.modT[:, at + KT:at + KT + 1],
                                                           ALU.mult, ALU.add)
                        last.then_inc(s_h, TT // tiles)
                    for c in range(CT):
                        dve.wait_ge(s_ev, turn * GROUPS + c + 1)
                        used = turn * CT + c - 1
                        if not isinstance(used, int) or used > 0:
                            dve.wait_ge(s_silu, used)
                        a = acc[:, c % 2, 0:n]
                        link.link(nc.vector.tensor_scalar(a, raw[:, c, 0:n], cw[:, c, HIST:HIST + 1], None, ALU.mult))
                        for i in range(1, CONV_W):
                            step = nc.vector.scalar_tensor_tensor(out=a, in0=raw[:, c, i:i + n], scalar=cw[:, c, HIST + i:HIST + i + 1],
                                                                  in1=a, op0=ALU.mult, op1=ALU.add)
                            link.link(step)
                    if first(turn):
                        nc.vector.tensor_copy(tail[:, :, HIST:2 * HIST], raw[:, :, n:n + HIST]).then_inc(s_tail, 1)
                        nc.vector.memset(raw[:, :, 0:HIST], 0.0).then_inc(s_carry, 1)
                    else:
                        nc.vector.tensor_copy(raw[:, :, 0:HIST], raw[:, :, n:n + HIST]).then_inc(s_carry, 1)
                    link.end()
                    prepare_next()
                    for c in range(KTILES):
                        dve.wait_ge(s_kt, turn * KTILES + c + 1)
                        if c == 0 and not first(turn):
                            dve.wait_ge(s_ko, turn * 16)
                        nc.vector.tensor_copy(krow[0:rows, 0:tiles, c * P:(c + 1) * P], p_kt[c % 2][0:rows, 0:tiles, :]).then_inc(s_kr, 1)
                    dve.wait_ge(s_bgm, turn + 1)
                    tile0 = g.TILES if first(turn) else (turn - 1) * TT
                    nc.vector.tensor_copy(g.bg[0:rows, bass.ds(tile0, tiles), :],
                                          p_bg[0:rows, 0:8 * tiles].rearrange("p (t c) -> p t c", c=8)).then_inc(s_bg, 1)

                slabs(body, prepare, dve)
                dve.wait_ge(s_carry, SLABS + 2)
                nc.vector.tensor_copy(tail[:, :, 0:HIST], raw[:, :, 0:HIST]).then_inc(s_tail, 1)
                dve.wait_ge(s_trt, 2)
                for b in range(CT // 4):
                    nc.vector.tensor_copy(tail_rows[:, b * 512:(b + 1) * 512], p_mm[b][0:2 * HIST, :]).then_inc(s_tail, 1)


class Line:

    def __init__(self, sem, steps, base=0):
        self.sem, self.steps, self.at, self.base = sem, list(steps), 0, base

    def __call__(self, turn, step):
        return turn * len(self.steps) + self.steps.index(step) + 1 + self.base

    def next_stage(self, turns, steps):
        return Line(self.sem, steps, self.base + turns * len(self.steps))

    def did(self, step):
        assert self.steps[self.at % len(self.steps)] == step, (step, self.steps[self.at % len(self.steps)])
        self.at += 1
        return 1


def wide(ap, *shape):
    if len(ap.shape) == 3:
        return ap.to_broadcast(list(shape))
    axis = 2 if ap.shape[1] == shape[1] and ap.shape[1] != shape[2] else 1
    return ap.unsqueeze(axis).to_broadcast(list(shape))


def delta(nc, g):
    H, DD, NEW = DN_HEADS, DN_DIM, g.NEW
    LEVELS = 7
    s_in, s_z, s_par, s_s0 = g.sem("d_in"), g.sem("d_z"), g.sem("d_par"), g.sem("d_s0")
    s_out, s_sout, s_pre, s_exp = g.sem("d_out"), g.sem("d_sout"), g.sem("d_pre"), g.sem("d_exp")
    pe_a = Line(g.sem("steps_pe_a"), ["rows", "v_rows", "sums", "decay"])
    act_a = Line(g.sem("steps_act_a"), ["squares", "v", "e_rows", "e_next", "decay"])
    dve_a = Line(g.sem("steps_dve_a"), ["bg", "sum_sq", "q_sq", "k_sq", "kn", "qn"])
    pool_a = Line(g.sem("steps_pool_a"), ["g_mask", "r"])
    pe_b = Line(g.sem("steps_pe_b"), ["knT", "kbT", "qnT", "qdT", "kk", "kq", "L"]
                + [f"{a}{l}{h}" for l in range(1, LEVELS) for a in ("LT", "TLT") for h in range(2)])
    act_b = Line(g.sem("steps_act_b"), ["knT", "kbT", "qnT", "qdT"])
    dve_b = Line(g.sem("steps_dve_b"), ["LT", "AT", "B0", "T0"] + [f"{a}{l}{h}" for l in range(1, LEVELS) for a in ("m", "T") for h in range(2)])
    pool_b = Line(g.sem("steps_pool_b"), ["D", "kb", "qd", "vb", "kbe", "kd", "e_all", "B0T", "T0T"])
    pe_c = Line(g.sem("steps_pe_c"), ["u", "wT", "wS", "qS", "aV", "kV"])
    act_c = Line(g.sem("steps_act_c"), ["wT", "o_sq"])
    dve_c = Line(g.sem("steps_dve_c"), ["v_new", "o_sum", "state", "o_eps", "o_n", "o_g", "o_z"])
    pool_c = Line(g.sem("steps_pool_c"), ["S_dec", "o_r"])
    s_fresh = g.sem("d_fresh")
    g.lines = dict(pe_a=pe_a, pe_b=pe_b, act_a=act_a, act_b=act_b, act_c=act_c, dve_a=dve_a, dve_b=dve_b, dve_c=dve_c,
                   pool_a=pool_a, pool_c=pool_c)
    with ExitStack() as life:
        ct = g.sb("d_ct", [P, 3 * H, P], at=life)
        zt = g.sb("d_zt", [P, H, DD], at=life)
        par = g.sb("d_param", [P, 2, H], at=life)
        gain = g.sb("d_gain", [P, DD], at=life)
        sp_in = g.sb("d_sp", [P, g.T17, H], at=life)
        sp_abs = g.sb("d_spabs", [P, g.T17, H], at=life)
        bgt = g.sb("d_bg", [P, 2 * H], at=life)
        sq = g.sb("d_sq", [P, 2 * H, DD], at=life)
        ss = g.sb("d_ss", [P, 2 * H], at=life)
        ssn = g.sb("d_ssn", [P, 2 * H], at=life)
        r = g.sb("d_r", [P, 2 * H], at=life)
        e_rows = g.sb("d_er", [P, 2, H], at=life)
        e_next = g.sb("d_en", [P, H], at=life)
        e_all = g.sb("d_ea", [P, H], at=life)
        vr = g.sb("d_vr", [P, H, DD], at=life)
        gm = g.sb("d_gm", [P, H, P], at=life)
        dec = g.sb("d_dec", [P, H, P], at=life)
        dm = g.sb("d_dm", [P, H, P], at=life)
        kn, qn, vb, kb, qd, kbe, kd = (g.sb("d_" + n, [P, H, DD], at=life) for n in ("kn", "qn", "vb", "kb", "qd", "kbe", "kd"))
        knT, kbT, qnT, qdT, wT = (g.sb("d_" + n, [P, H, P], at=life) for n in ("knT", "kbT", "qnT", "qdT", "wT"))
        LT, AT, T, TT, B, BT = (g.sb("d_" + n, [P, H, P], at=life) for n in ("LT", "AT", "T", "TT", "B", "BT"))
        M = g.sb("d_m", [P, H, P], at=life)
        vn = g.sb("d_vn", [P, H, DD], at=life)
        S = g.sb("d_S", [P, H, DD], at=life)
        osq = g.sb("d_osq", [P, H, DD], at=life)
        oss = g.sb("d_oss", [P, H], at=life)
        osn = g.sb("d_osn", [P, H], at=life)
        orr = g.sb("d_orr", [P, H], at=life)
        o = g.sb("d_o", [P, H, DD], at=life)
        og = g.sb("d_og", [P, H, DD], at=life)
        oz = g.sb("d_oz", [P, H, DD], at=life)
        zero = g.sb("d_zero", [P, g.D], at=life)
        s_zero, s_zeros = g.sem("d_zero_set"), g.sem("d_zeros")
        FILL = -(-(g.BLOCKS - g.EXPERTS) // g.TILES)
        X = [g.psum(f"d_x{i}", [P, H, P], at=life) for i in range(4)]
        P1 = [g.psum(f"d_p1{i}", [P, H, P], at=life) for i in range(2)]
        P2 = [g.psum(f"d_p2{i}", [P, 2, 2, P], at=life) for i in range(2)]

        def turns(eng, start, body, end=lambda: None):
            start(0)
            body(0, True)
            body(1, True)
            with eng.Fori(2, g.TILES) as turn:
                body(turn, True)
            body(g.TILES, False)
            end()

        def done(eng, line, turn, step):
            if not isinstance(turn, int) or turn >= 0:
                eng.wait_ge(line.sem, line(turn, step))

        def shape(turn):
            first = isinstance(turn, int) and turn == 0
            n = NEW if first else P
            return not first, n, (g.TILES if first else turn - 1), (slice(g.SEQ, g.TOK) if first else bass.ds((turn - 1) * P, P))

        with nc.Block() as block:
            @block.sync
            def _(sp):
                for i, name in enumerate(["a_log", "dt_bias"]):
                    sp.dma_start(par[:, i, :], g.ins[name][0].partition_broadcast(P)).then_inc(s_par, 16)
                sp.dma_start(gain[:], g.ins["onorm_a"][0].partition_broadcast(P)).then_inc(s_par, 16)
                sp.dma_start(S[:], g.ins["state_delta"][0, 0].rearrange("h k v -> k h v")).then_inc(s_s0, 16)

                def load_ct(turn):
                    later, n, tile, at = shape(turn)
                    done(sp, pe_a, turn - 1, "v_rows")
                    sp.dma_start(ct[:, :, 0:n], g.conv_d[:, :, at].rearrange("c p t -> p c t")).then_inc(s_in, 16)

                def body(turn, follows):
                    later, n, tile, at = shape(turn)
                    if follows:
                        load_ct(turn + 1)
                    done(sp, dve_c, turn - 1, "o_z")
                    sp.dma_start(zt[0:n].rearrange("p h d -> p (h d)"), g.z_d[at, :]).then_inc(s_z, 16)
                    if later:
                        sp.dma_start(g.y_d[bass.ds((turn - 1) * FILL * P + g.EXPERTS * P, FILL * P), :].rearrange("(b p) d -> p b d", p=P),
                                     zero[:].unsqueeze(1).to_broadcast([P, FILL, g.D])).then_inc(s_zeros, 16)
                    else:
                        sp.wait_ge(s_zero, 1)
                        sp.dma_start(g.h2_d[g.TOK:g.TOK + 1, :], zero[0:1]).then_inc(s_zeros, 16)

                turns(sp, load_ct, body)
                sp.wait_ge(s_zeros, (1 + g.TILES) * 16)

            @block.scalar
            def _(act):
                act.wait_ge(s_pre, 1)
                nc.scalar.activation(sp_abs[:], sp_abs[:], ACT.Exp, scale=-1.0).then_inc(s_exp, 1)
                nc.scalar.activation(g.bg[:, :, 0:H], g.bg[:, :, 0:H], ACT.Exp, scale=-1.0).then_inc(s_exp, 1)
                act.wait_ge(s_par, 48)
                nc.scalar.activation(par[:, 0, :], par[:, 0, :], ACT.Exp).then_inc(s_exp, 1)
                act.wait_ge(s_exp, 3)
                nc.scalar.activation(sp_abs[:], sp_abs[:], ACT.Ln, bias=1.0).then_inc(s_exp, 1)

                def part_a(turn):
                    later, n, tile, at = shape(turn)
                    done(act, pe_a, turn, "rows")
                    done(act, dve_a, turn - 1, "sum_sq")
                    nc.scalar.activation(sq[0:n, 0:H], X[0][0:n], ACT.Square)
                    nc.scalar.activation(sq[0:n, H:2 * H], X[1][0:n], ACT.Square).then_inc(act_a.sem, act_a.did("squares"))
                    done(act, pe_a, turn, "v_rows")
                    done(act, pool_b, turn - 1, "vb")
                    nc.scalar.copy(vr[0:n], X[2][0:n]).then_inc(act_a.sem, act_a.did("v"))
                    done(act, pe_a, turn, "sums")
                    done(act, pool_b, turn - 1, "e_all")
                    sums = X[3][:].rearrange("p h d -> p (h d)")
                    nc.scalar.activation(e_rows[0:n].rearrange("p a h -> p (a h)"), sums[0:n, 0:2 * H], ACT.Exp).then_inc(act_a.sem, act_a.did("e_rows"))
                    nc.scalar.activation(e_next[:], sums[:, 2 * H:3 * H], ACT.Exp).then_inc(act_a.sem, act_a.did("e_next"))
                    done(act, pe_a, turn, "decay")
                    done(act, pool_b, turn - 1, "D")
                    nc.scalar.activation(dec[0:n, :, 0:n], X[3][0:n, :, 0:n], ACT.Exp).then_inc(act_a.sem, act_a.did("decay"))

                def part_b(turn):
                    later, n, tile, at = shape(turn)
                    for name, src, dst, reads, reader in (("knT", P1[0][:], knT, pe_b, "kq"), ("kbT", P1[1][:], kbT, pe_b, "kk"),
                                                          ("qnT", P2[0][:].rearrange("p a b n -> p (a b) n"), qnT, pe_b, "kq"),
                                                          ("qdT", P2[1][:].rearrange("p a b n -> p (a b) n"), qdT, pe_c, "qS")):
                        done(act, pe_b, turn, name)
                        done(act, reads, turn - 1, reader)
                        nc.scalar.copy(dst[:, :, 0:n], src[:, :, 0:n]).then_inc(act_b.sem, act_b.did(name))

                def store(turn):
                    later, n, tile, at = shape(turn)
                    done(act, dve_c, turn, "o_z")
                    act.dma_start(g.merged_d[at, 0:H * DD], oz[0:n].rearrange("p h d -> p (h d)")).then_inc(s_out, 16)

                def store_before(turn):
                    store(turn - 1)

                def body(turn, follows):
                    later, n, tile, at = shape(turn)
                    if follows:
                        part_a(turn + 1)
                    if later:
                        store_before(turn)
                    done(act, pe_c, turn, "wT")
                    done(act, pe_c, turn - 1, "wS")
                    nc.scalar.mul(wT[:, :, 0:n], X[1][:, :, 0:n], -1.0).then_inc(act_c.sem, act_c.did("wT"))
                    if follows:
                        part_b(turn + 1)
                    done(act, pe_c, turn, "aV")
                    done(act, dve_c, turn - 1, "o_sum")
                    nc.scalar.activation(osq[0:n], X[2][0:n], ACT.Square).then_inc(act_c.sem, act_c.did("o_sq"))
                    if not later or not follows:
                        done(act, dve_c, turn, "state")
                        act.dma_start(g.outs["delta_prompt" if later else "delta_sample"].rearrange("h k v -> k h v"), S[:]).then_inc(s_sout, 16)

                def start(turn):
                    part_a(turn)
                    part_b(turn)

                turns(act, start, body, lambda: store(g.TILES))
                act.wait_ge(s_sout, 32)
                act.wait_ge(s_out, g.T17 * 16)

            @block.tensor
            def _(pe):
                def a_rows(turn):
                    later, n, tile, at = shape(turn)
                    pe.wait_ge(s_in, (turn + 1) * 16)
                    done(pe, dve_b, turn - 1, "AT")
                    for j in range(2 * H):
                        tr = nc.tensor.transpose(X[j // H][0:n, j % H, :], ct[:, j, 0:n], g.ident[:])
                    tr.then_inc(pe_a.sem, pe_a.did("rows"))

                def a_sums(turn):
                    later, n, tile, at = shape(turn)
                    if not isinstance(turn, int) or turn > 1:
                        done(pe, dve_c, turn - 2, "o_n")
                        done(pe, act_c, turn - 2, "o_sq")
                    for j in range(2 * H, 3 * H):
                        tr = nc.tensor.transpose(X[j // H][0:n, j % H, :], ct[:, j, 0:n], g.ident[:])
                    tr.then_inc(pe_a.sem, pe_a.did("v_rows"))
                    done(pe, dve_a, turn, "bg")
                    if not isinstance(turn, int) or turn > 1:
                        done(pe, dve_c, turn - 2, "state")
                    sums = X[3][:].rearrange("p h d -> p (h d)")
                    gt = bgt[0:n, H:2 * H]
                    nc.tensor.matmul(sums[0:n, 0:H], g.upto[0:n, 0:n], gt, start=True, stop=True)
                    nc.tensor.matmul(sums[0:n, H:2 * H], g.behind[0:n, 0:n], gt, start=True, stop=True)
                    nc.tensor.matmul(sums[:, 2 * H:3 * H], g.ones[0:n, :], gt, start=True, stop=True).then_inc(pe_a.sem, pe_a.did("sums"))

                def a_decay(turn):
                    later, n, tile, at = shape(turn)
                    done(pe, pool_a, turn, "g_mask")
                    done(pe, act_a, turn, "e_next")
                    for h in range(H):
                        mm = nc.tensor.matmul(X[3][0:n, h, 0:n], gm[0:n, h, 0:n], g.upto[0:n, 0:n], start=True, stop=True)
                    mm.then_inc(pe_a.sem, pe_a.did("decay"))

                def turned(turn, name, out, rows):
                    later, n, tile, at = shape(turn)
                    for h in range(H):
                        tr = nc.tensor.transpose(out[:, h, 0:n], rows[0:n, h, :], g.ident[0:n, 0:n])
                    tr.then_inc(pe_b.sem, pe_b.did(name))

                def b_keys(turn):
                    done(pe, dve_a, turn, "kn")
                    turned(turn, "knT", P1[0], kn)
                    done(pe, pool_b, turn, "kb")
                    turned(turn, "kbT", P1[1], kb)

                def b_queries(turn):
                    done(pe, dve_a, turn, "qn")
                    turned(turn, "qnT", P2[0][:].rearrange("p a b n -> p (a b) n"), qn)
                    done(pe, pool_b, turn, "qd")
                    turned(turn, "qdT", P2[1][:].rearrange("p a b n -> p (a b) n"), qd)

                def b_products(turn):
                    later, n, tile, at = shape(turn)
                    done(pe, act_b, turn, "kbT")
                    if not later:
                        done(pe, dve_a, turn, "qn")
                    for h in range(H):
                        mm = nc.tensor.matmul(X[0][0:n, h, 0:n], knT[:, h, 0:n], kbT[:, h, 0:n], start=True, stop=True)
                    mm.then_inc(pe_b.sem, pe_b.did("kk"))
                    done(pe, act_b, turn, "qnT")
                    for h in range(H):
                        mm = nc.tensor.matmul(X[1][0:n, h, 0:n], knT[:, h, 0:n], qnT[:, h, 0:n], start=True, stop=True)
                    mm.then_inc(pe_b.sem, pe_b.did("kq"))
                    done(pe, dve_b, turn, "LT")
                    for h in range(H):
                        tr = nc.tensor.transpose(P2[0][0:n, h // 2, h % 2, 0:n], LT[0:n, h, 0:n], g.ident[0:n, 0:n])
                    tr.then_inc(pe_b.sem, pe_b.did("L"))

                def level(turn, l):
                    later, n, tile, at = shape(turn)
                    for half in range(2):
                        if l == 1:
                            done(pe, dve_b, turn, "T0")
                            done(pe, pool_b, turn, "T0T")
                        else:
                            done(pe, dve_b, turn, f"T{l - 1}{half}")
                        for h in (2 * half, 2 * half + 1):
                            mm = nc.tensor.matmul(P1[half][0:n, h, 0:n], LT[0:n, h, 0:n], T[0:n, h, 0:n], start=True, stop=True)
                        mm.then_inc(pe_b.sem, pe_b.did(f"LT{l}{half}"))
                    for half in range(2):
                        done(pe, dve_b, turn, f"m{l}{half}")
                        if l == 1 and half == 1:
                            done(pe, act_b, turn, "qdT")
                        for h in (2 * half, 2 * half + 1):
                            if l < LEVELS - 1:
                                nc.tensor.matmul(P2[half][0:n, 0, h % 2, 0:n], TT[0:n, h, 0:n], M[0:n, h, 0:n], start=True, stop=True)
                            mm = nc.tensor.matmul(P2[half][0:n, 1, h % 2, 0:n], M[0:n, h, 0:n], TT[0:n, h, 0:n], start=True, stop=True)
                        mm.then_inc(pe_b.sem, pe_b.did(f"TLT{l}{half}"))

                def body(turn, follows):
                    later, n, tile, at = shape(turn)
                    for l in range(1, LEVELS):
                        level(turn, l)
                        if follows and l in (2, 3, 4):
                            (a_rows, a_sums, a_decay)[l - 2](turn + 1)
                    done(pe, dve_b, turn, f"T{LEVELS - 1}1")
                    done(pe, pool_b, turn, "vb")
                    if follows:
                        done(pe, dve_a, turn + 1, "qn")
                    for h in range(H):
                        mm = nc.tensor.matmul(X[0][0:n, h, :], TT[0:n, h, 0:n], vb[0:n, h, :], start=(h == 0), stop=False, skip_group_check=True)
                    mm.then_inc(pe_c.sem, pe_c.did("u"))
                    done(pe, pool_b, turn, "kbe")
                    for h in range(H):
                        mm = nc.tensor.matmul(X[1][:, h, 0:n], kbe[0:n, h, :], TT[0:n, h, 0:n], start=True, stop=True)
                    mm.then_inc(pe_c.sem, pe_c.did("wT"))
                    if follows:
                        b_keys(turn + 1)
                    done(pe, act_c, turn, "wT")
                    if later:
                        pe.wait_ge(s_fresh, 1)
                        done(pe, dve_c, turn - 1, "state")
                    else:
                        pe.wait_ge(s_s0, 16)
                    for h in range(H):
                        mm = nc.tensor.matmul(X[0][0:n, h, :], wT[:, h, 0:n], S[:, h, :], start=False, stop=True, skip_group_check=True)
                    mm.then_inc(pe_c.sem, pe_c.did("wS"))
                    if follows:
                        done(pe, act_a, turn + 1, "v")
                    for h in range(H):
                        mm = nc.tensor.matmul(X[2][0:n, h, :], qdT[:, h, 0:n], S[:, h, :], start=(h == 0), stop=False, skip_group_check=True)
                    mm.then_inc(pe_c.sem, pe_c.did("qS"))
                    if follows:
                        b_queries(turn + 1)
                    done(pe, dve_c, turn, "v_new")
                    for h in range(H):
                        mm = nc.tensor.matmul(X[2][0:n, h, :], AT[0:n, h, 0:n], vn[0:n, h, :], start=False, stop=True, skip_group_check=True)
                    mm.then_inc(pe_c.sem, pe_c.did("aV"))
                    done(pe, pool_b, turn, "kd")
                    if follows:
                        done(pe, act_a, turn + 1, "decay")
                    for h in range(H):
                        mm = nc.tensor.matmul(X[3][:, h, :], kd[0:n, h, :], vn[0:n, h, :], start=True, stop=True)
                    mm.then_inc(pe_c.sem, pe_c.did("kV"))
                    if follows:
                        b_products(turn + 1)

                def start(turn):
                    a_rows(turn)
                    a_sums(turn)
                    a_decay(turn)
                    b_keys(turn)
                    b_queries(turn)
                    b_products(turn)

                turns(pe, start, body)

            @block.vector
            def _(dve):
                link = Steps(g.sem("d_link"), dve, 7)
                link.begin(0)
                nc.vector.memset(zero[:], 0.0).then_inc(s_zero, 1)
                dve.wait_ge(s_par, 48)
                link.link(nc.vector.tensor_copy(sp_in[:], g.bg[:, :, H:2 * H]))
                link.link(nc.vector.tensor_tensor(sp_in[:], sp_in[:], wide(par[:, 1, :], P, g.T17, H), ALU.add))
                nc.vector.scalar_tensor_tensor(out=sp_abs[:], in0=sp_in[:], scalar=-1.0, in1=sp_in[:], op0=ALU.mult,
                                               op1=ALU.max).then_inc(s_pre, 1)
                dve.wait_ge(s_exp, 4)
                link.link(nc.vector.scalar_tensor_tensor(out=sp_in[:], in0=sp_in[:], scalar=0.0, in1=sp_abs[:], op0=ALU.max, op1=ALU.add))
                link.link(nc.vector.tensor_tensor(sp_in[:], sp_in[:], wide(par[:, 0, :], P, g.T17, H), ALU.mult))
                link.link(nc.vector.tensor_scalar(g.bg[:, :, H:2 * H], sp_in[:], -1.0, None, ALU.mult))
                link.link(nc.vector.tensor_scalar(g.bg[:, :, 0:H], g.bg[:, :, 0:H], 1.0, None, ALU.add))
                link.link(nc.vector.reciprocal(g.bg[:, :, 0:H], g.bg[:, :, 0:H]))

                V = nc.vector

                def heads(a, n):
                    return wide(a, n, H, DD)

                def a_decays(turn):
                    later, n, tile, at = shape(turn)
                    done(dve, pe_a, turn - 1, "sums")
                    done(dve, pool_b, turn - 1, "vb")
                    V.tensor_copy(bgt[0:n], g.bg[0:n, bass.ds(tile, 1), :].rearrange("p a c -> p (a c)")).then_inc(dve_a.sem, dve_a.did("bg"))

                def a_norms(turn):
                    later, n, tile, at = shape(turn)
                    done(dve, act_a, turn, "squares")
                    V.tensor_reduce(ss[0:n], sq[0:n], AX, ALU.add).then_inc(dve_a.sem, dve_a.did("sum_sq"))
                    done(dve, dve_a, turn, "sum_sq")
                    done(dve, pool_a, turn - 1, "r")
                    V.tensor_scalar(ssn[0:n, 0:H], ss[0:n, 0:H], EPS, float(DD), ALU.add, ALU.mult).then_inc(dve_a.sem, dve_a.did("q_sq"))
                    V.tensor_scalar(ssn[0:n, H:2 * H], ss[0:n, H:2 * H], EPS, None, ALU.add).then_inc(dve_a.sem, dve_a.did("k_sq"))

                def a_rows(turn):
                    later, n, tile, at = shape(turn)
                    done(dve, pool_a, turn, "r")
                    done(dve, pool_b, turn - 1, "kd")
                    done(dve, pe_b, turn - 1, "qnT")
                    V.tensor_tensor(kn[0:n], X[1][0:n], heads(r[0:n, H:2 * H], n), ALU.mult).then_inc(dve_a.sem, dve_a.did("kn"))
                    V.tensor_tensor(qn[0:n], X[0][0:n], heads(r[0:n, 0:H], n), ALU.mult).then_inc(dve_a.sem, dve_a.did("qn"))

                def b_lower(turn):
                    later, n, tile, at = shape(turn)
                    done(dve, pe_b, turn, "kk")
                    done(dve, pool_b, turn, "D")
                    V.tensor_tensor(LT[0:n, :, 0:n], X[0][0:n, :, 0:n], dm[0:n, :, 0:n], ALU.mult).then_inc(dve_b.sem, dve_b.did("LT"))
                    done(dve, pe_b, turn, "kq")
                    V.tensor_tensor(AT[0:n, :, 0:n], X[1][0:n, :, 0:n], dm[0:n, :, 0:n], ALU.mult).then_inc(dve_b.sem, dve_b.did("AT"))
                    done(dve, pe_b, turn, "L")
                    L_rows = P2[0][:].rearrange("p a b n -> p (a b) n")
                    V.tensor_tensor(B[0:n, :, 0:n], L_rows[0:n, :, 0:n], g.level[0:n, 0:1, 0:n].to_broadcast([n, H, n]), ALU.mult).then_inc(dve_b.sem, dve_b.did("B0"))
                    done(dve, dve_b, turn, "B0")
                    V.tensor_tensor(T[0:n, :, 0:n], g.ident[0:n, 0:n].unsqueeze(1).to_broadcast([n, H, n]), B[0:n, :, 0:n], ALU.subtract).then_inc(dve_b.sem, dve_b.did("T0"))

                def level(turn, l):
                    later, n, tile, at = shape(turn)
                    for half in range(2):
                        hh = slice(2 * half, 2 * half + 2)
                        done(dve, pe_b, turn, f"LT{l}{half}")
                        if l == 1:
                            done(dve, pool_b, turn, "T0T")
                        V.tensor_tensor(M[0:n, hh, 0:n], P1[half][0:n, hh, 0:n], g.level[0:n, l:l + 1, 0:n].to_broadcast([n, 2, n]),
                                        ALU.mult).then_inc(dve_b.sem, dve_b.did(f"m{l}{half}"))
                    for half in range(2):
                        hh = slice(2 * half, 2 * half + 2)
                        done(dve, pe_b, turn, f"TLT{l}{half}")
                        if l < LEVELS - 1:
                            V.tensor_tensor(T[0:n, hh, 0:n], T[0:n, hh, 0:n], P2[half][0:n, 0, :, 0:n], ALU.subtract)
                        V.tensor_tensor(TT[0:n, hh, 0:n], TT[0:n, hh, 0:n], P2[half][0:n, 1, :, 0:n], ALU.subtract).then_inc(dve_b.sem, dve_b.did(f"T{l}{half}"))

                def c_state(turn):
                    later, n, tile, at = shape(turn)
                    done(dve, pe_c, turn, "wS")
                    V.tensor_copy(vn[0:n], X[0][0:n]).then_inc(dve_c.sem, dve_c.did("v_new"))
                    done(dve, act_c, turn, "o_sq")
                    V.tensor_reduce(oss[0:n], osq[0:n], AX, ALU.add).then_inc(dve_c.sem, dve_c.did("o_sum"))
                    done(dve, pe_c, turn, "kV")
                    done(dve, pool_c, turn, "S_dec")
                    V.tensor_tensor(S[:], S[:], X[3][:], ALU.add).then_inc(dve_c.sem, dve_c.did("state"))
                    done(dve, dve_c, turn, "o_sum")
                    V.tensor_scalar(osn[0:n], oss[0:n], 1.0 / DD, EPS, ALU.mult, ALU.add).then_inc(dve_c.sem, dve_c.did("o_eps"))

                def c_norm(turn):
                    later, n, tile, at = shape(turn)
                    done(dve, pool_c, turn, "o_r")
                    V.tensor_tensor(o[0:n], X[2][0:n], heads(orr[0:n], n), ALU.mult).then_inc(dve_c.sem, dve_c.did("o_n"))

                def c_gain(turn):
                    later, n, tile, at = shape(turn)
                    done(dve, dve_c, turn, "o_n")
                    V.tensor_tensor(og[0:n], o[0:n], gain[0:n].unsqueeze(1).to_broadcast([n, H, DD]), ALU.mult).then_inc(dve_c.sem, dve_c.did("o_g"))

                def c_gate(turn):
                    later, n, tile, at = shape(turn)
                    done(dve, dve_c, turn, "o_g")
                    dve.wait_ge(s_z, (turn + 1) * 16)
                    if later:
                        dve.wait_ge(s_out, turn * 16)
                    V.tensor_tensor(oz[0:n], og[0:n], zt[0:n], ALU.mult).then_inc(dve_c.sem, dve_c.did("o_z"))

                def body(turn, follows):
                    later, n, tile, at = shape(turn)
                    for l in range(1, LEVELS):
                        level(turn, l)
                        if later and l in (1, 2, 4):
                            {1: c_norm, 2: c_gain, 4: c_gate}[l](turn - 1)
                        if follows and l in (1, 3, 5):
                            {1: a_decays, 3: a_norms, 5: a_rows}[l](turn + 1)
                    c_state(turn)
                    if follows:
                        b_lower(turn + 1)
                    if not later:
                        dve.wait_ge(s_sout, 16)
                        V.memset(S[:], 0.0).then_inc(s_fresh, 1)

                def start(turn):
                    a_decays(turn)
                    a_norms(turn)
                    a_rows(turn)
                    b_lower(turn)

                def end():
                    c_norm(g.TILES)
                    c_gain(g.TILES)
                    c_gate(g.TILES)

                turns(dve, start, body, end)

            @block.gpsimd
            def _(pool):
                G = nc.gpsimd

                def did(line, name, turn, ins):
                    ins.then_inc(line.sem, line.did(name))
                    if isinstance(turn, int):
                        done(pool, line, turn, name)

                def heads(a, n):
                    return wide(a, n, H, DD)

                def part_a(turn):
                    later, n, tile, at = shape(turn)
                    done(pool, dve_a, turn, "bg")
                    done(pool, pe_a, turn - 1, "decay")
                    did(pool_a, "g_mask", turn, G.tensor_tensor(gm[0:n, :, 0:n], g.behind[0:n, 0:n].unsqueeze(1).to_broadcast([n, H, n]),
                                                                bgt[0:n, H:2 * H].unsqueeze(2).to_broadcast([n, H, n]), ALU.mult))
                    done(pool, dve_a, turn, "k_sq")
                    done(pool, dve_a, turn - 1, "qn")
                    did(pool_a, "r", turn, G.tensor_tensor(r[0:n], ssn[0:n], g.half[0:n, 0:2 * H], ALU.pow))

                def b_rows(turn):
                    later, n, tile, at = shape(turn)
                    done(pool, act_a, turn, "decay")
                    done(pool, dve_b, turn - 1, "AT")
                    did(pool_b, "D", turn, G.tensor_tensor(dm[0:n, :, 0:n], dec[0:n, :, 0:n], g.upto[0:n, 0:n].unsqueeze(1).to_broadcast([n, H, n]), ALU.mult))
                    done(pool, dve_a, turn, "kn")
                    done(pool, pe_b, turn - 1, "qdT")
                    did(pool_b, "kb", turn, G.tensor_tensor(kb[0:n], kn[0:n], heads(bgt[0:n, 0:H], n), ALU.mult))
                    done(pool, dve_a, turn, "qn")
                    did(pool_b, "qd", turn, G.tensor_tensor(qd[0:n], qn[0:n], heads(e_rows[0:n, 0, :], n), ALU.mult))

                def b_solved(turn):
                    later, n, tile, at = shape(turn)
                    done(pool, pe_c, turn - 1, "u")
                    did(pool_b, "vb", turn, G.tensor_tensor(vb[0:n], vr[0:n], heads(bgt[0:n, 0:H], n), ALU.mult))
                    done(pool, pe_c, turn - 1, "wT")
                    done(pool, pool_b, turn, "kb")
                    did(pool_b, "kbe", turn, G.tensor_tensor(kbe[0:n], kb[0:n], heads(e_rows[0:n, 0, :], n), ALU.mult))

                def b_state(turn):
                    later, n, tile, at = shape(turn)
                    done(pool, pe_c, turn - 1, "kV")
                    did(pool_b, "kd", turn, G.tensor_tensor(kd[0:n], kn[0:n], heads(e_rows[0:n, 1, :], n), ALU.mult))
                    done(pool, pool_c, turn - 1, "S_dec")
                    did(pool_b, "e_all", turn, G.tensor_tensor(e_all[:], e_next[:], g.ones[:, 0:H], ALU.mult))

                def b_start(turn):
                    later, n, tile, at = shape(turn)
                    done(pool, dve_b, turn, "LT")
                    did(pool_b, "B0T", turn, G.tensor_tensor(BT[0:n, :, 0:n], LT[0:n, :, 0:n], g.level[0:n, LEVELS:LEVELS + 1, 0:n].to_broadcast([n, H, n]), ALU.mult))
                    done(pool, pool_b, turn, "B0T")
                    did(pool_b, "T0T", turn, G.tensor_tensor(TT[0:n, :, 0:n], g.ident[0:n, 0:n].unsqueeze(1).to_broadcast([n, H, n]), BT[0:n, :, 0:n], ALU.subtract))

                def body(turn, follows):
                    later, n, tile, at = shape(turn)
                    if follows:
                        part_a(turn + 1)
                        b_rows(turn + 1)
                        b_solved(turn + 1)
                    done(pool, pe_c, turn, "qS")
                    did(pool_c, "S_dec", turn, G.tensor_tensor(S[:], S[:], e_all[:].unsqueeze(2).to_broadcast([P, H, DD]), ALU.mult))
                    if follows:
                        b_state(turn + 1)
                    done(pool, dve_c, turn, "o_eps")
                    did(pool_c, "o_r", turn, G.tensor_tensor(orr[0:n], osn[0:n], g.half[0:n, 0:H], ALU.pow))
                    if follows:
                        b_start(turn + 1)

                def start(turn):
                    part_a(turn)
                    b_rows(turn)
                    b_solved(turn)
                    b_state(turn)
                    b_start(turn)

                turns(pool, start, body)


def sticks(nc, g):
    H, DD, NEW = SB_HEADS, SB_DIM, g.NEW
    HS = H // 2
    PAIRS = g.QKT // 2
    NEW_BLOCK, PAST_BLOCK = g.TILES, g.TILES + 1
    BLOCKS = g.TILES + 2
    SCALE = float(DD) ** -0.5
    MASKED = -1e30
    s_kv, s_new, s_past, s_gain = g.sem("a_kv"), g.sem("a_new"), g.sem("a_past"), g.sem("a_gain")
    s_zero, s_mask, s_turned, s_ready = g.sem("a_zero"), g.sem("a_mask"), g.sem("a_turned"), g.sem("a_ready")
    s_q, s_qz = g.sem("a_q"), g.sem("a_qz")
    pair = lambda name: [g.sem(f"a_{name}{a}") for a in range(2)]
    s_z, s_zm, s_keep, s_beta, s_scan, s_carry, s_a, s_t, s_ev, s_v = (
        pair(n) for n in ("z", "zm", "keep", "beta", "scan", "carry", "a", "t", "ev", "v"))
    end_act = g.lines["act_c"].next_stage(g.T17, ["o_sq"])
    end_dve = g.lines["dve_c"].next_stage(g.T17, ["o_sum", "o_eps", "o_n", "o_g"])
    end_pool = g.lines["pool_c"].next_stage(g.T17, ["o_r"])
    s_out = g.sem("a_out")
    with ExitStack() as life:
        KT = g.sb("a_KT", [P, PAIRS, BLOCKS * P], at=life)
        V = g.sb("a_V", [P, BLOCKS, H * DD], at=life)
        past = g.sb("a_past", [P, H * DD], at=life)
        gain = g.sb("a_gainb", [P, DD], at=life)
        mask = g.sb("a_maskb", [P, P], at=life)
        q_in = g.sb("a_qin", [P, PAIRS, P], at=life)
        QZ = g.sb("a_QZ", [P, H, P], at=life)
        zm = [g.sb(f"a_zm{a}", [P, HS, P], at=life) for a in range(2)]
        keep = [g.sb(f"a_keep{a}", [P, HS, P + 1], at=life) for a in range(2)]
        beta = [g.sb(f"a_beta{a}", [P, HS, P], at=life) for a in range(2)]
        carry = [g.sb(f"a_carry{a}", [P, HS, P + 1], at=life) for a in range(2)]
        prod = [g.sb(f"a_prod{a}", [P, HS, P + 1], at=life) for a in range(2)]
        A = [g.sb(f"a_A{a}", [P, HS, P], at=life) for a in range(2)]
        AT = [g.sb(f"a_AT{a}", [P, HS, P], at=life) for a in range(2)]
        osq = g.sb("a_osq", [P, H, DD], at=life)
        oss, osn, orr = (g.sb("a_" + n, [P, H], at=life) for n in ("oss", "osn", "orr"))
        o = g.sb("a_o", [P, H, DD], at=life)
        og = g.sb("a_og", [P, H, DD], at=life)
        Z = [g.psum(f"a_z{a}", [P, HS, P], at=life) for a in range(2)]
        TR = [g.psum(f"a_tr{a}", [P, HS, P], at=life) for a in range(2)]
        acc = g.psum("a_acc", [P, H, DD], at=life)
        p_past = g.psum("a_pp", [P, PAIRS, P], at=life)

        def shape(turn):
            if isinstance(turn, int) and turn == 0:
                return NEW, slice(g.SEQ, g.TOK), 0, 1, lambda i: (NEW_BLOCK, PAST_BLOCK)[i]
            q = turn - 1
            return P, bass.ds(q * P, P), 2 + q * (q + 1) // 2, q, lambda i: q - i

        STEPS = 2 + g.TILES * (g.TILES + 1) // 2

        def first_of_all(turn):
            return isinstance(turn, int) and turn == 0

        def turns(eng, body):
            for turn in range(3):
                body(turn)
            with eng.Fori(3, g.TILES + 1) as turn:
                body(turn)

        def after(eng, sem, count):
            if not isinstance(count, int) or count > 0:
                eng.wait_ge(sem, count)

        def later_steps(eng, first, last, body):
            if isinstance(last, int):
                for i in range(first, last + 1):
                    body(i)
            else:
                with eng.Fori(first, last + 1) as i:
                    body(i)

        def flat(t, n):
            return t[0:n].rearrange("p h k -> p (h k)")[:, ::-1]

        with nc.Block() as block:
            @block.sync
            def _(sp):
                sp.dma_start(past[:], g.ins["cache_k"][0, 0].rearrange("t h d -> t (h d)")).then_inc(s_past, 16)
                sp.dma_start(gain[:], g.ins["onorm_b"][0].partition_broadcast(P)).then_inc(s_gain, 16)
                sp.wait_ge(s_zero, 2)
                sp.dma_start(KT[:, :, NEW_BLOCK * P:NEW_BLOCK * P + NEW], g.qk_d[PAIRS:, :, g.SEQ:g.TOK].rearrange("c p t -> p c t")).then_inc(s_new, 16)
                sp.dma_start(V[0:NEW, NEW_BLOCK, :], g.outs["v_sample"]).then_inc(s_new, 16)
                sp.dma_start(V[:, PAST_BLOCK, :], g.ins["cache_v"][0, 0].rearrange("t h d -> t (h d)")).then_inc(s_new, 16)

                def body(turn):
                    n, at, g0, last, block_of = shape(turn)
                    if not first_of_all(turn):
                        sp.wait_ge(s_qz, 2 * turn)
                    sp.dma_start(q_in[:, :, 0:n], g.qk_d[0:PAIRS, :, at].rearrange("c p t -> p c t")).then_inc(s_q, 16)
                    if isinstance(turn, int) and turn == 0:
                        sp.dma_start(KT[:, :, 0:g.SEQ], g.qk_d[PAIRS:, :, 0:g.SEQ].rearrange("c p t -> p c t")).then_inc(s_kv, 16)
                        sp.dma_start(V[:, 0:g.TILES, :], g.outs["v_prompt"].rearrange("(b p) n -> p b n", p=P)).then_inc(s_kv, 16)
                        return
                    store(turn - 1, NEW if isinstance(turn, int) and turn == 1 else P,
                          slice(g.SEQ, g.TOK) if isinstance(turn, int) and turn == 1 else bass.ds((turn - 2) * P, P))

                def store(turn, n, at):
                    sp.wait_ge(end_dve.sem, end_dve(turn, "o_g"))
                    sp.dma_start(g.merged_d[at, DN_HEADS * DN_DIM:], og[0:n].rearrange("p h d -> p (h d)")).then_inc(s_out, 16)

                turns(sp, body)
                D = g.D
                for a in range(2):
                    for tile, row in ((g.post[a], 2), (g.scale[a], 4), (g.shift[a], 3)):
                        sp.dma_start(tile[:], g.mod_d[a, row * D:(row + 1) * D].partition_broadcast(P)).then_inc(g.s_rows_mixed, 16)
                for i, name in enumerate(["g_post_mix", "g_pre_ffn"]):
                    sp.dma_start(g.gains[:, i, :], g.ins[name][0].partition_broadcast(P)).then_inc(g.s_rows_mixed, 16)
                GE = g.GROUPS_E
                for name, cols in (("group", slice(0, GE)), ("expert", slice(GE, None))):
                    sp.dma_start(g.b_router[:, cols], g.ins[f"b_router_{name}"][0].partition_broadcast(P)).then_inc(g.s_rows_mixed, 16)
                    sp.dma_start(g.w_router[:, :, cols], g.ins[f"w_router_{name}"][0].rearrange("(k p) n -> p k n", p=P)).then_inc(g.s_w_mixed, 16)
                sp.dma_start(g.w_out[:], g.ins["w_out"][0].rearrange("(k p) n -> p k n", p=P)).then_inc(g.s_w_mixed, 16)
                store(g.TILES, P, slice(g.SEQ - P, g.SEQ))
                sp.wait_ge(s_out, g.T17 * 16)

            @block.tensor
            def _(pe):
                pe.wait_ge(s_past, 16)
                for j in range(PAIRS):
                    tr = nc.tensor.transpose(p_past[:, j, :], past[:, j * P:(j + 1) * P], g.ident[:])
                tr.then_inc(s_turned, 1)
                pe.wait_ge(s_ready, 1)
                pe.wait_ge(s_new, 48)

                def body(turn):
                    n, at, g0, last, block_of = shape(turn)

                    def block(i):
                        b = block_of(i)
                        return b if isinstance(b, int) else nc.s_assert_within(
                            b, 0, g.TILES - 1, skip_runtime_bounds_check_because="the walk ends at block 0")

                    def score(i, a):
                        after(pe, s_beta[a], g0 + i)
                        for h in range(HS):
                            head = a * HS + h
                            mm = nc.tensor.matmul(Z[a][0:n, h, :], QZ[:, head, 0:n], KT[:, head // 2, bass.ds(block(i) * P, P)],
                                                  start=True, stop=True)
                        mm.then_inc(s_z[a], 1)

                    def turn_over(i, a):
                        pe.wait_ge(s_a[a], g0 + i + 1)
                        after(pe, s_ev[a], g0 + i)
                        for h in range(HS):
                            tr = nc.tensor.transpose(TR[a][:, h, 0:n], A[a][0:n, h, :], g.ident[0:n, 0:n])
                        tr.then_inc(s_t[a], 1)

                    def weigh(i, a, first=False):
                        pe.wait_ge(s_ev[a], g0 + i + 1)
                        if first and not first_of_all(turn):
                            pe.wait_ge(end_dve.sem, end_dve(turn - 1, "o_n"))
                            pe.wait_ge(end_act.sem, end_act(turn - 1, "o_sq"))
                        for h in range(HS):
                            head = a * HS + h
                            mm = nc.tensor.matmul(acc[0:n, head, :], AT[a][:, h, 0:n],
                                                  V[:, bass.ds(block(i), 1), head * DD:(head + 1) * DD].rearrange("p a n -> p (a n)"),
                                                  start=(first and h == 0), stop=True, skip_group_check=True)
                        mm.then_inc(s_v[a], 1)

                    pe.wait_ge(s_qz, 2 * (turn + 1))
                    if isinstance(turn, int) and turn == 1:
                        pe.wait_ge(s_kv, 32)
                    score(0, 0)
                    score(0, 1)
                    if isinstance(last, int) and last == 0:
                        turn_over(0, 0)
                        turn_over(0, 1)
                        weigh(0, 0, True)
                        weigh(0, 1)
                        return
                    score(1, 0)
                    turn_over(0, 0)
                    score(1, 1)
                    turn_over(0, 1)
                    weigh(0, 0, True)

                    def step(i):
                        score(i, 0)
                        turn_over(i - 1, 0)
                        weigh(i - 2, 1)
                        score(i, 1)
                        turn_over(i - 1, 1)
                        weigh(i - 1, 0)

                    later_steps(pe, 2, last, step)
                    turn_over(last, 0)
                    weigh(last - 1, 1)
                    turn_over(last, 1)
                    weigh(last, 0)
                    weigh(last, 1)

                turns(pe, body)

            @block.scalar
            def _(act):
                act.wait_ge(s_turned, 1)
                nc.scalar.copy(KT[:, :, PAST_BLOCK * P:(PAST_BLOCK + 1) * P], p_past[:]).then_inc(s_ready, 1)

                def body(turn):
                    n, at, g0, last, block_of = shape(turn)

                    def squash(i, a, diagonal=False):
                        G = g0 + i
                        if diagonal:
                            act.wait_ge(s_zm[a], turn + 1)
                        else:
                            act.wait_ge(s_z[a], G + 1)
                        src = zm[a] if diagonal else Z[a]
                        after(act, s_scan[a], G)
                        after(act, s_keep[a], G)
                        nc.scalar.activation(keep[a][0:n, :, 0:P], src[0:n], ACT.Sigmoid, scale=-SCALE).then_inc(s_keep[a], 1)
                        after(act, s_a[a], G)
                        after(act, s_beta[a], G)
                        nc.scalar.activation(beta[a][0:n], src[0:n], ACT.Sigmoid, scale=SCALE).then_inc(s_beta[a], 1)

                    def take(i):
                        act.wait_ge(s_t[0], g0 + i + 1)
                        after(act, s_v[0], g0 + i)
                        nc.scalar.copy(AT[0][:, :, 0:n], TR[0][:, :, 0:n]).then_inc(s_ev[0], 1)

                    squash(0, 0, True)
                    squash(0, 1, True)
                    if not first_of_all(turn):
                        finish(turn - 1, NEW if isinstance(turn, int) and turn == 1 else P, g0)

                    def step(i):
                        squash(i, 0)
                        take(i - 1)
                        squash(i, 1)

                    later_steps(act, 1, last, step)
                    take(last)

                def finish(turn, n, steps):
                    act.wait_ge(s_v[1], steps)
                    if not first_of_all(turn):
                        act.wait_ge(end_dve.sem, end_dve(turn - 1, "o_sum"))
                        act.wait_ge(end_act.sem, end_act(turn - 1, "o_sq"))
                    nc.scalar.activation(osq[0:n], acc[0:n], ACT.Square).then_inc(end_act.sem, end_act.did("o_sq"))

                turns(act, body)
                finish(g.TILES, P, STEPS)

            @block.vector
            def _(dve):
                link = Steps(g.sem("a_link"), dve, 1 + 6)
                link.begin(0)
                link.link(nc.vector.tensor_scalar(mask[:], g.upto[:], MASKED, None, ALU.mult))
                for a in range(2):
                    link.link(nc.vector.memset(keep[a][:, :, P:P + 1], 0.0))
                    link.link(nc.vector.memset(carry[a][:], 0.0))
                link.link(nc.vector.memset(osq[:], 0.0))
                link.link(nc.vector.memset(oss[:], 0.0))
                dve.wait_ge(s_gain, 16)

                def body(turn):
                    n, at, g0, last, block_of = shape(turn)

                    def walk(i, a):
                        G = g0 + i
                        dve.wait_ge(s_keep[a], G + 1)
                        after(dve, s_carry[a], G + turn + 1)
                        after(dve, s_a[a], G)
                        nc.vector.tensor_tensor_scan(flat(prod[a], n), flat(keep[a], n), flat(carry[a], n), 0.0,
                                                     ALU.mult, ALU.add).then_inc(s_scan[a], 1)
                        dve.wait_ge(s_scan[a], G + 1)
                        nc.vector.tensor_copy(carry[a][0:n, :, P:P + 1], prod[a][0:n, :, 0:1]).then_inc(s_carry[a], 1)

                    def take(i):
                        dve.wait_ge(s_t[1], g0 + i + 1)
                        after(dve, s_v[1], g0 + i)
                        nc.vector.tensor_copy(AT[1][:, :, 0:n], TR[1][:, :, 0:n]).then_inc(s_ev[1], 1)

                    for a in range(2):
                        after(dve, s_carry[a], g0 + turn)
                        nc.vector.memset(carry[a][:, :, P:P + 1], 1.0).then_inc(s_carry[a], 1)
                        dve.wait_ge(s_z[a], g0 + 1)
                        after(dve, s_beta[a], g0)
                        nc.vector.tensor_tensor(zm[a][0:n], Z[a][0:n], mask[0:n].unsqueeze(1).to_broadcast([n, HS, P]),
                                                ALU.add).then_inc(s_zm[a], 1)
                    walk(0, 0)
                    walk(0, 1)
                    if not first_of_all(turn):
                        finish(turn - 1, NEW if isinstance(turn, int) and turn == 1 else P)

                    def step(i):
                        walk(i, 0)
                        take(i - 1)
                        walk(i, 1)

                    later_steps(dve, 1, last, step)
                    take(last)

                def finish(turn, n):
                    V3 = nc.vector
                    dve.wait_ge(end_act.sem, end_act(turn, "o_sq"))
                    V3.tensor_reduce(oss[0:n], osq[0:n], AX, ALU.add).then_inc(end_dve.sem, end_dve.did("o_sum"))
                    dve.wait_ge(end_dve.sem, end_dve(turn, "o_sum"))
                    V3.tensor_scalar(osn[0:n], oss[0:n], 1.0 / DD, EPS, ALU.mult, ALU.add).then_inc(end_dve.sem, end_dve.did("o_eps"))
                    dve.wait_ge(end_pool.sem, end_pool(turn, "o_r"))
                    V3.tensor_tensor(o[0:n], acc[0:n], orr[0:n].unsqueeze(2).to_broadcast([n, H, DD]), ALU.mult).then_inc(end_dve.sem, end_dve.did("o_n"))
                    dve.wait_ge(end_dve.sem, end_dve(turn, "o_n"))
                    if not first_of_all(turn):
                        dve.wait_ge(s_out, turn * 16)
                    V3.tensor_tensor(og[0:n], o[0:n], gain[0:n].unsqueeze(1).to_broadcast([n, H, DD]), ALU.mult).then_inc(end_dve.sem, end_dve.did("o_g"))

                turns(dve, body)
                finish(g.TILES, P)

            @block.gpsimd
            def _(pool):
                G_ = nc.gpsimd
                G_.memset(KT[:, :, NEW_BLOCK * P:(NEW_BLOCK + 1) * P], 0.0).then_inc(s_zero, 1)
                G_.memset(V[:, NEW_BLOCK, :], 0.0).then_inc(s_zero, 1)
                G_.memset(QZ[:], 0.0).then_inc(s_mask, 1)
                pool.wait_ge(s_mask, 1)

                def body(turn):
                    n, at, g0, last, block_of = shape(turn)
                    pool.wait_ge(s_q, (turn + 1) * 16)
                    after(pool, s_z[1], g0)
                    spread = QZ[:].rearrange("p (c e) n -> p c e n", e=2)
                    after(pool, s_a[1], g0)
                    for e in range(2):
                        half = slice(e * DD, (e + 1) * DD)
                        G_.tensor_tensor(spread[half, :, e, 0:n], q_in[half, :, 0:n],
                                         g.ones[half, 0:n].unsqueeze(1).to_broadcast([DD, PAIRS, n]), ALU.mult).then_inc(s_qz, 1)
                        pool.wait_ge(s_qz, 2 * turn + e + 1)

                    def weights(i, a):
                        G = g0 + i
                        pool.wait_ge(s_scan[a], G + 1)
                        pool.wait_ge(s_beta[a], G + 1)
                        after(pool, s_t[a], G)
                        G_.tensor_tensor(A[a][0:n], prod[a][0:n, :, 1:P + 1], beta[a][0:n], ALU.mult).then_inc(s_a[a], 1)

                    def step(i):
                        weights(i, 0)
                        weights(i, 1)

                    step(0)
                    if not first_of_all(turn):
                        finish(turn - 1, NEW if isinstance(turn, int) and turn == 1 else P)
                    later_steps(pool, 1, last, step)

                def finish(turn, n):
                    pool.wait_ge(end_dve.sem, end_dve(turn, "o_eps"))
                    G_.tensor_tensor(orr[0:n], osn[0:n], g.half[0:n, 0:H], ALU.pow).then_inc(end_pool.sem, end_pool.did("o_r"))
                    if first_of_all(turn):
                        pool.wait_ge(end_pool.sem, end_pool(turn, "o_r"))

                turns(pool, body)
                finish(g.TILES, P)


def mixed(nc, g):
    D, KT, NEW, T17 = g.D, g.KT, g.NEW, g.T17
    R = g.EXPERTS + g.GROUPS_E
    s_w, s_rows = g.s_w_mixed, g.s_rows_mixed
    s_m, s_x, s_x2, s_h2, s_link = (g.sem("x_" + n) for n in ("m", "x", "x2", "h2", "link"))
    L = g.lines
    pe_a, pe_b = L["pe_a"].next_stage(T17, ["mT", "out"]), L["pe_b"].next_stage(T17, ["hT", "router"])
    act_a, act_b = L["act_a"].next_stage(T17, ["mT", "out"]), L["act_b"].next_stage(T17, ["sq", "sq2", "hT"])
    dve_b = L["dve_b"].next_stage(T17, ["s1", "post", "x2", "s2", "h1", "h2", "logits"])
    pool_b = L["pool_a"].next_stage(T17, ["r", "r2"])
    with ExitStack() as life:
        w, wr, br, post, scale, shift, gains = g.w_out, g.w_router, g.b_router, g.post, g.scale, g.shift, g.gains
        m = g.sb("x_m", [P, D], at=life)
        mT = g.sb("x_mT", [P, KT, P], at=life)
        osb = g.sb("x_o", [P, D], at=life)
        x = g.sb("x_x", [P, D], at=life)
        junk = g.sb("x_junk", [P, D], at=life)
        po = g.sb("x_po", [P, D], at=life)
        x2 = g.sb("x_x2", [P, D], at=life)
        hn = g.sb("x_hn", [P, D], at=life)
        h = g.sb("x_h", [P, D], at=life)
        hT = g.sb("x_hT", [P, KT, P], at=life)
        ss, sn, r = (g.sb("x_" + n, [P, 2], at=life) for n in ("ss", "sn", "r"))
        p_m = g.psum("x_pm", [P, KT, P], at=life)
        p_o = g.psum("x_po_", [P, D], at=life)
        p_h = g.psum("x_ph", [P, KT, P], at=life)
        p_r = g.psum("x_pr", [P, 512], at=life)

        def group_of(turn):
            return (1, NEW, slice(g.SEQ, g.TOK), g.TILES) if isinstance(turn, int) and turn == 0 else \
                (0, P, slice(g.SEQ - P, g.SEQ) if isinstance(turn, int) and turn == g.TILES else bass.ds((turn - 1) * P, P),
                 turn - 1)

        def turns(eng, start, finish):
            start(0)
            start(1)
            finish(0)
            with eng.Fori(2, g.TILES + 1) as turn:
                start(turn)
                finish(turn - 1)
            finish(g.TILES)

        def later(turn, n=0):
            return not isinstance(turn, int) or turn > n

        with nc.Block() as block:
            @block.sync
            def _(sp):
                def load(turn):
                    grp, n, at, tile = group_of(turn)
                    if later(turn):
                        sp.wait_ge(pe_a.sem, pe_a(turn - 1, "mT"))
                    sp.dma_start(m[0:n], g.merged_d[at, :]).then_inc(s_m, 16)
                    if later(turn):
                        sp.wait_ge(dve_b.sem, dve_b(turn - 1, "x2"))
                    sp.dma_start(x[0:n], g.x[1] if grp else g.x[0][at, :]).then_inc(s_x, 16)

                load(0)
                with sp.Fori(1, g.TILES + 1) as turn:
                    load(turn)

            @block.tensor
            def _(pe):
                def start(turn):
                    grp, n, at, tile = group_of(turn)
                    pe.wait_ge(s_m, (turn + 1) * 16)
                    if later(turn):
                        pe.wait_ge(act_a.sem, act_a(turn - 1, "mT"))
                    for k in range(KT):
                        tr = nc.tensor.transpose(p_m[:, k, 0:n], m[0:n, k * P:(k + 1) * P], g.ident[0:n, 0:n])
                    tr.then_inc(pe_a.sem, pe_a.did("mT"))
                    if not later(turn):
                        pe.wait_ge(s_w, 48)
                    pe.wait_ge(act_a.sem, act_a(turn, "mT"))
                    for c in range(D // 512):
                        for k in range(KT):
                            mm = nc.tensor.matmul(p_o[0:n, c * 512:(c + 1) * 512], mT[:, k, 0:n], w[:, k, c * 512:(c + 1) * 512],
                                                  start=(k == 0), stop=(k == KT - 1))
                    mm.then_inc(pe_a.sem, pe_a.did("out"))

                def finish(turn):
                    grp, n, at, tile = group_of(turn)
                    pe.wait_ge(dve_b.sem, dve_b(turn, "h2"))
                    if later(turn):
                        pe.wait_ge(act_b.sem, act_b(turn - 1, "hT"))
                    for k in range(KT):
                        tr = nc.tensor.transpose(p_h[:, k, 0:n], h[0:n, k * P:(k + 1) * P], g.ident[0:n, 0:n])
                    tr.then_inc(pe_b.sem, pe_b.did("hT"))
                    pe.wait_ge(act_b.sem, act_b(turn, "hT"))
                    if later(turn):
                        pe.wait_ge(dve_b.sem, dve_b(turn - 1, "logits"))
                    for k in range(KT):
                        mm = nc.tensor.matmul(p_r[0:n, 0:R], hT[:, k, 0:n], wr[:, k, :], start=(k == 0), stop=(k == KT - 1))
                    mm.then_inc(pe_b.sem, pe_b.did("router"))

                turns(pe, start, finish)

            @block.scalar
            def _(act):
                def start(turn):
                    grp, n, at, tile = group_of(turn)
                    act.wait_ge(pe_a.sem, pe_a(turn, "mT"))
                    if later(turn):
                        act.wait_ge(pe_a.sem, pe_a(turn - 1, "out"))
                        act.wait_ge(act_a.sem, act_a(turn - 1, "mT"))
                    nc.scalar.copy(mT[:, :, 0:n], p_m[:, :, 0:n]).then_inc(act_a.sem, act_a.did("mT"))
                    if later(turn):
                        chain(turn - 1)
                    act.wait_ge(pe_a.sem, pe_a(turn, "out"))
                    if later(turn):
                        act.wait_ge(dve_b.sem, dve_b(turn - 1, "post"))
                    nc.scalar.copy(osb[0:n], p_o[0:n]).then_inc(act_a.sem, act_a.did("out"))

                def chain(turn):
                    grp, n, at, tile = group_of(turn)
                    act.wait_ge(act_a.sem, act_a(turn, "out"))
                    if later(turn):
                        act.wait_ge(dve_b.sem, dve_b(turn - 1, "h1"))
                        act.wait_ge(act_b.sem, act_b(turn - 1, "sq2"))
                    nc.scalar.activation(junk[0:n], osb[0:n], ACT.Square, accum_out=ss[0:n, 0:1]).then_inc(act_b.sem, act_b.did("sq"))
                    act.wait_ge(dve_b.sem, dve_b(turn, "x2"))
                    act.wait_ge(act_b.sem, act_b(turn, "sq"))
                    nc.scalar.activation(junk[0:n], x2[0:n], ACT.Square, accum_out=ss[0:n, 1:2]).then_inc(act_b.sem, act_b.did("sq2"))
                    act.dma_start(g.x2_d[at, :], x2[0:n]).then_inc(s_x2, 16)

                def finish(turn):
                    grp, n, at, tile = group_of(turn)
                    act.wait_ge(pe_b.sem, pe_b(turn, "hT"))
                    if later(turn):
                        act.wait_ge(pe_b.sem, pe_b(turn - 1, "router"))
                        act.wait_ge(act_b.sem, act_b(turn - 1, "hT"))
                    nc.scalar.copy(hT[:, :, 0:n], p_h[:, :, 0:n]).then_inc(act_b.sem, act_b.did("hT"))
                    act.wait_ge(dve_b.sem, dve_b(turn, "h2"))
                    act.dma_start(g.h2_d[at, :], h[0:n]).then_inc(s_h2, 16)

                start(0)
                start(1)
                finish(0)
                with act.Fori(2, g.TILES + 1) as turn:
                    start(turn)
                    finish(turn - 1)
                chain(g.TILES)
                finish(g.TILES)
                act.wait_ge(s_x2, T17 * 16)
                act.wait_ge(s_h2, T17 * 16)

            @block.vector
            def _(dve):
                V = nc.vector
                link = Steps(s_link, dve, 5)
                link.begin(0)
                dve.wait_ge(s_rows, 160)
                for a in range(2):
                    link.link(V.tensor_tensor(post[a][:], post[a][:], gains[:, 0, :], ALU.mult))
                    link.link(V.scalar_tensor_tensor(out=scale[a][:], in0=scale[a][:], scalar=1.0, in1=gains[:, 1, :], op0=ALU.add, op1=ALU.mult))
                link.link(V.memset(g.logits[:], 0.0))

                def chain(turn):
                    grp, n, at, tile = group_of(turn)

                    def did(name):
                        return dve_b.sem, dve_b.did(name)

                    def after(name, t=turn):
                        dve.wait_ge(dve_b.sem, dve_b(t, name))

                    dve.wait_ge(act_b.sem, act_b(turn, "sq"))
                    if later(turn):
                        dve.wait_ge(pool_b.sem, pool_b(turn - 1, "r2"))
                    V.tensor_scalar(sn[0:n, 0:1], ss[0:n, 0:1], 1.0 / D, EPS, ALU.mult, ALU.add).then_inc(*did("s1"))
                    dve.wait_ge(pool_b.sem, pool_b(turn, "r"))
                    V.scalar_tensor_tensor(out=po[0:n], in0=osb[0:n], scalar=r[0:n, 0:1], in1=post[grp][0:n], op0=ALU.mult, op1=ALU.mult).then_inc(*did("post"))
                    after("post")
                    dve.wait_ge(s_x, (turn + 1) * 16)
                    if later(turn):
                        dve.wait_ge(s_x2, turn * 16)
                    V.tensor_tensor(x2[0:n], po[0:n], x[0:n], ALU.add).then_inc(*did("x2"))
                    dve.wait_ge(act_b.sem, act_b(turn, "sq2"))
                    V.tensor_scalar(sn[0:n, 1:2], ss[0:n, 1:2], 1.0 / D, EPS, ALU.mult, ALU.add).then_inc(*did("s2"))
                    dve.wait_ge(pool_b.sem, pool_b(turn, "r2"))
                    V.scalar_tensor_tensor(out=hn[0:n], in0=x2[0:n], scalar=r[0:n, 1:2], in1=scale[grp][0:n], op0=ALU.mult, op1=ALU.mult).then_inc(*did("h1"))
                    after("h1")
                    if later(turn):
                        dve.wait_ge(s_h2, turn * 16)
                        dve.wait_ge(pe_b.sem, pe_b(turn - 1, "hT"))
                    V.tensor_tensor(h[0:n], hn[0:n], shift[grp][0:n], ALU.add).then_inc(*did("h2"))
                    dve.wait_ge(pe_b.sem, pe_b(turn, "router"))
                    V.tensor_tensor(g.logits[0:n, bass.ds(tile, 1), :].rearrange("p a c -> p (a c)"), p_r[0:n, 0:R], br[0:n], ALU.add).then_inc(*did("logits"))

                chain(0)
                with dve.Fori(1, g.TILES + 1) as turn:
                    chain(turn)

            @block.gpsimd
            def _(pool):
                def body(turn):
                    grp, n, at, tile = group_of(turn)
                    pool.wait_ge(dve_b.sem, dve_b(turn, "s1"))
                    if later(turn):
                        pool.wait_ge(dve_b.sem, dve_b(turn - 1, "h1"))
                    nc.gpsimd.tensor_tensor(r[0:n, 0:1], sn[0:n, 0:1], g.half[0:n, 0:1], ALU.pow).then_inc(pool_b.sem, pool_b.did("r"))
                    pool.wait_ge(dve_b.sem, dve_b(turn, "s2"))
                    nc.gpsimd.tensor_tensor(r[0:n, 1:2], sn[0:n, 1:2], g.half[0:n, 0:1], ALU.pow).then_inc(pool_b.sem, pool_b.did("r2"))
                    if not later(turn):
                        pool.wait_ge(pool_b.sem, pool_b(turn, "r2"))

                body(0)
                with pool.Fori(1, g.TILES + 1) as turn:
                    body(turn)


def routing(nc, g):
    T17, E, GE, NEW = g.T17, g.EXPERTS, g.GROUPS_E, g.NEW
    PER = E // GE
    BIG = 1e30
    FAR = 1e6
    MOST = g.TOK // P + 1
    s_dve, s_act, s_pool, s_pe = (g.sem("r_" + n) for n in ("dve", "act", "pool", "pe"))
    s_fill, s_sc = g.sem("r_fill"), g.sem("r_sc")
    with ExitStack() as life:
        def t(name, shape, dt=F32):
            return g.sb("r_" + name, shape, dt, at=life)

        iota_g, iota_e, iota_b = t("ig", [P, GE]), t("ie", [P, E]), t("ib", [P, MOST])
        token = t("token", [P, T17], I32)
        fill = t("fill", [P, g.COLS], I32)
        valid = t("valid", [P, T17])
        gmax, gi, sg, pg = t("gmax", [P, T17]), t("gi", [P, T17]), t("sg", [P, T17]), t("pg", [P, T17])
        dg, eg, cg, ohg = (t(n, [P, T17, GE]) for n in ("dg", "eg", "cg", "ohg"))
        le, c1, c2, eq = (t(n, [P, T17, E]) for n in ("le", "c1", "c2", "eq"))
        oh = [t(f"oh{i}", [P, T17, E]) for i in range(2)]
        m1, m2, e1, e2, dm, em, den = (t(n, [P, T17]) for n in ("m1", "m2", "e1", "e2", "dm", "em", "den"))
        chosen = t("chosen", [P, T17, E])
        before = t("before", [P, T17 + 1, E])
        counts, blocks, ends, starts = (t(n, [P, E]) for n in ("counts", "blocks", "ends", "starts"))
        over = t("over", [P, E, MOST])
        place = t("place", [P, T17, E])
        sel = t("sel", [P, T17, E])
        destf = t("destf", [P, 2, T17])
        tab, tab2 = t("tab", [P, 2, T17], U32), t("tab2", [P, 2, T17], U32)
        p_rank = g.psum("r_rank", [P, 512], at=life)
        p_rank2 = g.psum("r_rank2", [P, 512], at=life)
        p_cnt = g.psum("r_cnt", [P, 512], at=life)

        def over_last(a, n):
            return a.unsqueeze(2).to_broadcast([P, a.shape[1], n])

        def over_tiles(a):
            return a.unsqueeze(1).to_broadcast([P, T17, a.shape[1]])

        mark = {}
        with nc.Block() as block:
            @block.sync
            def _(sp):
                load_expert(g, sp, 0, 0)
                load_expert(g, sp, 1, 1)

            @block.vector
            def _(dve):
                V = nc.vector
                link = Steps(s_dve, dve, 10 ** 6)
                link.begin(0)
                L = link.link
                dve.wait_ge(s_pool, 6)
                lg = g.logits[:, :, 0:GE]
                L(V.tensor_reduce(gmax[:], lg, AX, ALU.max))
                L(V.tensor_tensor(dg[:], lg, over_last(gmax[:], GE), ALU.subtract))
                mark['group'] = link.k
                L(V.tensor_scalar(cg[:], dg[:], 0.0, -FAR, ALU.is_equal, ALU.mult))
                L(V.tensor_tensor(cg[:], cg[:], over_tiles(iota_g[:]), ALU.add))
                L(V.tensor_reduce(gi[:], cg[:], AX, ALU.min))
                L(V.tensor_tensor(ohg[:], cg[:], over_last(gi[:], GE), ALU.is_equal))
                L(V.tensor_scalar(cg[:], ohg[:], -1.0, BIG, ALU.add, ALU.mult))
                L(V.tensor_tensor(le[:].rearrange("p t (g e) -> p t g e", g=GE), g.logits[:, :, GE:].rearrange("p t (g e) -> p t g e", g=GE),
                                  cg[:].unsqueeze(3).to_broadcast([P, T17, GE, PER]), ALU.add))
                for i, (top, idx) in enumerate(((m1, e1), (m2, e2))):
                    L(V.tensor_reduce(top[:], le[:], AX, ALU.max))
                    L(V.tensor_tensor(eq[:], le[:], over_last(top[:], E), ALU.is_equal))
                    L(V.tensor_scalar(c1[:], eq[:], -FAR, None, ALU.mult))
                    L(V.tensor_tensor(c1[:], c1[:], over_tiles(iota_e[:]), ALU.add))
                    L(V.tensor_reduce(idx[:], c1[:], AX, ALU.min))
                    L(V.tensor_tensor(oh[i][:], c1[:], over_last(idx[:], E), ALU.is_equal))
                    if i == 0:
                        L(V.scalar_tensor_tensor(out=le[:].rearrange("p t e -> p (t e)"), in0=oh[0][:].rearrange("p t e -> p (t e)"), scalar=-2 * BIG,
                                                 in1=le[:].rearrange("p t e -> p (t e)"), op0=ALU.mult, op1=ALU.add))
                L(V.tensor_tensor(dm[:], m2[:], m1[:], ALU.subtract))
                mark['pair'] = link.k
                L(V.tensor_tensor(chosen[:], oh[0][:], oh[1][:], ALU.add))
                L(V.tensor_tensor(chosen[:], chosen[:], over_last(valid[:], E), ALU.mult))
                L(V.memset(before[:, 0, :], 0.0))
                for tile in range(T17):
                    L(V.tensor_tensor(before[:, tile + 1, :], before[:, tile, :], chosen[:, tile, :], ALU.add))
                mark['chosen'] = link.k
                dve.wait_ge(s_act, 2)
                L(V.tensor_reduce(sg[:], eg[:], AX, ALU.add))
                L(V.reciprocal(pg[:], sg[:]))
                L(V.tensor_scalar(den[:], em[:], 1.0, None, ALU.add))
                L(V.reciprocal(den[:], den[:]))
                L(V.tensor_tensor(g.weight[:, 0, :], den[:], pg[:], ALU.mult))
                L(V.tensor_tensor(g.weight[:, 1, :], g.weight[:, 0, :], em[:], ALU.mult))
                dve.wait_ge(s_pe, 1)
                L(V.tensor_copy(counts[:], p_cnt[:, 0:E]))
                L(V.tensor_tensor(over[:], over_last(counts[:], MOST), iota_b[:].unsqueeze(1).to_broadcast([P, E, MOST]), ALU.is_gt))
                L(V.tensor_reduce(blocks[:], over[:], AX, ALU.add))
                L(V.tensor_scalar(blocks[:], blocks[:], 1.0, None, ALU.max))
                L(V.tensor_tensor_scan(ends[:], g.ones[:, 0:E], blocks[:], 0.0, ALU.mult, ALU.add))
                L(V.tensor_tensor(starts[:], ends[:], blocks[:], ALU.subtract))
                L(V.memset(g.bounds[:], 0.0))
                L(V.tensor_copy(g.bounds[:, 1:E + 1], ends[0:1, :]))
                L(V.tensor_scalar(starts[:], starts[:], float(P), -1.0, ALU.mult, ALU.add))
                L(V.tensor_tensor(place[:, 0:16, :], p_rank[:].rearrange("p (t e) -> p t e", e=E), starts[:].unsqueeze(1).to_broadcast([P, 16, E]), ALU.add))
                L(V.tensor_tensor(place[:, 16, :], p_rank2[:, 0:E], starts[:], ALU.add))
                for i in range(2):
                    L(V.tensor_tensor(sel[:], oh[i][:], place[:], ALU.mult))
                    L(V.tensor_reduce(destf[:, i, :], sel[:], AX, ALU.add))
                L(V.tensor_copy(g.dest[:], destf[:]))
                L(V.tensor_single_scalar(tab[:], g.dest[:], P - 1, ALU.bitwise_and))
                L(V.tensor_single_scalar(tab2[:], g.dest[:], 7, ALU.logical_shift_right))
                L(V.tensor_scalar(tab[:], tab[:], float(g.COLS), None, ALU.mult))
                L(V.tensor_tensor(g.slot[:], tab[:], tab2[:], ALU.add))
                mark['places'] = link.k

            @block.gpsimd
            def _(pool):
                G = nc.gpsimd
                G.iota(iota_g[:], pattern=[[1, GE]], base=0, channel_multiplier=0, allow_small_or_imprecise_dtypes=True).then_inc(s_pool, 1)
                G.iota(iota_e[:], pattern=[[1, E]], base=0, channel_multiplier=0, allow_small_or_imprecise_dtypes=True).then_inc(s_pool, 1)
                G.iota(iota_b[:], pattern=[[P, MOST]], base=0, channel_multiplier=0, allow_small_or_imprecise_dtypes=True).then_inc(s_pool, 1)
                G.iota(token[:], pattern=[[P, T17]], base=0, channel_multiplier=1).then_inc(s_pool, 1)
                G.iota(fill[:], pattern=[[0, g.COLS]], base=g.TOK, channel_multiplier=0).then_inc(s_pool, 1)
                G.affine_select(out=valid[:], in_=g.ones[:, 0:T17], compare_op=ALU.is_gt, fill=0.0, base=g.TOK,
                                pattern=[[-P, T17]], channel_multiplier=-1).then_inc(s_pool, 1)
                pool.wait_ge(s_pool, 6)
                pool.dma_start(g.token_d, fill[:]).then_inc(s_fill, 16)
                pool.wait_ge(s_fill, 16)
                pool.wait_ge(s_dve, mark['places'])
                table = g.token_d.rearrange("p (b o) -> (p b) o", o=1)
                for tile in range(T17):
                    n = NEW if tile == g.TILES else P
                    for i in range(2):
                        G.indirect_dma_start(out=table, out_offset=bass.IndirectOffsetOnAxis(ap=g.slot[0:n, i, tile:tile + 1], axis=0),
                                             in_=token[0:n, tile:tile + 1], in_offset=None).then_inc(s_sc, 16)
                pool.wait_ge(s_sc, 32 * T17)

            @block.scalar
            def _(act):
                act.wait_ge(s_dve, mark['group'])
                nc.scalar.activation(eg[:], dg[:], ACT.Exp).then_inc(s_act, 1)
                act.wait_ge(s_dve, mark['pair'])
                nc.scalar.activation(em[:], dm[:], ACT.Exp).then_inc(s_act, 1)

            @block.tensor
            def _(pe):
                pe.wait_ge(s_dve, mark['chosen'])
                for out, a, b in ((p_rank, 0, 16), (p_rank2, 16, T17)):
                    n = (b - a) * E
                    nc.tensor.matmul(out[:, 0:n], g.upto[:], chosen[:, a:b, :].rearrange("p t e -> p (t e)"), start=True, stop=False)
                    nc.tensor.matmul(out[:, 0:n], g.ones[:], before[:, a:b, :].rearrange("p t e -> p (t e)"), start=False, stop=True)
                nc.tensor.matmul(p_cnt[:, 0:E], g.ones[:], before[:, T17, :], start=True, stop=True).then_inc(s_pe, 1)


def load_expert(g, sp, e, buf):
    wg, wu, wd = g.expert_w
    s_wg, s_wd = g.s_expert
    for w, src in ((wg, "w_gate"), (wu, "w_up")):
        sp.dma_start(w[:, buf], g.ins[src][0, bass.ds(e, 1)].rearrange("a (k p) f -> p (a k) f", p=P)).then_inc(s_wg[buf], 16)
    sp.dma_start(wd[:, buf], g.ins["w_down"][0, bass.ds(e, 1)].rearrange("a (k p) d -> p (a k) d", p=P)).then_inc(s_wd[buf], 16)


def experts(nc, g):
    D, KT, E = g.D, g.KT, g.EXPERTS
    F = g.ins["w_gate"].shape[3]
    FT = F // P
    s_wg, s_wd = g.s_expert
    s_tab, s_stored = g.sem("e_tab"), g.sem("e_stored")
    s_idx, s_started, s_x, s_y = g.sem("e_idx"), g.sem("e_started"), g.sem("e_x"), g.sem("e_y")
    s_xt, s_gate, s_up, s_ht, s_down = [g.sem("e_xt0"), g.sem("e_xt1")], *(g.sem("e_" + n) for n in ("gate", "up", "ht", "down"))
    s_silu, s_h, s_hTs, s_xe0, s_xe1, s_ye0, s_ye1 = (g.sem("e_" + n) for n in ("silu", "h", "hTs", "xe0", "xe1", "ye0", "ye1"))
    HALF = KT // 2
    with ExitStack() as life:
        wg, wu, wd = g.expert_w
        table = g.sb("e_table", [P, g.COLS], I32, at=life)
        idx = g.sb("e_idx_", [P, 1], U32, at=life)
        x = g.sb("e_x_", [P, D], at=life)
        xT = g.sb("e_xT", [P, KT, P], at=life)
        sg = g.sb("e_sg", [P, F], at=life)
        h = g.sb("e_h_", [P, F], at=life)
        hT = g.sb("e_hT", [P, FT, P], at=life)
        y = g.sb("e_y_", [P, D], at=life)
        p_x = [g.psum(f"e_px{i}", [P, HALF, P], at=life) for i in range(2)]
        p_g = g.psum("e_pg", [P, F], at=life)
        p_u = g.psum("e_pu", [P, F], at=life)
        p_h = g.psum("e_ph", [P, FT, P], at=life)
        p_y = [g.psum(f"e_py{i}", [P, D // 2], at=life) for i in range(2)]

        def bound(eng, e):
            return eng.value_load(g.bounds[0:1, bass.ds(e, 1)], min_val=0, max_val=g.BLOCKS)

        def blocks_of(eng, e, body):
            first, last = bound(eng, e), bound(eng, e + 1)
            with eng.Fori(first, last) as b:
                body(b)

        with nc.Block() as block:
            @block.sync
            def _(sp):
                sp.dma_start(table[:], g.token_d).then_inc(s_tab, 16)

                with sp.Fori(1, E // 2) as pair:
                    for buf in range(2):
                        sp.wait_ge(s_down, bound(sp, pair * 2 + buf - 1))
                        load_expert(g, sp, pair * 2 + buf, buf)

            @block.gpsimd
            def _(pool):
                with pool.Fori(0, bound(pool, E) + 1) as b:
                    pool.wait_ge(s_idx, b + 1)
                    pool.sem_inc(s_started, 1)
                    nc.gpsimd.indirect_dma_start(out=x[:], out_offset=None, in_=g.h2_d,
                                                 in_offset=bass.IndirectOffsetOnAxis(ap=idx[:], axis=0)).then_inc(s_x, 16)

            @block.tensor
            def _(pe):
                def turn_rows(b, half):
                    if half == 0:
                        pe.wait_ge(s_x, b * 16 + 16)
                    for k in range(half * HALF, (half + 1) * HALF):
                        tr = nc.tensor.transpose(p_x[half][:, k % HALF, :], x[:, k * P:(k + 1) * P], g.ident[:])
                    tr.then_inc(s_xt[half], 1)

                turn_rows(0, 0)
                turn_rows(0, 1)

                def multiply(pair, buf, b):
                    pe.wait_ge(s_wg[buf], pair * 32 + 32)
                    pe.wait_ge(s_xe0, b + 1)
                    pe.wait_ge(s_xe1, b + 1)
                    for out, w, done in ((p_g, wg, s_gate), (p_u, wu, s_up)):
                        for k in range(KT):
                            mm = nc.tensor.matmul(out[:], xT[:, k, :], w[:, buf, k, :], start=(k == 0), stop=(k == KT - 1))
                        mm.then_inc(done, 1)
                    turn_rows(b + 1, 0)
                    pe.wait_ge(s_h, b + 1)
                    for f in range(FT):
                        tr = nc.tensor.transpose(p_h[:, f, :], h[:, f * P:(f + 1) * P], g.ident[:])
                    tr.then_inc(s_ht, 1)
                    turn_rows(b + 1, 1)
                    pe.wait_ge(s_wd[buf], pair * 16 + 16)
                    pe.wait_ge(s_hTs, b + 1)
                    for c in range(2):
                        for f in range(FT):
                            mm = nc.tensor.matmul(p_y[c][:], hT[:, f, :], wd[:, buf, f, c * (D // 2):(c + 1) * (D // 2)],
                                                  start=(f == 0), stop=(f == FT - 1))
                    mm.then_inc(s_down, 1)

                with pe.Fori(0, E // 2) as pair:
                    for buf in range(2):
                        blocks_of(pe, pair * 2 + buf, lambda b: multiply(pair, buf, b))

            @block.scalar
            def _(act):
                def take_x(b):
                    act.wait_ge(s_xt[0], b + 1)
                    nc.scalar.copy(xT[:, 0:HALF, :], p_x[0][:]).then_inc(s_xe0, 1)

                take_x(0)

                def body(b):
                    act.wait_ge(s_gate, b + 1)
                    nc.scalar.activation(sg[:], p_g[:], ACT.Silu).then_inc(s_silu, 1)
                    act.wait_ge(s_up, b + 1)
                    take_x(b + 1)
                    act.wait_ge(s_ht, b + 1)
                    nc.scalar.copy(hT[:], p_h[:]).then_inc(s_hTs, 1)
                    if not isinstance(b, int):
                        act.wait_ge(s_y, b * 16)
                    act.wait_ge(s_down, b + 1)
                    nc.scalar.copy(y[:, 0:D // 2], p_y[0][:]).then_inc(s_ye0, 1)
                    act.wait_ge(s_ye0, b + 1)
                    act.wait_ge(s_ye1, b + 1)
                    act.dma_start(g.y_d[bass.ds(b * P, P), :], y[:]).then_inc(s_y, 16)

                body(0)
                with act.Fori(1, bound(act, E)) as b:
                    body(b)
                act.wait_ge(s_y, bound(act, E) * 16)
                act.sem_inc(s_stored, 1)

            @block.vector
            def _(dve):
                def take_x(b):
                    dve.wait_ge(s_xt[1], b + 1)
                    nc.vector.tensor_copy(xT[:, HALF:, :], p_x[1][:]).then_inc(s_xe1, 1)

                def name_rows(b):
                    nc.vector.tensor_scalar(idx[:], table[:, bass.ds(b, 1)], 0.0, None, ALU.add).then_inc(s_idx, 1)

                dve.wait_ge(s_tab, 16)
                name_rows(0)
                take_x(0)
                dve.wait_ge(s_idx, 1)
                name_rows(1)

                def body(b):
                    dve.wait_ge(s_silu, b + 1)
                    dve.wait_ge(s_up, b + 1)
                    nc.vector.tensor_tensor(h[:], sg[:], p_u[:], ALU.mult).then_inc(s_h, 1)
                    take_x(b + 1)
                    dve.wait_ge(s_idx, b + 2)
                    name_rows(b + 2)
                    if not isinstance(b, int):
                        dve.wait_ge(s_y, b * 16)
                    dve.wait_ge(s_down, b + 1)
                    nc.vector.tensor_copy(y[:, D // 2:], p_y[1][:]).then_inc(s_ye1, 1)

                body(0)
                with dve.Fori(1, bound(dve, E)) as b:
                    body(b)


def combine(nc, g):
    D, NEW = g.D, g.NEW
    GT = 5
    s_rows, s_idx, s_started, s_y0, s_y1, s_x2, s_out, s_link = (g.sem("o_" + n) for n in
                                                               ("rows", "idx", "started", "y0", "y1", "x2", "out", "link"))
    by_dve = g.lines["dve_a"].next_stage(g.T17, ["w0", "w1", "mean", "gated", "out"])
    s_sq, s_r = g.sem("o_sq"), g.sem("o_r")
    with ExitStack() as life:
        post = [g.sb(f"o_post{a}", [P, D], at=life) for a in range(2)]
        gain = g.sb("o_gain", [P, D], at=life)
        idx = [g.sb(f"o_idx{i}", [P, 1], U32, at=life) for i in range(2)]
        rows = [g.sb(f"o_row{i}", [P, D], at=life) for i in range(2)]
        t0, t1, junk, gated, x2, out = (g.sb("o_" + n, [P, D], at=life) for n in ("t0", "t1", "junk", "gated", "x2_", "out_"))
        ss, sn, r = (g.sb("o_" + n, [P, 1], at=life) for n in ("ss", "sn", "rr"))

        def shape(turn):
            first = isinstance(turn, int)
            return not first, (NEW if first else P), (g.TILES if first else turn - 1),                 (slice(g.SEQ, g.TOK) if first else bass.ds((turn - 1) * P, P))

        def turns(eng, body):
            body(0)
            with eng.Fori(1, g.TILES + 1) as turn:
                body(turn)

        with nc.Block() as block:
            @block.sync
            def _(sp):
                for a in range(2):
                    sp.dma_start(post[a][:], g.mod_d[a, GT * D:(GT + 1) * D].partition_broadcast(P)).then_inc(s_rows, 16)
                sp.dma_start(gain[:], g.ins["g_post_ffn"][0].partition_broadcast(P)).then_inc(s_rows, 16)

                def body(turn):
                    later, n, tile, at = shape(turn)
                    if later:
                        sp.wait_ge(by_dve.sem, by_dve(turn - 1, "out"))
                    sp.dma_start(x2[0:n], g.x2_d[at, :]).then_inc(s_x2, 16)

                turns(sp, body)

            @block.gpsimd
            def _(pool):
                def body(turn):
                    later, n, tile, at = shape(turn)
                    pool.wait_ge(s_idx, 2 * turn + 2)
                    pool.sem_inc(s_started, 1)
                    for i, done in enumerate((s_y0, s_y1)):
                        nc.gpsimd.indirect_dma_start(out=rows[i][0:n], out_offset=None, in_=g.y_d,
                                                     in_offset=bass.IndirectOffsetOnAxis(ap=idx[i][0:n], axis=0)).then_inc(done, 16)
                    pool.wait_ge(by_dve.sem, by_dve(turn, "mean"))
                    nc.gpsimd.tensor_tensor(r[0:n], sn[0:n], g.half[0:n, 0:1], ALU.pow).then_inc(s_r, 1)
                    if not later:
                        pool.wait_ge(s_r, 1)

                turns(pool, body)

            @block.scalar
            def _(act):
                def body(turn):
                    later, n, tile, at = shape(turn)
                    act.wait_ge(by_dve.sem, by_dve(turn, "w1"))
                    if later:
                        act.wait_ge(s_sq, turn)
                    nc.scalar.activation(junk[0:n], t1[0:n], ACT.Square, accum_out=ss[0:n]).then_inc(s_sq, 1)
                    act.wait_ge(by_dve.sem, by_dve(turn, "out"))
                    act.dma_start(g.outs["y_prompt"][at, :] if later else g.outs["y_sample"], out[0:n]).then_inc(s_out, 16)

                turns(act, body)
                act.wait_ge(s_out, g.T17 * 16)

            @block.vector
            def _(dve):
                V = nc.vector
                link = Steps(s_link, dve, 2)
                link.begin(0)
                dve.wait_ge(s_rows, 48)
                for a in range(2):
                    link.link(V.tensor_tensor(post[a][:], post[a][:], gain[:], ALU.mult))

                def name_rows(turn):
                    tile = g.TILES if isinstance(turn, int) and turn == 0 else (turn - 1)
                    for i in range(2):
                        V.tensor_scalar(idx[i][:], g.dest[:, i, bass.ds(tile, 1)], 0.0, None, ALU.add).then_inc(s_idx, 1)

                def body(turn):
                    later, n, tile, at = shape(turn)
                    grp = 0 if later else 1

                    def did(name):
                        return by_dve.sem, by_dve.did(name)

                    dve.wait_ge(s_y0, (turn + 1) * 16)
                    V.tensor_scalar(t0[0:n], rows[0][0:n], g.weight[0:n, 0, bass.ds(tile, 1)], None, ALU.mult).then_inc(*did("w0"))
                    dve.wait_ge(s_y1, (turn + 1) * 16)
                    dve.wait_ge(by_dve.sem, by_dve(turn, "w0"))
                    V.scalar_tensor_tensor(out=t1[0:n], in0=rows[1][0:n], scalar=g.weight[0:n, 1, bass.ds(tile, 1)], in1=t0[0:n],
                                           op0=ALU.mult, op1=ALU.add).then_inc(*did("w1"))
                    dve.wait_ge(by_dve.sem, by_dve(turn, "w1"))
                    dve.wait_ge(s_idx, 2 * turn + 2)
                    name_rows(turn + 1)
                    dve.wait_ge(s_sq, turn + 1)
                    V.tensor_scalar(sn[0:n], ss[0:n], 1.0 / D, EPS, ALU.mult, ALU.add).then_inc(*did("mean"))
                    dve.wait_ge(s_r, turn + 1)
                    V.scalar_tensor_tensor(out=gated[0:n], in0=t1[0:n], scalar=r[0:n, 0:1], in1=post[grp][0:n],
                                           op0=ALU.mult, op1=ALU.mult).then_inc(*did("gated"))
                    dve.wait_ge(by_dve.sem, by_dve(turn, "gated"))
                    dve.wait_ge(s_x2, (turn + 1) * 16)
                    if later:
                        dve.wait_ge(s_out, turn * 16)
                    V.tensor_tensor(out[0:n], gated[0:n], x2[0:n], ALU.add).then_inc(*did("out"))

                name_rows(0)
                turns(dve, body)


_OUTS = [("y_prompt", (1, 2048, 1024)), ("y_sample", (1, 32, 1024)),
         ("k_prompt", (1, 1, 2048, 8, 64)), ("v_prompt", (1, 1, 2048, 8, 64)),
         ("delta_prompt", (1, 1, 4, 128, 128)), ("conv_prompt", (1, 1, 3, 1536)),
         ("k_sample", (1, 1, 32, 8, 64)), ("v_sample", (1, 1, 32, 8, 64)),
         ("delta_sample", (1, 1, 4, 128, 128)), ("conv_sample", (1, 1, 3, 1536))]


def _flat(name, ap):
    if name[0] == "y":
        return ap.rearrange("a t d -> (a t) d")
    if name[0] in "kv":
        return ap.rearrange("l b t h d -> (l b t) (h d)")
    if name[0] == "d":
        return ap.rearrange("l b h k v -> (l b h) k v")
    return ap.rearrange("l b t c -> (l b t) c")


def kernel(**inputs):
    import numpy as _np
    import concourse.bacc as _bacc
    from concourse import mybir as _mybir
    from concourse.bass_utils import run_bass_kernel_spmd as _run

    nc = _bacc.Bacc("TRN2", target_bir_lowering=False, num_devices=1)
    arrays, ins, outs = {}, {}, {}
    for name, value in inputs.items():
        a = _np.ascontiguousarray(value)
        arrays[f"in_{name}"] = a
        ins[name] = nc.dram_tensor(f"in_{name}", a.shape, _mybir.dt.from_np(a.dtype), kind="ExternalInput").ap()
    for name, shape in _OUTS:
        outs[name] = _flat(name, nc.dram_tensor(f"out_{name}", shape, _mybir.dt.float32, kind="ExternalOutput").ap())
    build(nc, ins, outs)
    r = _run(nc, [arrays], core_ids=[0])
    return tuple(r.results[0][f"out_{name}"] for name, _ in _OUTS)
```

```python
from contextlib import ExitStack

import concourse.bass as bass
from concourse import mybir

ALU = mybir.AluOpType
ACT = mybir.ActivationFunctionType
F32 = mybir.dt.float32
I32 = mybir.dt.int32
U32 = mybir.dt.uint32
AX = mybir.AxisListType.X

P = 128
EPS = 1e-6
CONV_W = 4
DN_HEADS = 4
DN_DIM = 128
SB_HEADS = 8
SB_DIM = 64


class Steps:

    def __init__(self, sem, eng, per):
        self.sem, self.eng, self.per, self.k, self.base = sem, eng, per, 0, 0

    def begin(self, turn, done=0):
        self.base, self.k = turn * self.per, done

    def link(self, ins):
        self.k += 1
        assert self.k <= self.per, (self.sem, self.per)
        ins.then_inc(self.sem, 1)
        self.eng.wait_ge(self.sem, self.base + self.k)

    def end(self):
        assert self.k == self.per, (self.sem, self.k, self.per)


class Plan:
    pass


def build(nc, ins, outs):
    g = Plan()
    g.x = [ins["x_prompt"][0], ins["x_sample"][0]]
    g.SEQ, g.D = g.x[0].shape
    g.NEW = g.x[1].shape[0]
    g.KT = g.D // P
    g.TILES = g.SEQ // P
    g.CONV_CH = ins["conv_w"].shape[2]
    g.CT = g.CONV_CH // P
    g.IN_COLS = ins["w_in"].shape[2]
    g.ROWS = SB_HEADS * SB_DIM
    g.QKT = 2 * g.ROWS // P
    g.OFF_Z = g.CONV_CH
    g.OFF_B = g.OFF_Z + DN_HEADS * DN_DIM
    g.OFF_QB = g.OFF_B + 2 * DN_HEADS
    g.OFF_VB = g.OFF_QB + 2 * g.ROWS
    g.TOK = g.SEQ + g.NEW
    g.T17 = g.TILES + 1
    g.ins, g.outs, g.nc = ins, outs, nc
    with ExitStack() as life:
        g.sb = lambda name, shape, dt=F32, at=life: at.enter_context(nc.sbuf_tensor(name, shape, dt))
        g.psum = lambda name, shape, dt=F32, at=life: at.enter_context(nc.psum_tensor(name, shape, dt))
        g.sem = lambda name: life.enter_context(nc.semaphore(name))
        g.mod_d = nc.dram_tensor("mod_d", [2, 6 * g.D], F32, kind="Internal").ap()
        g.conv_d = nc.dram_tensor("conv_d", [g.CT, P, g.TOK], F32, kind="Internal").ap()
        g.qk_d = nc.dram_tensor("qk_d", [g.QKT, P, g.TOK], F32, kind="Internal").ap()
        g.z_d = nc.dram_tensor("z_d", [g.TOK, g.ROWS], F32, kind="Internal").ap()
        g.merged_d = nc.dram_tensor("merged_d", [g.TOK, DN_HEADS * DN_DIM + g.ROWS], F32, kind="Internal").ap()
        g.ident = g.sb("ident", [P, P])
        g.bg = g.sb("bg", [P, g.T17, 2 * DN_HEADS])
        g.modT = g.sb("modT", [P, 4 * g.KT])
        constants(nc, g)
        with ExitStack() as until_projected:
            g.w_in = g.sb("w_in", [P, g.KT, g.IN_COLS], at=until_projected)
            g.s_w_in = g.sem("p_w")
            modulation(nc, g)
            projection(nc, g)
        g.ones = g.sb("ones", [P, P])
        g.half = g.sb("minus_half", [P, 2 * DN_HEADS])
        g.upto = g.sb("upto", [P, P])
        g.behind = g.sb("behind", [P, P])
        g.level = g.sb("level", [P, 8, P])
        g.GROUPS_E = g.ins["w_router_group"].shape[2]
        g.EXPERTS = g.ins["w_router_expert"].shape[2]
        g.BLOCKS = 2 * g.TOK // P + g.EXPERTS
        g.COLS = g.BLOCKS + 2
        g.x2_d = nc.dram_tensor("x2_d", [g.TOK, g.D], F32, kind="Internal").ap()
        g.h2_d = nc.dram_tensor("h2_d", [g.TOK + 1, g.D], F32, kind="Internal").ap()
        g.Y_BLOCKS = g.EXPERTS + -(-(g.BLOCKS - g.EXPERTS) // g.TILES) * g.TILES
        g.y_d = nc.dram_tensor("y_d", [g.Y_BLOCKS * P, g.D], F32, kind="Internal").ap()
        g.token_d = nc.dram_tensor("token_d", [P, g.COLS], I32, kind="Internal").ap()
        g.logits = g.sb("logits", [P, g.T17, g.GROUPS_E + g.EXPERTS])
        g.weight = g.sb("weight", [P, 2, g.T17])
        g.dest = g.sb("dest", [P, 2, g.T17], U32)
        g.slot = g.sb("slot", [P, 2, g.T17], U32)
        g.bounds = g.sb("bounds", [1, g.EXPERTS + 1], I32)
        masks(nc, g)
        with ExitStack() as until_mixed:
            g.keysT = g.sb("keysT", [P, g.QKT // 2, (g.TILES + 2) * P], at=until_mixed)
            g.values = g.sb("values", [P, g.TILES + 2, g.ROWS], at=until_mixed)
            g.s_kv = g.sem("a_kv")
            delta(nc, g)
            R = g.EXPERTS + g.GROUPS_E
            g.w_out = g.sb("w_out", [P, g.KT, g.D], at=until_mixed)
            g.w_router = g.sb("w_router", [P, g.KT, R], at=until_mixed)
            g.b_router = g.sb("b_router", [P, R], at=until_mixed)
            g.post, g.scale, g.shift = ([g.sb(f"x_{n}{a}", [P, g.D], at=until_mixed) for a in range(2)] for n in ("post", "scale", "shift"))
            g.gains = g.sb("x_gains", [P, 2, g.D], at=until_mixed)
            g.s_w_mixed, g.s_rows_mixed = g.sem("x_w"), g.sem("x_rows")
            sticks(nc, g)
            mixed(nc, g)
        with ExitStack() as until_combine:
            F = ins["w_gate"].shape[3]
            g.expert_w = [g.sb("e_wg", [P, 2, g.KT, F], at=until_combine), g.sb("e_wu", [P, 2, g.KT, F], at=until_combine),
                          g.sb("e_wd", [P, 2, F // P, g.D], at=until_combine)]
            g.s_expert = [g.sem("e_wg0"), g.sem("e_wg1")], [g.sem("e_wd0"), g.sem("e_wd1")]
            routing(nc, g)
            experts(nc, g)
        combine(nc, g)


def constants(nc, g):
    s_cleared, s_ident = g.sem("s_cleared"), g.sem("s_ident")
    with nc.Block() as block:
        @block.gpsimd
        def _(pool):
            nc.gpsimd.memset(g.ident[:], 0.0).then_inc(s_cleared, 1)
            pool.wait_ge(s_cleared, 1)
            nc.gpsimd.affine_select(out=g.ident[:], in_=g.ident[:], compare_op=ALU.not_equal, fill=1.0,
                                    base=0, pattern=[[-1, P]], channel_multiplier=1).then_inc(s_ident, 1)
            nc.gpsimd.memset(g.bg[:], 0.0).then_inc(s_ident, 1)
            pool.wait_ge(s_ident, 2)


def masks(nc, g):
    s_set, s_tri = g.sem("k_set"), g.sem("k_tri")
    LEVELS = 7
    with nc.sbuf_tensor("row_no", [P, P], I32) as row_no, nc.sbuf_tensor("col_no", [P, P], I32) as col_no, \
            nc.sbuf_tensor("xor", [P, P], I32) as xor, nc.sbuf_tensor("xor_f", [P, P], F32) as xor_f, \
            nc.sbuf_tensor("below", [P, 2, P], F32) as below, nc.Block() as block:
        @block.vector
        def _(dve):
            link = Steps(g.sem("k_link"), dve, 2 + 3 * (LEVELS + 1))
            link.begin(0)
            dve.wait_ge(s_tri, 6)
            link.link(nc.vector.tensor_tensor(xor[:], row_no[:], col_no[:], ALU.bitwise_xor))
            link.link(nc.vector.tensor_copy(xor_f[:], xor[:]))
            for l in range(LEVELS + 1):
                low = 2 ** (l % LEVELS)
                link.link(nc.vector.tensor_scalar(g.level[:, l, :], xor_f[:], float(low), None, ALU.is_ge))
                link.link(nc.vector.scalar_tensor_tensor(out=g.level[:, l, :], in0=xor_f[:], scalar=float(2 * low), in1=g.level[:, l, :],
                                                         op0=ALU.is_lt, op1=ALU.mult))
                link.link(nc.vector.tensor_tensor(g.level[:, l, :], g.level[:, l, :], below[:, l // LEVELS, :], ALU.mult))

        @block.gpsimd
        def _(pool):
            nc.gpsimd.memset(g.half[:], -0.5).then_inc(s_set, 1)
            nc.gpsimd.memset(g.ones[:], 1.0).then_inc(s_set, 1)
            pool.wait_ge(s_set, 2)
            for out, sign, least in ((g.upto[:], -1, 0), (g.behind[:], 1, 1), (below[:, 0, :], 1, 1), (below[:, 1, :], -1, 1)):
                nc.gpsimd.affine_select(out=out, in_=g.ones[:], compare_op=ALU.is_ge, fill=0.0, base=-least,
                                        pattern=[[-sign, P]], channel_multiplier=sign).then_inc(s_tri, 1)
            nc.gpsimd.iota(row_no[:], pattern=[[0, P]], base=0, channel_multiplier=1).then_inc(s_tri, 1)
            nc.gpsimd.iota(col_no[:], pattern=[[1, P]], base=0, channel_multiplier=0).then_inc(s_tri, 1)


def modulation(nc, g):
    KT, D = g.KT, g.D
    WIDE = 512
    CHUNKS = 6 * D // WIDE
    w_ada = g.ins["w_ada"][0].rearrange("(k p) n -> p k n", p=P)
    s_c, s_w = g.sem("m_c"), [g.sem("m_w0"), g.sem("m_w1")]
    s_gain = g.sem("m_gain")
    s_silu, s_cT, s_cTs = g.sem("m_silu"), g.sem("m_cT"), g.sem("m_cTs")
    s_mm, s_add, s_row = g.sem("m_mm"), g.sem("m_add"), g.sem("m_row")
    s_tr, s_col = g.sem("m_tr"), g.sem("m_col")
    with ExitStack() as life:
        c_rows = g.sb("c_rows", [2, D], at=life)
        c_silu = g.sb("c_silu", [2, D], at=life)
        cT = g.sb("cT", [P, KT, 2], at=life)
        w = [g.sb(f"w_ada{b}", [P, KT, WIDE], at=life) for b in range(2)]
        rows = bias = g.sb("mod_rows", [2, 6 * D], at=life)
        gain_rows = g.sb("gain_rows", [KT, P], at=life)
        gain = g.sb("gain_cols", [P, KT], at=life)
        cols = g.sb("mod_cols", [P, 2 * KT, 2], at=life)
        p_c = g.psum("m_pc", [P, 512], at=life)
        p_mod = [g.psum(f"m_pm{b}", [2, WIDE], at=life) for b in range(2)]
        p_col = g.psum("m_pcol", [P, 512], at=life)
        with nc.Block() as block:
            @block.sync
            def _(sp):
                sp.dma_start(c_rows[0:1, :], g.ins["c_prompt"]).then_inc(s_c, 16)
                sp.dma_start(c_rows[1:2, :], g.ins["c_sample"]).then_inc(s_c, 16)
                for r in range(2):
                    sp.dma_start(bias[r:r + 1, :], g.ins["b_ada"]).then_inc(s_c, 16)
                sp.dma_start(gain_rows[:], g.ins["g_pre_mix"][0].rearrange("(k p) -> k p", p=P)).then_inc(s_gain, 16)
                for b in range(2):
                    sp.dma_start(w[b][:], w_ada[:, :, b * WIDE:(b + 1) * WIDE]).then_inc(s_w[b], 16)
                with sp.Fori(1, CHUNKS // 2) as i:
                    for b in range(2):
                        sp.wait_ge(s_mm, 2 * i - 1 + b)
                        sp.dma_start(w[b][:], w_ada[:, :, bass.ds(i * (2 * WIDE) + b * WIDE, WIDE)]).then_inc(s_w[b], 16)

            @block.scalar
            def _(act):
                act.wait_ge(s_c, 64)
                nc.scalar.activation(c_silu[:], c_rows[:], ACT.Silu).then_inc(s_silu, 1)
                w_in = g.ins["w_in"][0].rearrange("(k p) n -> p k n", p=P)
                for k in range(KT):
                    act.wait_ge(s_mm, k + 1)
                    act.dma_start(g.w_in[:, k, :], w_in[:, k, :]).then_inc(g.s_w_in, 16)
                act.wait_ge(s_add, CHUNKS)
                act.dma_start(g.mod_d, rows[:]).then_inc(s_row, 16)
                act.wait_ge(s_row, 16)

            @block.tensor
            def _(pe):
                pe.wait_ge(s_silu, 1)
                for k in range(KT):
                    last = nc.tensor.transpose(p_c[:, 2 * k:2 * k + 2], c_silu[:, k * P:(k + 1) * P], g.ident[0:2, 0:2])
                last.then_inc(s_cT, 1)
                pe.wait_ge(s_cTs, 1)

                def chunk(b):
                    for k in range(KT):
                        mm = nc.tensor.matmul(p_mod[b][:], cT[:, k, :], w[b][:, k, :], start=(k == 0), stop=(k == KT - 1))
                    mm.then_inc(s_mm, 1)

                for b in range(2):
                    pe.wait_ge(s_w[b], 16)
                    chunk(b)
                with pe.Fori(1, CHUNKS // 2) as i:
                    for b in range(2):
                        pe.wait_ge(s_w[b], 16 * i + 16)
                        pe.wait_ge(s_add, 2 * i - 1 + b)
                        chunk(b)
                pe.wait_ge(s_add, CHUNKS)
                for j in range(2 * KT):
                    nc.tensor.transpose(p_col[:, 2 * j:2 * j + 2], rows[:, j * P:(j + 1) * P], g.ident[0:2, 0:2])
                pe.wait_ge(s_gain, 16)
                nc.tensor.transpose(p_col[:, 4 * KT:5 * KT], gain_rows[:], g.ident[0:KT, 0:KT]).then_inc(s_tr, 1)

            @block.vector
            def _(dve):
                dve.wait_ge(s_cT, 1)
                nc.vector.tensor_copy(cT[:].rearrange("p k c -> p (k c)"), p_c[:, 0:2 * KT]).then_inc(s_cTs, 1)
                dve.wait_ge(s_c, 64)

                def add(b, at):
                    nc.vector.tensor_tensor(rows[:, at], p_mod[b][:], bias[:, at], ALU.add).then_inc(s_add, 1)

                with dve.Fori(0, CHUNKS // 2) as i:
                    for b in range(2):
                        dve.wait_ge(s_mm, 2 * i + 1 + b)
                        add(b, bass.ds(i * (2 * WIDE) + b * WIDE, WIDE))
                dve.wait_ge(s_tr, 1)
                nc.vector.tensor_copy(cols[:].rearrange("p k c -> p (k c)"), p_col[:, 0:4 * KT]).then_inc(s_col, 1)
                nc.vector.tensor_copy(gain[:], p_col[:, 4 * KT:5 * KT]).then_inc(s_col, 1)
                dve.wait_ge(s_col, 2)
                for grp in range(2):
                    at = grp * 2 * KT
                    nc.vector.scalar_tensor_tensor(out=g.modT[:, at:at + KT], in0=cols[:, KT:2 * KT, grp], scalar=1.0,
                                                   in1=gain[:], op0=ALU.add, op1=ALU.mult).then_inc(s_col, 1)
                    nc.vector.tensor_copy(g.modT[:, at + KT:at + 2 * KT], cols[:, 0:KT, grp]).then_inc(s_col, 1)
                dve.wait_ge(s_col, 6)


def projection(nc, g):
    KT, D, CT, QKT, NEW = g.KT, g.D, g.CT, g.QKT, g.NEW
    SLAB = 512
    TT = SLAB // P
    SLABS = g.SEQ // SLAB
    HIST = CONV_W - 1
    T_GROUPS = CT + QKT
    R_GROUPS = 2 * TT
    GROUPS = T_GROUPS + R_GROUPS
    BANKS = 3
    KTILES = QKT // 2
    s_w, s_small = g.s_w_in, g.sem("p_small")
    s_x, s_sq, s_std, s_xn = [g.sem(f"p_x{t}") for t in range(TT)], g.sem("p_sq"), g.sem("p_std"), g.sem("p_xn")
    s_xt, s_h, s_h2, s_mm, s_ev = g.sem("p_xt"), g.sem("p_h"), g.sem("p_h2"), g.sem("p_mm"), g.sem("p_ev")
    s_bgm, s_bg, s_link, s_silu = g.sem("p_bgm"), g.sem("p_bg"), g.sem("p_link"), g.sem("p_silu")
    s_kt, s_kr, s_carry, s_tail = g.sem("p_kt"), g.sem("p_kr"), g.sem("p_carry"), g.sem("p_tail")
    CHAIN = 1 + CONV_W * CT
    s_co, s_qo = [g.sem("p_co0"), g.sem("p_co1")], [g.sem(f"p_qo{b}") for b in range(4)]
    s_zo, s_vo, s_ko, s_to, s_trt, s_wc = g.sem("p_zo"), g.sem("p_vo"), g.sem("p_ko"), g.sem("p_to"), g.sem("p_trt"), g.sem("p_wc")
    with ExitStack() as life:
        w = g.w_in
        x = g.sb("x_in", [P, TT, D], at=life)
        hT = g.sb("hT", [P, KT, SLAB], at=life)
        junk = g.sb("junk", [P, D], at=life)
        sq = g.sb("sq", [P, TT], at=life)
        std = g.sb("std", [P, TT], at=life)
        rstd = g.sb("rstd", [P, TT], at=life)
        raw = g.sb("raw", [P, CT, HIST + SLAB], at=life)
        acc = g.sb("conv_acc", [P, 2, SLAB], at=life)
        conv = g.sb("conv_out", [P, 2, SLAB], at=life)
        qk = g.sb("qk_out", [P, 4, SLAB], at=life)
        zv = g.sb("zv_out", [P, 4, g.ROWS], at=life)
        krow = g.sb("k_rows", [P, TT, g.ROWS], at=life)
        small = krow[0:HIST + CONV_W].rearrange("p t n -> p (t n)")[:, 0:g.CONV_CH]
        cw = g.sb("conv_cols", [P, CT, HIST + CONV_W], at=life)
        tail = g.sb("tail", [P, CT, 2 * HIST], at=life)
        tail_rows = x[0:2 * HIST].rearrange("p t n -> p (t n)")[:, 0:g.CONV_CH]
        eps = g.sb("eps_p", [P, 1], at=life)
        p_x = g.psum("p_px", [P, KT, P], at=life)
        p_mm = [g.psum(f"p_pm{b}", [P, 512], at=life) for b in range(BANKS)]
        p_bg = g.psum("p_pbg", [P, 512], at=life)
        p_kt = [g.psum(f"p_pk{b}", [P, TT, P], at=life) for b in range(2)]

        def first(turn):
            return isinstance(turn, int) and turn == 0

        def slab_shape(turn):
            return (1, NEW, 1, NEW) if first(turn) else (0, P, TT, SLAB)

        def tokens(turn, n):
            return bass.ds(g.SEQ, n) if first(turn) else bass.ds((turn - 1) * SLAB, n)

        def last_of(tiles, zi):
            return 1 + 2 * (TT - tiles) * zi

        def slabs(body, prepare, eng):
            prepare(0)
            body(0, lambda: prepare(1))
            with eng.Fori(1, SLABS) as turn:
                body(turn, lambda: prepare(turn + 1))
            body(SLABS, lambda: None)

        with nc.Block() as block:
            @block.sync
            def _(sp):
                sp.dma_start(small[0:HIST, :], g.ins["state_conv"][0, 0]).then_inc(s_small, 16)
                sp.dma_start(small[HIST:, :], g.ins["conv_w"][0]).then_inc(s_small, 16)

                def load_x(turn):
                    grp, rows, tiles, _ = slab_shape(turn)
                    for t in range(TT):
                        if not first(turn):
                            sp.wait_ge(s_xt, turn * TT)
                        if t < tiles:
                            src = g.x[1] if grp else g.x[0][bass.ds((turn - 1) * SLAB + t * P, P), :]
                            sp.dma_start(x[0:rows, t, :], src).then_inc(s_x[t], 16)

                load_x(0)
                with sp.Fori(1, SLABS + 1) as turn:
                    load_x(turn)

            @block.scalar
            def _(act):
                def prepare(turn):
                    grp, rows, tiles, n = slab_shape(turn)
                    for t in range(tiles):
                        act.wait_ge(s_x[t], (turn + (t == 0)) * 16)
                        if t or not grp:
                            act.wait_ge(s_sq, turn * TT + t)
                        nc.scalar.activation(junk[0:rows, :], x[0:rows, t, :], ACT.Square,
                                             accum_out=sq[0:rows, t:t + 1]).then_inc(s_sq, TT // tiles)
                    if first(turn):
                        act.wait_ge(s_wc, 2)
                    act.wait_ge(s_sq, (turn + 1) * TT)
                    if not first(turn):
                        act.wait_ge(s_link, (turn - 1) * CHAIN + 1)
                    nc.scalar.activation(std[0:rows, 0:tiles], sq[0:rows, 0:tiles], ACT.Sqrt, bias=eps[0:rows, :],
                                         scale=1.0 / D).then_inc(s_std, 1)

                def convolved(turn, n, c):
                    act.wait_ge(s_link, turn * CHAIN + 1 + CONV_W * (c + 1))
                    stored = turn * (CT // 2) + c // 2
                    if not isinstance(stored, int) or stored > 0:
                        act.wait_ge(s_co[c % 2], stored * 16)
                    nc.scalar.activation(conv[:, c % 2, 0:n], acc[:, c % 2, 0:n], ACT.Silu).then_inc(s_silu, 1)
                    act.wait_ge(s_silu, turn * CT + c + 1)
                    act.dma_start(g.conv_d[c, :, tokens(turn, n)], conv[:, c % 2, 0:n]).then_inc(s_co[c % 2], 16)

                def body(turn, prepare_next):
                    grp, rows, tiles, n = slab_shape(turn)
                    if not first(turn):
                        act.wait_ge(s_bgm, turn)
                    for t in range(tiles):
                        act.wait_ge(s_xt, turn * TT + t + 1)
                        for k in range(KT // 2, KT):
                            at = grp * 2 * KT + k
                            last = nc.scalar.activation(hT[:, k, t * P:t * P + rows], p_x[:, k, 0:rows], ACT.Identity,
                                                        bias=g.modT[:, at + KT:at + KT + 1], scale=g.modT[:, at:at + 1])
                        last.then_inc(s_h2, TT // tiles)
                    for j in range(T_GROUPS):
                        act.wait_ge(s_mm, turn * GROUPS + j + 1)
                        bank = p_mm[j % BANKS]
                        if j < CT:
                            if j == 0:
                                act.wait_ge(s_carry, turn + 1)
                            nc.scalar.copy(raw[:, j, HIST:HIST + n], bank[:, 0:n]).then_inc(s_ev, 1)
                        else:
                            q = (j - CT) % 4
                            stores = 2 * turn + (j - CT) // 4
                            if not (first(turn) and j - CT < 4):
                                act.wait_ge(s_qo[q], stores * 16)
                            if j - CT < 4 and not first(turn):
                                act.wait_ge(s_kt, turn * KTILES)
                            nc.scalar.copy(qk[:, q, 0:n], bank[:, 0:n]).then_inc(s_ev, 1)
                            act.wait_ge(s_ev, turn * GROUPS + j + 1)
                            act.dma_start(g.qk_d[j - CT, :, tokens(turn, n)], qk[:, q, 0:n]).then_inc(s_qo[q], 16)
                        if 0 < j <= CT:
                            convolved(turn, n, j - 1)
                    prepare_next()
                    for t in range(TT):
                        for zi in range(2):
                            k = T_GROUPS + 2 * t + zi
                            done = s_vo if zi else s_zo
                            if t >= tiles:
                                continue
                            slot = 2 * (t % 2) + zi
                            act.wait_ge(s_mm, turn * GROUPS + k + 1)
                            if not grp:
                                act.wait_ge(done, (1 + (turn - 1) * TT + t) * 16)
                            nc.scalar.activation(zv[0:rows, slot, :], p_mm[k % BANKS][0:rows, :],
                                                 ACT.Copy if zi else ACT.Silu).then_inc(s_ev, last_of(tiles, zi))
                            if grp:
                                dst = g.outs["v_sample"] if zi else g.z_d[g.SEQ:g.TOK, :]
                            else:
                                dst = (g.outs["v_prompt"] if zi else g.z_d)[bass.ds((turn - 1) * SLAB + t * P, P), :]
                            act.wait_ge(s_ev, turn * GROUPS + T_GROUPS + 2 * t + zi + last_of(tiles, zi))
                            act.dma_start(dst, zv[0:rows, slot, :]).then_inc(done, 16)
                    act.wait_ge(s_kr, (turn + 1) * KTILES)
                    if grp:
                        act.dma_start(g.outs["k_sample"], krow[0:rows, 0, :]).then_inc(s_ko, 16)
                    else:
                        act.dma_start(g.outs["k_prompt"][bass.ds((turn - 1) * SLAB, SLAB), :].rearrange("(t p) n -> p t n", p=P),
                                      krow[:]).then_inc(s_ko, 16)

                slabs(body, prepare, act)
                act.wait_ge(s_tail, 2 + CT // 4)
                act.dma_start(g.outs["conv_prompt"], tail_rows[0:HIST, :]).then_inc(s_to, 16)
                act.dma_start(g.outs["conv_sample"], tail_rows[HIST:, :]).then_inc(s_to, 16)
                turns = SLABS + 1
                act.wait_ge(s_to, 32)
                act.wait_ge(s_ko, turns * 16)
                act.wait_ge(s_zo, (1 + g.TILES) * 16)
                act.wait_ge(s_vo, (1 + g.TILES) * 16)
                for s in s_co:
                    act.wait_ge(s, turns * (CT // 2) * 16)
                for s in s_qo:
                    act.wait_ge(s, turns * (QKT // 4) * 16)

            @block.tensor
            def _(pe):
                pe.wait_ge(s_small, 32)
                for c in range(CT):
                    last = nc.tensor.transpose(p_kt[0][:].rearrange("p t n -> p (t n)")[:, 8 * c:8 * c + HIST + CONV_W],
                                               small[:, c * P:(c + 1) * P], g.ident[0:HIST + CONV_W, 0:HIST + CONV_W])
                last.then_inc(s_trt, 1)

                def body(turn, _):
                    grp, rows, tiles, n = slab_shape(turn)
                    for t in range(tiles):
                        pe.wait_ge(s_xn, turn * TT + t + 1)
                        before = turn * TT + t
                        if not isinstance(before, int) or before > 0:
                            pe.wait_ge(s_h, before)
                            pe.wait_ge(s_h2, before)
                        for k in range(KT):
                            last = nc.tensor.transpose(p_x[:, k, 0:rows], x[0:rows, t, k * P:(k + 1) * P], g.ident[0:rows, 0:rows])
                        last.then_inc(s_xt, TT // tiles)
                    pe.wait_ge(s_h, (turn + 1) * TT)
                    pe.wait_ge(s_h2, (turn + 1) * TT)
                    if first(turn):
                        pe.wait_ge(s_w, 16 * KT)

                    def bank_free(k):
                        free = turn * GROUPS + k + 1 - BANKS
                        if not isinstance(free, int) or free > 0:
                            pe.wait_ge(s_ev, free)

                    for j in range(T_GROUPS):
                        col = j * P if j < CT else g.OFF_QB + (j - CT) * P
                        bank_free(j)
                        for k in range(KT):
                            mm = nc.tensor.matmul(p_mm[j % BANKS][:, 0:n], w[:, k, col:col + P], hT[:, k, 0:n],
                                                  start=(k == 0), stop=(k == KT - 1))
                        mm.then_inc(s_mm, 1)
                    for t in range(TT):
                        for zi in range(2):
                            k2 = T_GROUPS + 2 * t + zi
                            if t >= tiles:
                                continue
                            col = g.OFF_VB if zi else g.OFF_Z
                            bank_free(k2)
                            for k in range(KT):
                                mm = nc.tensor.matmul(p_mm[k2 % BANKS][0:rows, :], hT[:, k, t * P:t * P + rows],
                                                      w[:, k, col:col + g.ROWS], start=(k == 0), stop=(k == KT - 1))
                            mm.then_inc(s_mm, last_of(tiles, zi))
                        if t == 0:
                            keys_to_rows(turn, rows, tiles)
                    if not first(turn):
                        pe.wait_ge(s_bg, turn)
                    for t in range(tiles):
                        for k in range(KT):
                            mm = nc.tensor.matmul(p_bg[0:rows, 8 * t:8 * t + 8], hT[:, k, t * P:t * P + rows],
                                                  w[:, k, g.OFF_B:g.OFF_QB], start=(k == 0), stop=(k == KT - 1))
                    mm.then_inc(s_bgm, 1)

                def keys_to_rows(turn, rows, tiles):
                    for c in range(KTILES):
                        pe.wait_ge(s_ev, turn * GROUPS + CT + KTILES + c + 1)
                        free = turn * KTILES + c - 1
                        if c < 1 or c < 2:
                            if first(turn):
                                pe.wait_ge(s_wc, 2)
                        if not isinstance(free, int) or free > 0:
                            pe.wait_ge(s_kr, free)
                        for t in range(tiles):
                            tr = nc.tensor.transpose(p_kt[c % 2][0:rows, t, :], qk[:, c, t * P:t * P + rows], g.ident[:])
                        tr.then_inc(s_kt, 1)

                slabs(body, lambda turn: None, pe)
                pe.wait_ge(s_tail, 2)
                pe.wait_ge(s_ev, (SLABS + 1) * GROUPS)
                for c in range(CT):
                    last = nc.tensor.transpose(p_mm[c // 4][0:2 * HIST, (c % 4) * P:(c % 4 + 1) * P], tail[:, c, :], g.ident[:])
                last.then_inc(s_trt, 1)

            @block.vector
            def _(dve):
                link = Steps(s_link, dve, CHAIN)
                nc.vector.memset(eps[:], EPS).then_inc(s_wc, 1)
                dve.wait_ge(s_trt, 1)
                nc.vector.tensor_copy(cw[:], p_kt[0][:].rearrange("p t n -> p (t n)")[:, 0:8 * CT]
                                      .rearrange("p (c e) -> p c e", e=8)[:, :, 0:HIST + CONV_W]).then_inc(s_wc, 1)
                dve.wait_ge(s_wc, 2)
                nc.vector.tensor_copy(raw[:, :, 0:HIST], cw[:, :, 0:HIST]).then_inc(s_carry, 1)

                def prepare(turn):
                    grp, rows, tiles, n = slab_shape(turn)
                    link.begin(turn)
                    dve.wait_ge(s_std, turn + 1)
                    rec = nc.vector.reciprocal(rstd[0:rows, 0:tiles], std[0:rows, 0:tiles])
                    link.link(rec)
                    for t in range(tiles):
                        nc.vector.tensor_scalar(x[0:rows, t, :], x[0:rows, t, :], rstd[0:rows, t:t + 1], None,
                                                ALU.mult).then_inc(s_xn, TT // tiles)

                def body(turn, prepare_next):
                    grp, rows, tiles, n = slab_shape(turn)
                    link.begin(turn, 1)
                    if not first(turn):
                        dve.wait_ge(s_bgm, turn)
                    for t in range(tiles):
                        dve.wait_ge(s_xt, turn * TT + t + 1)
                        for k in range(KT // 2):
                            at = grp * 2 * KT + k
                            last = nc.vector.tensor_scalar(hT[:, k, t * P:t * P + rows], p_x[:, k, 0:rows],
                                                           g.modT[:, at:at + 1], g.modT[:, at + KT:at + KT + 1],
                                                           ALU.mult, ALU.add)
                        last.then_inc(s_h, TT // tiles)
                    for c in range(CT):
                        dve.wait_ge(s_ev, turn * GROUPS + c + 1)
                        used = turn * CT + c - 1
                        if not isinstance(used, int) or used > 0:
                            dve.wait_ge(s_silu, used)
                        a = acc[:, c % 2, 0:n]
                        link.link(nc.vector.tensor_scalar(a, raw[:, c, 0:n], cw[:, c, HIST:HIST + 1], None, ALU.mult))
                        for i in range(1, CONV_W):
                            step = nc.vector.scalar_tensor_tensor(out=a, in0=raw[:, c, i:i + n], scalar=cw[:, c, HIST + i:HIST + i + 1],
                                                                  in1=a, op0=ALU.mult, op1=ALU.add)
                            link.link(step)
                    if first(turn):
                        nc.vector.tensor_copy(tail[:, :, HIST:2 * HIST], raw[:, :, n:n + HIST]).then_inc(s_tail, 1)
                        nc.vector.memset(raw[:, :, 0:HIST], 0.0).then_inc(s_carry, 1)
                    else:
                        nc.vector.tensor_copy(raw[:, :, 0:HIST], raw[:, :, n:n + HIST]).then_inc(s_carry, 1)
                    link.end()
                    prepare_next()
                    for c in range(KTILES):
                        dve.wait_ge(s_kt, turn * KTILES + c + 1)
                        if c == 0 and not first(turn):
                            dve.wait_ge(s_ko, turn * 16)
                        nc.vector.tensor_copy(krow[0:rows, 0:tiles, c * P:(c + 1) * P], p_kt[c % 2][0:rows, 0:tiles, :]).then_inc(s_kr, 1)
                    dve.wait_ge(s_bgm, turn + 1)
                    tile0 = g.TILES if first(turn) else (turn - 1) * TT
                    nc.vector.tensor_copy(g.bg[0:rows, bass.ds(tile0, tiles), :],
                                          p_bg[0:rows, 0:8 * tiles].rearrange("p (t c) -> p t c", c=8)).then_inc(s_bg, 1)

                slabs(body, prepare, dve)
                dve.wait_ge(s_carry, SLABS + 2)
                nc.vector.tensor_copy(tail[:, :, 0:HIST], raw[:, :, 0:HIST]).then_inc(s_tail, 1)
                dve.wait_ge(s_trt, 2)
                for b in range(CT // 4):
                    nc.vector.tensor_copy(tail_rows[:, b * 512:(b + 1) * 512], p_mm[b][0:2 * HIST, :]).then_inc(s_tail, 1)


class Line:

    def __init__(self, sem, steps, base=0):
        self.sem, self.steps, self.at, self.base = sem, list(steps), 0, base

    def __call__(self, turn, step):
        return turn * len(self.steps) + self.steps.index(step) + 1 + self.base

    def next_stage(self, turns, steps):
        return Line(self.sem, steps, self.base + turns * len(self.steps))

    def did(self, step):
        assert self.steps[self.at % len(self.steps)] == step, (step, self.steps[self.at % len(self.steps)])
        self.at += 1
        return 1


def wide(ap, *shape):
    if len(ap.shape) == 3:
        return ap.to_broadcast(list(shape))
    axis = 2 if ap.shape[1] == shape[1] and ap.shape[1] != shape[2] else 1
    return ap.unsqueeze(axis).to_broadcast(list(shape))


def delta(nc, g):
    H, DD, NEW = DN_HEADS, DN_DIM, g.NEW
    LEVELS = 7
    s_in, s_z, s_par, s_s0 = g.sem("d_in"), g.sem("d_z"), g.sem("d_par"), g.sem("d_s0")
    s_out, s_sout, s_pre, s_exp = g.sem("d_out"), g.sem("d_sout"), g.sem("d_pre"), g.sem("d_exp")
    pe_a = Line(g.sem("steps_pe_a"), ["rows", "v_rows", "sums", "decay"])
    act_a = Line(g.sem("steps_act_a"), ["squares", "v", "e_rows", "e_next", "decay"])
    dve_a = Line(g.sem("steps_dve_a"), ["bg", "sum_sq", "q_sq", "k_sq", "kn", "qn"])
    pool_a = Line(g.sem("steps_pool_a"), ["g_mask", "r"])
    pe_b = Line(g.sem("steps_pe_b"), ["knT", "kbT", "qnT", "qdT", "kk", "kq", "L"]
                + [f"{a}{l}{h}" for l in range(1, LEVELS) for a in ("LT", "TLT") for h in range(2)])
    act_b = Line(g.sem("steps_act_b"), ["knT", "kbT", "qnT", "qdT"])
    dve_b = Line(g.sem("steps_dve_b"), ["LT", "B0", "T0", "AT"] + [f"{a}{l}{h}" for l in range(1, LEVELS) for a in ("m", "T") for h in range(2)])
    pool_b = Line(g.sem("steps_pool_b"), ["D", "kb", "qd", "vb", "kbe", "kd", "e_all", "B0T", "T0T"])
    pe_c = Line(g.sem("steps_pe_c"), ["u", "wT", "wS", "qS", "aV", "kV"])
    act_c = Line(g.sem("steps_act_c"), ["wT", "o_sq"])
    dve_c = Line(g.sem("steps_dve_c"), ["v_new", "o_sum", "state", "o_eps", "o_n", "o_g", "o_z"])
    pool_c = Line(g.sem("steps_pool_c"), ["S_dec", "o_r"])
    s_fresh = g.sem("d_fresh")
    g.lines = dict(pe_a=pe_a, pe_b=pe_b, act_a=act_a, act_b=act_b, act_c=act_c, dve_a=dve_a, dve_b=dve_b, dve_c=dve_c,
                   pool_a=pool_a, pool_c=pool_c)
    with ExitStack() as life:
        ct = g.sb("d_ct", [P, 3 * H, P], at=life)
        zt = g.sb("d_zt", [P, H, DD], at=life)
        par = g.sb("d_param", [P, 2, H], at=life)
        gain = g.sb("d_gain", [P, DD], at=life)
        sp_in = g.sb("d_sp", [P, g.T17, H], at=life)
        sp_abs = g.sb("d_spabs", [P, g.T17, H], at=life)
        bgt = g.sb("d_bg", [P, 2 * H], at=life)
        sq = g.sb("d_sq", [P, 2 * H, DD], at=life)
        ss = g.sb("d_ss", [P, 2 * H], at=life)
        ssn = g.sb("d_ssn", [P, 2 * H], at=life)
        r = g.sb("d_r", [P, 2 * H], at=life)
        e_rows = g.sb("d_er", [P, 2, H], at=life)
        e_next = g.sb("d_en", [P, H], at=life)
        e_all = g.sb("d_ea", [P, H], at=life)
        vr = g.sb("d_vr", [P, H, DD], at=life)
        gm = g.sb("d_gm", [P, H, P], at=life)
        dec = g.sb("d_dec", [P, H, P], at=life)
        dm = g.sb("d_dm", [P, H, P], at=life)
        kn, qn, vb, kb, qd, kbe, kd = (g.sb("d_" + n, [P, H, DD], at=life) for n in ("kn", "qn", "vb", "kb", "qd", "kbe", "kd"))
        knT, kbT, qnT, qdT, wT = (g.sb("d_" + n, [P, H, P], at=life) for n in ("knT", "kbT", "qnT", "qdT", "wT"))
        LT, AT, T, TT, B, BT = (g.sb("d_" + n, [P, H, P], at=life) for n in ("LT", "AT", "T", "TT", "B", "BT"))
        M = g.sb("d_m", [P, H, P], at=life)
        vn = g.sb("d_vn", [P, H, DD], at=life)
        S = g.sb("d_S", [P, H, DD], at=life)
        osq = g.sb("d_osq", [P, H, DD], at=life)
        oss = g.sb("d_oss", [P, H], at=life)
        osn = g.sb("d_osn", [P, H], at=life)
        orr = g.sb("d_orr", [P, H], at=life)
        o = g.sb("d_o", [P, H, DD], at=life)
        og = g.sb("d_og", [P, H, DD], at=life)
        oz = g.sb("d_oz", [P, H, DD], at=life)
        zero = g.sb("d_zero", [P, g.D], at=life)
        s_zero, s_zeros = g.sem("d_zero_set"), g.sem("d_zeros")
        FILL = -(-(g.BLOCKS - g.EXPERTS) // g.TILES)
        X = [g.psum(f"d_x{i}", [P, H, P], at=life) for i in range(4)]
        P1 = [g.psum(f"d_p1{i}", [P, H, P], at=life) for i in range(2)]
        P2 = [g.psum(f"d_p2{i}", [P, 2, 2, P], at=life) for i in range(2)]

        def turns(eng, start, body, end=lambda: None):
            start(0)
            body(0, True)
            body(1, True)
            with eng.Fori(2, g.TILES) as turn:
                body(turn, True)
            body(g.TILES, False)
            end()

        def done(eng, line, turn, step):
            if not isinstance(turn, int) or turn >= 0:
                eng.wait_ge(line.sem, line(turn, step))

        def shape(turn):
            first = isinstance(turn, int) and turn == 0
            n = NEW if first else P
            return not first, n, (g.TILES if first else turn - 1), (slice(g.SEQ, g.TOK) if first else bass.ds((turn - 1) * P, P))

        with nc.Block() as block:
            @block.sync
            def _(sp):
                for i, name in enumerate(["a_log", "dt_bias"]):
                    sp.dma_start(par[:, i, :], g.ins[name][0].partition_broadcast(P)).then_inc(s_par, 16)
                sp.dma_start(gain[:], g.ins["onorm_a"][0].partition_broadcast(P)).then_inc(s_par, 16)
                sp.dma_start(S[:], g.ins["state_delta"][0, 0].rearrange("h k v -> k h v")).then_inc(s_s0, 16)

                def load_ct(turn):
                    later, n, tile, at = shape(turn)
                    done(sp, pe_a, turn - 1, "v_rows")
                    sp.dma_start(ct[:, :, 0:n], g.conv_d[:, :, at].rearrange("c p t -> p c t")).then_inc(s_in, 16)

                def body(turn, follows):
                    later, n, tile, at = shape(turn)
                    if follows:
                        load_ct(turn + 1)
                    done(sp, dve_c, turn - 1, "o_z")
                    sp.dma_start(zt[0:n].rearrange("p h d -> p (h d)"), g.z_d[at, :]).then_inc(s_z, 16)
                    if later:
                        sp.dma_start(g.keysT[:, :, at], g.qk_d[g.QKT // 2:, :, at].rearrange("c p t -> p c t")).then_inc(g.s_kv, 16)
                        sp.dma_start(g.values[:, bass.ds(turn - 1, 1), :].rearrange("p a n -> p (a n)"), g.outs["v_prompt"][at, :]).then_inc(g.s_kv, 16)
                        sp.dma_start(g.y_d[bass.ds((turn - 1) * FILL * P + g.EXPERTS * P, FILL * P), :].rearrange("(b p) d -> p b d", p=P),
                                     zero[:].unsqueeze(1).to_broadcast([P, FILL, g.D])).then_inc(s_zeros, 16)
                    else:
                        sp.wait_ge(s_zero, 1)
                        sp.dma_start(g.h2_d[g.TOK:g.TOK + 1, :], zero[0:1]).then_inc(s_zeros, 16)

                turns(sp, load_ct, body)
                sp.wait_ge(s_zeros, (1 + g.TILES) * 16)

            @block.scalar
            def _(act):
                act.wait_ge(s_pre, 1)
                nc.scalar.activation(sp_abs[:], sp_abs[:], ACT.Exp, scale=-1.0).then_inc(s_exp, 1)
                nc.scalar.activation(g.bg[:, :, 0:H], g.bg[:, :, 0:H], ACT.Exp, scale=-1.0).then_inc(s_exp, 1)
                act.wait_ge(s_par, 48)
                nc.scalar.activation(par[:, 0, :], par[:, 0, :], ACT.Exp).then_inc(s_exp, 1)
                act.wait_ge(s_exp, 3)
                nc.scalar.activation(sp_abs[:], sp_abs[:], ACT.Ln, bias=1.0).then_inc(s_exp, 1)

                def part_a(turn):
                    later, n, tile, at = shape(turn)
                    done(act, pe_a, turn, "rows")
                    done(act, dve_a, turn - 1, "sum_sq")
                    nc.scalar.activation(sq[0:n, 0:H], X[0][0:n], ACT.Square)
                    nc.scalar.activation(sq[0:n, H:2 * H], X[1][0:n], ACT.Square).then_inc(act_a.sem, act_a.did("squares"))
                    done(act, pe_a, turn, "v_rows")
                    done(act, pool_b, turn - 1, "vb")
                    nc.scalar.copy(vr[0:n], X[2][0:n]).then_inc(act_a.sem, act_a.did("v"))
                    done(act, pe_a, turn, "sums")
                    done(act, pool_b, turn - 1, "e_all")
                    sums = X[3][:].rearrange("p h d -> p (h d)")
                    nc.scalar.activation(e_rows[0:n].rearrange("p a h -> p (a h)"), sums[0:n, 0:2 * H], ACT.Exp).then_inc(act_a.sem, act_a.did("e_rows"))
                    nc.scalar.activation(e_next[:], sums[:, 2 * H:3 * H], ACT.Exp).then_inc(act_a.sem, act_a.did("e_next"))
                    done(act, pe_a, turn, "decay")
                    done(act, pool_b, turn - 1, "D")
                    nc.scalar.activation(dec[0:n, :, 0:n], X[3][0:n, :, 0:n], ACT.Exp).then_inc(act_a.sem, act_a.did("decay"))

                def part_b(turn):
                    later, n, tile, at = shape(turn)
                    for name, src, dst, reads, reader in (("knT", P1[0][:], knT, pe_b, "kq"), ("kbT", P1[1][:], kbT, pe_b, "kk"),
                                                          ("qnT", P2[0][:].rearrange("p a b n -> p (a b) n"), qnT, pe_b, "kq"),
                                                          ("qdT", P2[1][:].rearrange("p a b n -> p (a b) n"), qdT, pe_c, "qS")):
                        done(act, pe_b, turn, name)
                        done(act, reads, turn - 1, reader)
                        nc.scalar.copy(dst[:, :, 0:n], src[:, :, 0:n]).then_inc(act_b.sem, act_b.did(name))

                def store(turn):
                    later, n, tile, at = shape(turn)
                    done(act, dve_c, turn, "o_z")
                    act.dma_start(g.merged_d[at, 0:H * DD], oz[0:n].rearrange("p h d -> p (h d)")).then_inc(s_out, 16)

                def store_before(turn):
                    store(turn - 1)

                def body(turn, follows):
                    later, n, tile, at = shape(turn)
                    if follows:
                        part_a(turn + 1)
                    if later:
                        store_before(turn)
                    done(act, pe_c, turn, "wT")
                    done(act, pe_c, turn - 1, "wS")
                    nc.scalar.mul(wT[:, :, 0:n], X[1][:, :, 0:n], -1.0).then_inc(act_c.sem, act_c.did("wT"))
                    if follows:
                        part_b(turn + 1)
                    done(act, pe_c, turn, "aV")
                    done(act, dve_c, turn - 1, "o_sum")
                    nc.scalar.activation(osq[0:n], X[2][0:n], ACT.Square).then_inc(act_c.sem, act_c.did("o_sq"))
                    if not later or not follows:
                        done(act, dve_c, turn, "state")
                        act.dma_start(g.outs["delta_prompt" if later else "delta_sample"].rearrange("h k v -> k h v"), S[:]).then_inc(s_sout, 16)

                def start(turn):
                    part_a(turn)
                    part_b(turn)

                turns(act, start, body, lambda: store(g.TILES))
                act.wait_ge(s_sout, 32)
                act.wait_ge(s_out, g.T17 * 16)

            @block.tensor
            def _(pe):
                def a_rows(turn):
                    later, n, tile, at = shape(turn)
                    pe.wait_ge(s_in, (turn + 1) * 16)
                    done(pe, dve_b, turn - 1, "AT")
                    for j in range(2 * H):
                        tr = nc.tensor.transpose(X[j // H][0:n, j % H, :], ct[:, j, 0:n], g.ident[:])
                    tr.then_inc(pe_a.sem, pe_a.did("rows"))

                def a_sums(turn):
                    later, n, tile, at = shape(turn)
                    if not isinstance(turn, int) or turn > 1:
                        done(pe, dve_c, turn - 2, "o_n")
                        done(pe, act_c, turn - 2, "o_sq")
                    for j in range(2 * H, 3 * H):
                        tr = nc.tensor.transpose(X[j // H][0:n, j % H, :], ct[:, j, 0:n], g.ident[:])
                    tr.then_inc(pe_a.sem, pe_a.did("v_rows"))
                    done(pe, dve_a, turn, "bg")
                    if not isinstance(turn, int) or turn > 1:
                        done(pe, dve_c, turn - 2, "state")
                    sums = X[3][:].rearrange("p h d -> p (h d)")
                    gt = bgt[0:n, H:2 * H]
                    nc.tensor.matmul(sums[0:n, 0:H], g.upto[0:n, 0:n], gt, start=True, stop=True)
                    nc.tensor.matmul(sums[0:n, H:2 * H], g.behind[0:n, 0:n], gt, start=True, stop=True)
                    nc.tensor.matmul(sums[:, 2 * H:3 * H], g.ones[0:n, :], gt, start=True, stop=True).then_inc(pe_a.sem, pe_a.did("sums"))

                def a_decay(turn):
                    later, n, tile, at = shape(turn)
                    done(pe, pool_a, turn, "g_mask")
                    done(pe, act_a, turn, "e_next")
                    for h in range(H):
                        mm = nc.tensor.matmul(X[3][0:n, h, 0:n], gm[0:n, h, 0:n], g.upto[0:n, 0:n], start=True, stop=True)
                    mm.then_inc(pe_a.sem, pe_a.did("decay"))

                def turned(turn, name, out, rows):
                    later, n, tile, at = shape(turn)
                    for h in range(H):
                        tr = nc.tensor.transpose(out[:, h, 0:n], rows[0:n, h, :], g.ident[0:n, 0:n])
                    tr.then_inc(pe_b.sem, pe_b.did(name))

                def b_keys(turn):
                    done(pe, dve_a, turn, "kn")
                    turned(turn, "knT", P1[0], kn)
                    done(pe, pool_b, turn, "kb")
                    turned(turn, "kbT", P1[1], kb)

                def b_queries(turn):
                    done(pe, dve_a, turn, "qn")
                    turned(turn, "qnT", P2[0][:].rearrange("p a b n -> p (a b) n"), qn)
                    done(pe, pool_b, turn, "qd")
                    turned(turn, "qdT", P2[1][:].rearrange("p a b n -> p (a b) n"), qd)

                def b_products(turn):
                    later, n, tile, at = shape(turn)
                    done(pe, act_b, turn, "kbT")
                    if not later:
                        done(pe, dve_a, turn, "qn")
                    for h in range(H):
                        mm = nc.tensor.matmul(X[0][0:n, h, 0:n], knT[:, h, 0:n], kbT[:, h, 0:n], start=True, stop=True)
                    mm.then_inc(pe_b.sem, pe_b.did("kk"))
                    done(pe, act_b, turn, "qnT")
                    for h in range(H):
                        mm = nc.tensor.matmul(X[1][0:n, h, 0:n], knT[:, h, 0:n], qnT[:, h, 0:n], start=True, stop=True)
                    mm.then_inc(pe_b.sem, pe_b.did("kq"))
                    done(pe, dve_b, turn, "LT")
                    for h in range(H):
                        tr = nc.tensor.transpose(P2[0][0:n, h // 2, h % 2, 0:n], LT[0:n, h, 0:n], g.ident[0:n, 0:n])
                    tr.then_inc(pe_b.sem, pe_b.did("L"))

                def level(turn, l):
                    later, n, tile, at = shape(turn)
                    for half in range(2):
                        if l == 1:
                            done(pe, dve_b, turn, "T0")
                            done(pe, pool_b, turn, "T0T")
                        else:
                            done(pe, dve_b, turn, f"T{l - 1}{half}")
                        for h in (2 * half, 2 * half + 1):
                            mm = nc.tensor.matmul(P1[half][0:n, h, 0:n], LT[0:n, h, 0:n], T[0:n, h, 0:n], start=True, stop=True)
                        mm.then_inc(pe_b.sem, pe_b.did(f"LT{l}{half}"))
                    for half in range(2):
                        done(pe, dve_b, turn, f"m{l}{half}")
                        if l == 1 and half == 1:
                            done(pe, act_b, turn, "qdT")
                        for h in (2 * half, 2 * half + 1):
                            if l < LEVELS - 1:
                                nc.tensor.matmul(P2[half][0:n, 0, h % 2, 0:n], TT[0:n, h, 0:n], M[0:n, h, 0:n], start=True, stop=True)
                            mm = nc.tensor.matmul(P2[half][0:n, 1, h % 2, 0:n], M[0:n, h, 0:n], TT[0:n, h, 0:n], start=True, stop=True)
                        mm.then_inc(pe_b.sem, pe_b.did(f"TLT{l}{half}"))

                def body(turn, follows):
                    later, n, tile, at = shape(turn)
                    for l in range(1, LEVELS):
                        level(turn, l)
                        if follows and l in (2, 3, 4):
                            (a_rows, a_sums, a_decay)[l - 2](turn + 1)
                    done(pe, dve_b, turn, f"T{LEVELS - 1}1")
                    done(pe, pool_b, turn, "vb")
                    if follows:
                        done(pe, dve_a, turn + 1, "qn")
                    for h in range(H):
                        mm = nc.tensor.matmul(X[0][0:n, h, :], TT[0:n, h, 0:n], vb[0:n, h, :], start=(h == 0), stop=False, skip_group_check=True)
                    mm.then_inc(pe_c.sem, pe_c.did("u"))
                    done(pe, pool_b, turn, "kbe")
                    for h in range(H):
                        mm = nc.tensor.matmul(X[1][:, h, 0:n], kbe[0:n, h, :], TT[0:n, h, 0:n], start=True, stop=True)
                    mm.then_inc(pe_c.sem, pe_c.did("wT"))
                    if follows:
                        b_keys(turn + 1)
                    done(pe, act_c, turn, "wT")
                    if later:
                        pe.wait_ge(s_fresh, 1)
                        done(pe, dve_c, turn - 1, "state")
                    else:
                        pe.wait_ge(s_s0, 16)
                    for h in range(H):
                        mm = nc.tensor.matmul(X[0][0:n, h, :], wT[:, h, 0:n], S[:, h, :], start=False, stop=True, skip_group_check=True)
                    mm.then_inc(pe_c.sem, pe_c.did("wS"))
                    if follows:
                        done(pe, act_a, turn + 1, "v")
                    for h in range(H):
                        mm = nc.tensor.matmul(X[2][0:n, h, :], qdT[:, h, 0:n], S[:, h, :], start=(h == 0), stop=False, skip_group_check=True)
                    mm.then_inc(pe_c.sem, pe_c.did("qS"))
                    if follows:
                        b_queries(turn + 1)
                    done(pe, dve_c, turn, "v_new")
                    for h in range(H):
                        mm = nc.tensor.matmul(X[2][0:n, h, :], AT[0:n, h, 0:n], vn[0:n, h, :], start=False, stop=True, skip_group_check=True)
                    mm.then_inc(pe_c.sem, pe_c.did("aV"))
                    done(pe, pool_b, turn, "kd")
                    if follows:
                        done(pe, act_a, turn + 1, "decay")
                    for h in range(H):
                        mm = nc.tensor.matmul(X[3][:, h, :], kd[0:n, h, :], vn[0:n, h, :], start=True, stop=True)
                    mm.then_inc(pe_c.sem, pe_c.did("kV"))
                    if follows:
                        b_products(turn + 1)

                def start(turn):
                    a_rows(turn)
                    a_sums(turn)
                    a_decay(turn)
                    b_keys(turn)
                    b_queries(turn)
                    b_products(turn)

                turns(pe, start, body)

            @block.vector
            def _(dve):
                link = Steps(g.sem("d_link"), dve, 7)
                link.begin(0)
                nc.vector.memset(zero[:], 0.0).then_inc(s_zero, 1)
                dve.wait_ge(s_par, 48)
                link.link(nc.vector.tensor_copy(sp_in[:], g.bg[:, :, H:2 * H]))
                link.link(nc.vector.tensor_tensor(sp_in[:], sp_in[:], wide(par[:, 1, :], P, g.T17, H), ALU.add))
                nc.vector.scalar_tensor_tensor(out=sp_abs[:], in0=sp_in[:], scalar=-1.0, in1=sp_in[:], op0=ALU.mult,
                                               op1=ALU.max).then_inc(s_pre, 1)
                dve.wait_ge(s_exp, 4)
                link.link(nc.vector.scalar_tensor_tensor(out=sp_in[:], in0=sp_in[:], scalar=0.0, in1=sp_abs[:], op0=ALU.max, op1=ALU.add))
                link.link(nc.vector.tensor_tensor(sp_in[:], sp_in[:], wide(par[:, 0, :], P, g.T17, H), ALU.mult))
                link.link(nc.vector.tensor_scalar(g.bg[:, :, H:2 * H], sp_in[:], -1.0, None, ALU.mult))
                link.link(nc.vector.tensor_scalar(g.bg[:, :, 0:H], g.bg[:, :, 0:H], 1.0, None, ALU.add))
                link.link(nc.vector.reciprocal(g.bg[:, :, 0:H], g.bg[:, :, 0:H]))

                V = nc.vector

                def heads(a, n):
                    return wide(a, n, H, DD)

                def a_decays(turn):
                    later, n, tile, at = shape(turn)
                    done(dve, pe_a, turn - 1, "sums")
                    done(dve, pool_b, turn - 1, "vb")
                    V.tensor_copy(bgt[0:n], g.bg[0:n, bass.ds(tile, 1), :].rearrange("p a c -> p (a c)")).then_inc(dve_a.sem, dve_a.did("bg"))

                def a_norms(turn):
                    later, n, tile, at = shape(turn)
                    done(dve, act_a, turn, "squares")
                    V.tensor_reduce(ss[0:n], sq[0:n], AX, ALU.add).then_inc(dve_a.sem, dve_a.did("sum_sq"))
                    done(dve, dve_a, turn, "sum_sq")
                    done(dve, pool_a, turn - 1, "r")
                    V.tensor_scalar(ssn[0:n, 0:H], ss[0:n, 0:H], EPS, float(DD), ALU.add, ALU.mult).then_inc(dve_a.sem, dve_a.did("q_sq"))
                    V.tensor_scalar(ssn[0:n, H:2 * H], ss[0:n, H:2 * H], EPS, None, ALU.add).then_inc(dve_a.sem, dve_a.did("k_sq"))

                def a_rows(turn):
                    later, n, tile, at = shape(turn)
                    done(dve, pool_a, turn, "r")
                    done(dve, pool_b, turn - 1, "kd")
                    done(dve, pe_b, turn - 1, "qnT")
                    V.tensor_tensor(kn[0:n], X[1][0:n], heads(r[0:n, H:2 * H], n), ALU.mult).then_inc(dve_a.sem, dve_a.did("kn"))
                    V.tensor_tensor(qn[0:n], X[0][0:n], heads(r[0:n, 0:H], n), ALU.mult).then_inc(dve_a.sem, dve_a.did("qn"))

                def b_lower(turn):
                    later, n, tile, at = shape(turn)
                    done(dve, pe_b, turn, "kk")
                    done(dve, pool_b, turn, "D")
                    V.tensor_tensor(LT[0:n, :, 0:n], X[0][0:n, :, 0:n], dm[0:n, :, 0:n], ALU.mult).then_inc(dve_b.sem, dve_b.did("LT"))

                def b_begin(turn):
                    later, n, tile, at = shape(turn)
                    done(dve, pe_b, turn, "L")
                    L_rows = P2[0][:].rearrange("p a b n -> p (a b) n")
                    V.tensor_tensor(B[0:n, :, 0:n], L_rows[0:n, :, 0:n], g.level[0:n, 0:1, 0:n].to_broadcast([n, H, n]), ALU.mult).then_inc(dve_b.sem, dve_b.did("B0"))
                    done(dve, dve_b, turn, "B0")
                    V.tensor_tensor(T[0:n, :, 0:n], g.ident[0:n, 0:n].unsqueeze(1).to_broadcast([n, H, n]), B[0:n, :, 0:n], ALU.subtract).then_inc(dve_b.sem, dve_b.did("T0"))

                def b_weights(turn):
                    later, n, tile, at = shape(turn)
                    done(dve, pe_b, turn, "kq")
                    V.tensor_tensor(AT[0:n, :, 0:n], X[1][0:n, :, 0:n], dm[0:n, :, 0:n], ALU.mult).then_inc(dve_b.sem, dve_b.did("AT"))

                def level(turn, l):
                    later, n, tile, at = shape(turn)
                    for half in range(2):
                        hh = slice(2 * half, 2 * half + 2)
                        done(dve, pe_b, turn, f"LT{l}{half}")
                        if l == 1:
                            done(dve, pool_b, turn, "T0T")
                        V.tensor_tensor(M[0:n, hh, 0:n], P1[half][0:n, hh, 0:n], g.level[0:n, l:l + 1, 0:n].to_broadcast([n, 2, n]),
                                        ALU.mult).then_inc(dve_b.sem, dve_b.did(f"m{l}{half}"))
                    for half in range(2):
                        hh = slice(2 * half, 2 * half + 2)
                        done(dve, pe_b, turn, f"TLT{l}{half}")
                        if l < LEVELS - 1:
                            V.tensor_tensor(T[0:n, hh, 0:n], T[0:n, hh, 0:n], P2[half][0:n, 0, :, 0:n], ALU.subtract)
                        V.tensor_tensor(TT[0:n, hh, 0:n], TT[0:n, hh, 0:n], P2[half][0:n, 1, :, 0:n], ALU.subtract).then_inc(dve_b.sem, dve_b.did(f"T{l}{half}"))

                def c_values(turn):
                    later, n, tile, at = shape(turn)
                    done(dve, pe_c, turn, "wS")
                    V.tensor_copy(vn[0:n], X[0][0:n]).then_inc(dve_c.sem, dve_c.did("v_new"))

                def c_sums(turn):
                    later, n, tile, at = shape(turn)
                    done(dve, act_c, turn, "o_sq")
                    V.tensor_reduce(oss[0:n], osq[0:n], AX, ALU.add).then_inc(dve_c.sem, dve_c.did("o_sum"))

                def c_state(turn):
                    later, n, tile, at = shape(turn)
                    done(dve, pe_c, turn, "kV")
                    done(dve, pool_c, turn, "S_dec")
                    V.tensor_tensor(S[:], S[:], X[3][:], ALU.add).then_inc(dve_c.sem, dve_c.did("state"))
                    done(dve, dve_c, turn, "o_sum")
                    V.tensor_scalar(osn[0:n], oss[0:n], 1.0 / DD, EPS, ALU.mult, ALU.add).then_inc(dve_c.sem, dve_c.did("o_eps"))

                def c_norm(turn):
                    later, n, tile, at = shape(turn)
                    done(dve, pool_c, turn, "o_r")
                    V.tensor_tensor(o[0:n], X[2][0:n], heads(orr[0:n], n), ALU.mult).then_inc(dve_c.sem, dve_c.did("o_n"))

                def c_gain(turn):
                    later, n, tile, at = shape(turn)
                    done(dve, dve_c, turn, "o_n")
                    V.tensor_tensor(og[0:n], o[0:n], gain[0:n].unsqueeze(1).to_broadcast([n, H, DD]), ALU.mult).then_inc(dve_c.sem, dve_c.did("o_g"))

                def c_gate(turn):
                    later, n, tile, at = shape(turn)
                    done(dve, dve_c, turn, "o_g")
                    dve.wait_ge(s_z, (turn + 1) * 16)
                    if later:
                        dve.wait_ge(s_out, turn * 16)
                    V.tensor_tensor(oz[0:n], og[0:n], zt[0:n], ALU.mult).then_inc(dve_c.sem, dve_c.did("o_z"))

                def body(turn, follows):
                    later, n, tile, at = shape(turn)
                    for l in range(1, LEVELS):
                        level(turn, l)
                        if later and l in (1, 2, 4):
                            {1: c_norm, 2: c_gain, 4: c_gate}[l](turn - 1)
                        if follows and l in (1, 3, 5):
                            {1: a_decays, 3: a_norms, 5: a_rows}[l](turn + 1)
                    c_values(turn)
                    if follows:
                        b_lower(turn + 1)
                    c_sums(turn)
                    if follows:
                        b_begin(turn + 1)
                    c_state(turn)
                    if follows:
                        b_weights(turn + 1)
                    if not later:
                        dve.wait_ge(s_sout, 16)
                        V.memset(S[:], 0.0).then_inc(s_fresh, 1)

                def start(turn):
                    a_decays(turn)
                    a_norms(turn)
                    a_rows(turn)
                    b_lower(turn)
                    b_begin(turn)
                    b_weights(turn)

                def end():
                    c_norm(g.TILES)
                    c_gain(g.TILES)
                    c_gate(g.TILES)

                turns(dve, start, body, end)

            @block.gpsimd
            def _(pool):
                G = nc.gpsimd

                def did(line, name, turn, ins):
                    ins.then_inc(line.sem, line.did(name))
                    if isinstance(turn, int):
                        done(pool, line, turn, name)

                def heads(a, n):
                    return wide(a, n, H, DD)

                def part_a(turn):
                    later, n, tile, at = shape(turn)
                    done(pool, dve_a, turn, "bg")
                    done(pool, pe_a, turn - 1, "decay")
                    did(pool_a, "g_mask", turn, G.tensor_tensor(gm[0:n, :, 0:n], g.behind[0:n, 0:n].unsqueeze(1).to_broadcast([n, H, n]),
                                                                bgt[0:n, H:2 * H].unsqueeze(2).to_broadcast([n, H, n]), ALU.mult))
                    done(pool, dve_a, turn, "k_sq")
                    done(pool, dve_a, turn - 1, "qn")
                    did(pool_a, "r", turn, G.tensor_tensor(r[0:n], ssn[0:n], g.half[0:n, 0:2 * H], ALU.pow))

                def b_rows(turn):
                    later, n, tile, at = shape(turn)
                    done(pool, act_a, turn, "decay")
                    done(pool, dve_b, turn - 1, "AT")
                    did(pool_b, "D", turn, G.tensor_tensor(dm[0:n, :, 0:n], dec[0:n, :, 0:n], g.upto[0:n, 0:n].unsqueeze(1).to_broadcast([n, H, n]), ALU.mult))
                    done(pool, dve_a, turn, "kn")
                    done(pool, pe_b, turn - 1, "qdT")
                    did(pool_b, "kb", turn, G.tensor_tensor(kb[0:n], kn[0:n], heads(bgt[0:n, 0:H], n), ALU.mult))
                    done(pool, dve_a, turn, "qn")
                    did(pool_b, "qd", turn, G.tensor_tensor(qd[0:n], qn[0:n], heads(e_rows[0:n, 0, :], n), ALU.mult))

                def b_solved(turn):
                    later, n, tile, at = shape(turn)
                    done(pool, pe_c, turn - 1, "u")
                    did(pool_b, "vb", turn, G.tensor_tensor(vb[0:n], vr[0:n], heads(bgt[0:n, 0:H], n), ALU.mult))
                    done(pool, pe_c, turn - 1, "wT")
                    done(pool, pool_b, turn, "kb")
                    did(pool_b, "kbe", turn, G.tensor_tensor(kbe[0:n], kb[0:n], heads(e_rows[0:n, 0, :], n), ALU.mult))

                def b_state(turn):
                    later, n, tile, at = shape(turn)
                    done(pool, pe_c, turn - 1, "kV")
                    did(pool_b, "kd", turn, G.tensor_tensor(kd[0:n], kn[0:n], heads(e_rows[0:n, 1, :], n), ALU.mult))
                    done(pool, pool_c, turn - 1, "S_dec")
                    did(pool_b, "e_all", turn, G.tensor_tensor(e_all[:], e_next[:], g.ones[:, 0:H], ALU.mult))

                def b_start(turn):
                    later, n, tile, at = shape(turn)
                    done(pool, dve_b, turn, "LT")
                    did(pool_b, "B0T", turn, G.tensor_tensor(BT[0:n, :, 0:n], LT[0:n, :, 0:n], g.level[0:n, LEVELS:LEVELS + 1, 0:n].to_broadcast([n, H, n]), ALU.mult))
                    done(pool, pool_b, turn, "B0T")
                    did(pool_b, "T0T", turn, G.tensor_tensor(TT[0:n, :, 0:n], g.ident[0:n, 0:n].unsqueeze(1).to_broadcast([n, H, n]), BT[0:n, :, 0:n], ALU.subtract))

                def body(turn, follows):
                    later, n, tile, at = shape(turn)
                    if follows:
                        part_a(turn + 1)
                        b_rows(turn + 1)
                        b_solved(turn + 1)
                    done(pool, pe_c, turn, "qS")
                    did(pool_c, "S_dec", turn, G.tensor_tensor(S[:], S[:], e_all[:].unsqueeze(2).to_broadcast([P, H, DD]), ALU.mult))
                    if follows:
                        b_state(turn + 1)
                        b_start(turn + 1)
                    done(pool, dve_c, turn, "o_eps")
                    did(pool_c, "o_r", turn, G.tensor_tensor(orr[0:n], osn[0:n], g.half[0:n, 0:H], ALU.pow))

                def start(turn):
                    part_a(turn)
                    b_rows(turn)
                    b_solved(turn)
                    b_state(turn)
                    b_start(turn)

                turns(pool, start, body)


def sticks(nc, g):
    H, DD, NEW = SB_HEADS, SB_DIM, g.NEW
    HS = H // 2
    PAIRS = g.QKT // 2
    NEW_BLOCK, PAST_BLOCK = g.TILES, g.TILES + 1
    SCALE = float(DD) ** -0.5
    MASKED = -1e30
    s_kv, s_new, s_past, s_gain = g.s_kv, g.sem("a_new"), g.sem("a_past"), g.sem("a_gain")
    s_zero, s_mask, s_turned, s_ready = g.sem("a_zero"), g.sem("a_mask"), g.sem("a_turned"), g.sem("a_ready")
    s_q, s_qz = g.sem("a_q"), g.sem("a_qz")
    pair = lambda name: [g.sem(f"a_{name}{a}") for a in range(2)]
    s_z, s_zm, s_keep, s_beta, s_scan, s_carry, s_a, s_t, s_ev, s_v = (
        pair(n) for n in ("z", "zm", "keep", "beta", "scan", "carry", "a", "t", "ev", "v"))
    end_act = g.lines["act_c"] = g.lines["act_c"].next_stage(g.T17, ["o_sq"])
    end_dve = g.lines["dve_c"].next_stage(g.T17, ["o_sum", "o_eps", "o_n", "o_g"])
    end_pool = g.lines["pool_c"].next_stage(g.T17, ["o_r"])
    s_out = g.sem("a_out")
    with ExitStack() as life:
        KT, V = g.keysT, g.values
        past = g.sb("a_past", [P, H * DD], at=life)
        gain = g.sb("a_gainb", [P, DD], at=life)
        mask = g.sb("a_maskb", [P, P], at=life)
        q_in = g.sb("a_qin", [P, PAIRS, P], at=life)
        QZ = [g.sb(f"a_QZ{b}", [P, H, P], at=life) for b in range(2)]
        zm = [g.sb(f"a_zm{a}", [P, HS, P], at=life) for a in range(2)]
        keep = [g.sb(f"a_keep{a}", [P, HS, P + 1], at=life) for a in range(2)]
        beta = [g.sb(f"a_beta{a}", [P, HS, P], at=life) for a in range(2)]
        carry = [g.sb(f"a_carry{a}", [P, HS, P + 1], at=life) for a in range(2)]
        prod = [g.sb(f"a_prod{a}", [P, HS, P + 1], at=life) for a in range(2)]
        A = [g.sb(f"a_A{a}", [P, HS, P], at=life) for a in range(2)]
        AT = [g.sb(f"a_AT{a}", [P, HS, P], at=life) for a in range(2)]
        osq = g.sb("a_osq", [P, H, DD], at=life)
        oss, osn, orr = (g.sb("a_" + n, [P, H], at=life) for n in ("oss", "osn", "orr"))
        o = g.sb("a_o", [P, H, DD], at=life)
        og = g.sb("a_og", [P, H, DD], at=life)
        Z = [g.psum(f"a_z{a}", [P, HS, P], at=life) for a in range(2)]
        TR = [g.psum(f"a_tr{a}", [P, HS, P], at=life) for a in range(2)]
        acc = [g.psum(f"a_acc{b}", [P, H, DD], at=life) for b in range(2)]
        p_past = g.psum("a_pp", [P, PAIRS, P], at=life)

        def shape(turn):
            if isinstance(turn, int) and turn == 0:
                return NEW, slice(g.SEQ, g.TOK), 0, 1, lambda i: (NEW_BLOCK, PAST_BLOCK)[i]
            q = turn - 1
            return P, bass.ds(q * P, P), 2 + q * (q + 1) // 2, q, lambda i: i * -1 + q

        STEPS = 2 + g.TILES * (g.TILES + 1) // 2

        def first_of_all(turn):
            return isinstance(turn, int) and turn == 0

        def turns(eng, body):
            for turn in range(3):
                body(turn, turn % 2)
            with eng.Fori(1, (g.TILES - 2) // 2) as p:
                body(2 * p + 1, 1)
                body(2 * p + 2, 0)
            for turn in range(g.TILES - 1, g.TILES + 1):
                body(turn, turn % 2)

        def after(eng, sem, count):
            if not isinstance(count, int) or count > 0:
                eng.wait_ge(sem, count)

        def later_steps(eng, first, last, body):
            if isinstance(last, int) and last < first + 2:
                for i in range(first, last + 1):
                    body(i)
            else:
                with eng.Fori(first, last + 1) as i:
                    body(i)

        def flat(t, n):
            return t[0:n].rearrange("p h k -> p (h k)")[:, ::-1]

        with nc.Block() as block:
            @block.sync
            def _(sp):
                sp.dma_start(past[:], g.ins["cache_k"][0, 0].rearrange("t h d -> t (h d)")).then_inc(s_past, 16)
                sp.dma_start(gain[:], g.ins["onorm_b"][0].partition_broadcast(P)).then_inc(s_gain, 16)
                sp.wait_ge(s_zero, 2)
                sp.dma_start(KT[:, :, NEW_BLOCK * P:NEW_BLOCK * P + NEW], g.qk_d[PAIRS:, :, g.SEQ:g.TOK].rearrange("c p t -> p c t")).then_inc(s_new, 16)
                sp.dma_start(V[0:NEW, NEW_BLOCK, :], g.outs["v_sample"]).then_inc(s_new, 16)
                sp.dma_start(V[:, PAST_BLOCK, :], g.ins["cache_v"][0, 0].rearrange("t h d -> t (h d)")).then_inc(s_new, 16)

                def body(turn, b):
                    n, at, g0, last, block_of = shape(turn)
                    if not first_of_all(turn):
                        sp.wait_ge(s_qz, 2 * turn)
                    sp.dma_start(q_in[:, :, 0:n], g.qk_d[0:PAIRS, :, at].rearrange("c p t -> p c t")).then_inc(s_q, 16)
                    if isinstance(turn, int) and turn == 0:
                        return
                    store(turn - 1, NEW if isinstance(turn, int) and turn == 1 else P,
                          slice(g.SEQ, g.TOK) if isinstance(turn, int) and turn == 1 else bass.ds((turn - 2) * P, P))

                def store(turn, n, at):
                    sp.wait_ge(end_dve.sem, end_dve(turn, "o_g"))
                    sp.dma_start(g.merged_d[at, DN_HEADS * DN_DIM:], og[0:n].rearrange("p h d -> p (h d)")).then_inc(s_out, 16)

                turns(sp, body)
                D = g.D
                for a in range(2):
                    for tile, row in ((g.post[a], 2), (g.scale[a], 4), (g.shift[a], 3)):
                        sp.dma_start(tile[:], g.mod_d[a, row * D:(row + 1) * D].partition_broadcast(P)).then_inc(g.s_rows_mixed, 16)
                for i, name in enumerate(["g_post_mix", "g_pre_ffn"]):
                    sp.dma_start(g.gains[:, i, :], g.ins[name][0].partition_broadcast(P)).then_inc(g.s_rows_mixed, 16)
                GE = g.GROUPS_E
                for name, cols in (("group", slice(0, GE)), ("expert", slice(GE, None))):
                    sp.dma_start(g.b_router[:, cols], g.ins[f"b_router_{name}"][0].partition_broadcast(P)).then_inc(g.s_rows_mixed, 16)
                    sp.dma_start(g.w_router[:, :, cols], g.ins[f"w_router_{name}"][0].rearrange("(k p) n -> p k n", p=P)).then_inc(g.s_w_mixed, 16)
                sp.dma_start(g.w_out[:], g.ins["w_out"][0].rearrange("(k p) n -> p k n", p=P)).then_inc(g.s_w_mixed, 16)
                store(g.TILES, P, slice(g.SEQ - P, g.SEQ))
                sp.wait_ge(s_out, g.T17 * 16)

            @block.tensor
            def _(pe):
                pe.wait_ge(s_past, 16)
                for j in range(PAIRS):
                    tr = nc.tensor.transpose(p_past[:, j, :], past[:, j * P:(j + 1) * P], g.ident[:])
                tr.then_inc(s_turned, 1)
                pe.wait_ge(s_ready, 1)
                pe.wait_ge(s_new, 48)

                def score(turn, b, i, a):
                    n, at, g0, last, block_of = shape(turn)
                    key = block_of(i)
                    if not isinstance(key, int):
                        key = nc.s_assert_within(key, 0, g.TILES - 1, skip_runtime_bounds_check_because="the walk ends at block 0")
                    if isinstance(i, int) and i == 0:
                        pe.wait_ge(s_qz, 2 * (turn + 1))
                        if isinstance(turn, int) and turn == 1:
                            pe.wait_ge(s_kv, 32 * g.TILES)
                    after(pe, s_beta[a], g0 + i)
                    for h in range(HS):
                        head = a * HS + h
                        mm = nc.tensor.matmul(Z[a][0:n, h, :], QZ[b][:, head, 0:n], KT[:, head // 2, bass.ds(key * P, P)],
                                              start=True, stop=True)
                    mm.then_inc(s_z[a], 1)

                def body(turn, b):
                    n, at, g0, last, block_of = shape(turn)

                    def block(i):
                        key = block_of(i)
                        return key if isinstance(key, int) else nc.s_assert_within(
                            key, 0, g.TILES - 1, skip_runtime_bounds_check_because="the walk ends at block 0")

                    def score_next(a):
                        if not (isinstance(turn, int) and turn == g.TILES):
                            score(turn + 1, 1 - b, 0, a)

                    def turn_over(i, a):
                        pe.wait_ge(s_a[a], g0 + i + 1)
                        after(pe, s_ev[a], g0 + i)
                        for h in range(HS):
                            tr = nc.tensor.transpose(TR[a][:, h, 0:n], A[a][0:n, h, :], g.ident[0:n, 0:n])
                        tr.then_inc(s_t[a], 1)

                    def weigh(i, a, first=False):
                        pe.wait_ge(s_ev[a], g0 + i + 1)
                        if first and not (isinstance(turn, int) and turn < 2):
                            pe.wait_ge(end_dve.sem, end_dve(turn - 2, "o_n"))
                            pe.wait_ge(end_act.sem, end_act(turn - 2, "o_sq"))
                        for h in range(HS):
                            head = a * HS + h
                            mm = nc.tensor.matmul(acc[b][0:n, head, :], AT[a][:, h, 0:n],
                                                  V[:, bass.ds(block(i), 1), head * DD:(head + 1) * DD].rearrange("p a n -> p (a n)"),
                                                  start=(first and h == 0), stop=True, skip_group_check=True)
                        mm.then_inc(s_v[a], 1)

                    if isinstance(last, int) and last == 0:
                        turn_over(0, 0)
                        score_next(0)
                        turn_over(0, 1)
                        weigh(0, 0, True)
                        score_next(1)
                        weigh(0, 1)
                        return
                    score(turn, b, 1, 0)
                    turn_over(0, 0)
                    score(turn, b, 1, 1)
                    turn_over(0, 1)
                    weigh(0, 0, True)

                    def step(i):
                        score(turn, b, i, 0)
                        turn_over(i - 1, 0)
                        weigh(i - 2, 1)
                        score(turn, b, i, 1)
                        turn_over(i - 1, 1)
                        weigh(i - 1, 0)

                    later_steps(pe, 2, last, step)
                    turn_over(last, 0)
                    weigh(last - 1, 1)
                    score_next(0)
                    turn_over(last, 1)
                    weigh(last, 0)
                    score_next(1)
                    weigh(last, 1)

                score(0, 0, 0, 0)
                score(0, 0, 0, 1)
                turns(pe, body)

            @block.scalar
            def _(act):
                act.wait_ge(s_turned, 1)
                nc.scalar.copy(KT[:, :, PAST_BLOCK * P:(PAST_BLOCK + 1) * P], p_past[:]).then_inc(s_ready, 1)

                def body(turn, b):
                    n, at, g0, last, block_of = shape(turn)

                    def squash(i, a, diagonal=False):
                        G = g0 + i
                        if diagonal:
                            act.wait_ge(s_zm[a], turn + 1)
                        else:
                            act.wait_ge(s_z[a], G + 1)
                        src = zm[a] if diagonal else Z[a]
                        after(act, s_scan[a], G)
                        after(act, s_keep[a], G)
                        nc.scalar.activation(keep[a][0:n, :, 0:P], src[0:n], ACT.Sigmoid, scale=-SCALE).then_inc(s_keep[a], 1)
                        after(act, s_a[a], G)
                        after(act, s_beta[a], G)
                        nc.scalar.activation(beta[a][0:n], src[0:n], ACT.Sigmoid, scale=SCALE).then_inc(s_beta[a], 1)

                    def take(i):
                        act.wait_ge(s_t[0], g0 + i + 1)
                        after(act, s_v[0], g0 + i)
                        nc.scalar.copy(AT[0][:, :, 0:n], TR[0][:, :, 0:n]).then_inc(s_ev[0], 1)

                    squash(0, 0, True)
                    squash(0, 1, True)
                    if not first_of_all(turn):
                        finish(turn - 1, 1 - b, NEW if isinstance(turn, int) and turn == 1 else P, g0)

                    def step(i):
                        squash(i, 0)
                        take(i - 1)
                        squash(i, 1)

                    later_steps(act, 1, last, step)
                    take(last)

                def finish(turn, b, n, steps):
                    act.wait_ge(s_v[1], steps)
                    if not first_of_all(turn):
                        act.wait_ge(end_dve.sem, end_dve(turn - 1, "o_sum"))
                        act.wait_ge(end_act.sem, end_act(turn - 1, "o_sq"))
                    nc.scalar.activation(osq[0:n], acc[b][0:n], ACT.Square).then_inc(end_act.sem, end_act.did("o_sq"))

                turns(act, body)
                finish(g.TILES, g.TILES % 2, P, STEPS)

            @block.vector
            def _(dve):
                link = Steps(g.sem("a_link"), dve, 1 + 6)
                link.begin(0)
                link.link(nc.vector.tensor_scalar(mask[:], g.upto[:], MASKED, None, ALU.mult))
                for a in range(2):
                    link.link(nc.vector.memset(keep[a][:, :, P:P + 1], 0.0))
                    link.link(nc.vector.memset(carry[a][:], 0.0))
                link.link(nc.vector.memset(osq[:], 0.0))
                link.link(nc.vector.memset(oss[:], 0.0))
                dve.wait_ge(s_gain, 16)

                def body(turn, b):
                    n, at, g0, last, block_of = shape(turn)

                    def walk(i, a):
                        G = g0 + i
                        dve.wait_ge(s_keep[a], G + 1)
                        after(dve, s_carry[a], G + turn + 1)
                        after(dve, s_a[a], G)
                        nc.vector.tensor_tensor_scan(flat(prod[a], n), flat(keep[a], n), flat(carry[a], n), 0.0,
                                                     ALU.mult, ALU.add).then_inc(s_scan[a], 1)
                        dve.wait_ge(s_scan[a], G + 1)
                        nc.vector.tensor_copy(carry[a][0:n, :, P:P + 1], prod[a][0:n, :, 0:1]).then_inc(s_carry[a], 1)

                    def take(i):
                        dve.wait_ge(s_t[1], g0 + i + 1)
                        after(dve, s_v[1], g0 + i)
                        nc.vector.tensor_copy(AT[1][:, :, 0:n], TR[1][:, :, 0:n]).then_inc(s_ev[1], 1)

                    for a in range(2):
                        after(dve, s_carry[a], g0 + turn)
                        nc.vector.memset(carry[a][:, :, P:P + 1], 1.0).then_inc(s_carry[a], 1)
                        dve.wait_ge(s_z[a], g0 + 1)
                        after(dve, s_beta[a], g0)
                        nc.vector.tensor_tensor(zm[a][0:n], Z[a][0:n], mask[0:n].unsqueeze(1).to_broadcast([n, HS, P]),
                                                ALU.add).then_inc(s_zm[a], 1)
                    walk(0, 0)
                    walk(0, 1)
                    before = NEW if isinstance(turn, int) and turn == 1 else P
                    if not first_of_all(turn):
                        finish_sums(turn - 1, before)

                    def step(i):
                        walk(i, 0)
                        take(i - 1)
                        walk(i, 1)

                    if not (isinstance(last, int) and last == 0):
                        step(1)
                    if not first_of_all(turn):
                        finish(turn - 1, 1 - b, before)
                    later_steps(dve, 2, last, step)
                    if not (isinstance(turn, int) and turn == g.TILES):
                        spread_queries(turn + 1, 1 - b)
                    take(last)

                def spread_queries(turn, b):
                    n, at, g0, last, block_of = shape(turn)
                    dve.wait_ge(s_q, (turn + 1) * 16)
                    spread = QZ[b][:].rearrange("p (c e) n -> p c e n", e=2)
                    for e in range(2):
                        half = slice(e * DD, (e + 1) * DD)
                        nc.vector.tensor_copy(spread[half, :, e, 0:n], q_in[half, :, 0:n]).then_inc(s_qz, 1)

                V3 = nc.vector

                def finish_sums(turn, n):
                    dve.wait_ge(end_act.sem, end_act(turn, "o_sq"))
                    V3.tensor_reduce(oss[0:n], osq[0:n], AX, ALU.add).then_inc(end_dve.sem, end_dve.did("o_sum"))
                    dve.wait_ge(end_dve.sem, end_dve(turn, "o_sum"))
                    V3.tensor_scalar(osn[0:n], oss[0:n], 1.0 / DD, EPS, ALU.mult, ALU.add).then_inc(end_dve.sem, end_dve.did("o_eps"))

                def finish(turn, b, n):
                    dve.wait_ge(end_pool.sem, end_pool(turn, "o_r"))
                    V3.tensor_tensor(o[0:n], acc[b][0:n], orr[0:n].unsqueeze(2).to_broadcast([n, H, DD]), ALU.mult).then_inc(end_dve.sem, end_dve.did("o_n"))
                    dve.wait_ge(end_dve.sem, end_dve(turn, "o_n"))
                    if not first_of_all(turn):
                        dve.wait_ge(s_out, turn * 16)
                    V3.tensor_tensor(og[0:n], o[0:n], gain[0:n].unsqueeze(1).to_broadcast([n, H, DD]), ALU.mult).then_inc(end_dve.sem, end_dve.did("o_g"))

                dve.wait_ge(s_mask, 2)
                spread_queries(0, 0)
                turns(dve, body)
                finish_sums(g.TILES, P)
                finish(g.TILES, g.TILES % 2, P)

            @block.gpsimd
            def _(pool):
                G_ = nc.gpsimd
                G_.memset(KT[:, :, NEW_BLOCK * P:(NEW_BLOCK + 1) * P], 0.0).then_inc(s_zero, 1)
                G_.memset(V[:, NEW_BLOCK, :], 0.0).then_inc(s_zero, 1)
                for b in range(2):
                    G_.memset(QZ[b][:], 0.0).then_inc(s_mask, 1)

                def body(turn, b):
                    n, at, g0, last, block_of = shape(turn)

                    def weights(i, a):
                        G = g0 + i
                        pool.wait_ge(s_scan[a], G + 1)
                        pool.wait_ge(s_beta[a], G + 1)
                        after(pool, s_t[a], G)
                        G_.tensor_tensor(A[a][0:n], prod[a][0:n, :, 1:P + 1], beta[a][0:n], ALU.mult).then_inc(s_a[a], 1)

                    def step(i):
                        weights(i, 0)
                        weights(i, 1)

                    step(0)
                    if not first_of_all(turn):
                        finish(turn - 1, NEW if isinstance(turn, int) and turn == 1 else P)
                    later_steps(pool, 1, last, step)

                def finish(turn, n):
                    pool.wait_ge(end_dve.sem, end_dve(turn, "o_eps"))
                    G_.tensor_tensor(orr[0:n], osn[0:n], g.half[0:n, 0:H], ALU.pow).then_inc(end_pool.sem, end_pool.did("o_r"))
                    if first_of_all(turn):
                        pool.wait_ge(end_pool.sem, end_pool(turn, "o_r"))

                turns(pool, body)
                finish(g.TILES, P)


def mixed(nc, g):
    D, KT, NEW, T17 = g.D, g.KT, g.NEW, g.T17
    R = g.EXPERTS + g.GROUPS_E
    s_w, s_rows = g.s_w_mixed, g.s_rows_mixed
    s_m, s_x, s_x2, s_h2, s_link = (g.sem("x_" + n) for n in ("m", "x", "x2", "h2", "link"))
    L = g.lines
    pe_a, pe_b = L["pe_a"].next_stage(T17, ["mT", "out0", "out1"]), L["pe_b"].next_stage(T17, ["hT", "router"])
    act_a, act_b = L["act_a"].next_stage(T17, ["mT", "out0", "out1"]), L["act_b"].next_stage(T17, ["sq", "sq2"])
    act_h = L["act_c"].next_stage(T17, ["hT"])
    dve_b = L["dve_b"] = L["dve_b"].next_stage(T17, ["s1", "post", "x2", "s2", "h1", "h2"])
    dve_l = L["dve_a"] = L["dve_a"].next_stage(T17, ["logits"])
    pool_b = L["pool_a"].next_stage(T17, ["r", "r2"])
    with ExitStack() as life:
        w, wr, br, post, scale, shift, gains = g.w_out, g.w_router, g.b_router, g.post, g.scale, g.shift, g.gains
        m = g.sb("x_m", [P, D], at=life)
        mT = g.sb("x_mT", [P, KT, P], at=life)
        osb = g.sb("x_o", [P, D], at=life)
        x = g.sb("x_x", [P, D], at=life)
        junk = g.sb("x_junk", [P, D], at=life)
        po = g.sb("x_po", [P, D], at=life)
        x2 = g.sb("x_x2", [P, D], at=life)
        hn = g.sb("x_hn", [P, D], at=life)
        h = g.sb("x_h", [P, D], at=life)
        hT = g.sb("x_hT", [P, KT, P], at=life)
        ss, sn, r = (g.sb("x_" + n, [P, 2], at=life) for n in ("ss", "sn", "r"))
        p_m = g.psum("x_pm", [P, KT, P], at=life)
        p_o = g.psum("x_po_", [P, D], at=life)
        p_h = g.psum("x_ph", [P, KT, P], at=life)
        p_r = g.psum("x_pr", [P, 512], at=life)

        def group_of(turn):
            return (1, NEW, slice(g.SEQ, g.TOK), g.TILES) if isinstance(turn, int) and turn == 0 else \
                (0, P, slice(g.SEQ - P, g.SEQ) if isinstance(turn, int) and turn == g.TILES else bass.ds((turn - 1) * P, P),
                 turn - 1)

        def turns(eng, body):
            for turn in range(3):
                body(turn)
            with eng.Fori(3, g.TILES + 1) as turn:
                body(turn)
            body(g.TILES + 1)
            body(g.TILES + 2)

        def there(turn):
            return not isinstance(turn, int) or 0 <= turn <= g.TILES

        HALVES = D // 512

        def later(turn, n=0):
            return not isinstance(turn, int) or turn > n

        with nc.Block() as block:
            @block.sync
            def _(sp):
                def load(turn):
                    grp, n, at, tile = group_of(turn)
                    if later(turn):
                        sp.wait_ge(pe_a.sem, pe_a(turn - 1, "mT"))
                    sp.dma_start(m[0:n], g.merged_d[at, :]).then_inc(s_m, 16)
                    if later(turn):
                        sp.wait_ge(dve_b.sem, dve_b(turn - 1, "x2"))
                    sp.dma_start(x[0:n], g.x[1] if grp else g.x[0][at, :]).then_inc(s_x, 16)

                load(0)
                with sp.Fori(1, g.TILES + 1) as turn:
                    load(turn)

            @block.tensor
            def _(pe):
                def turn_merged(turn):
                    grp, n, at, tile = group_of(turn)
                    pe.wait_ge(s_m, (turn + 1) * 16)
                    if later(turn):
                        pe.wait_ge(act_a.sem, act_a(turn - 1, "mT"))
                    for k in range(KT):
                        tr = nc.tensor.transpose(p_m[:, k, 0:n], m[0:n, k * P:(k + 1) * P], g.ident[0:n, 0:n])
                    tr.then_inc(pe_a.sem, pe_a.did("mT"))

                def project(turn, c):
                    grp, n, at, tile = group_of(turn)
                    if c == 0:
                        if not later(turn):
                            pe.wait_ge(s_w, 48)
                        pe.wait_ge(act_a.sem, act_a(turn, "mT"))
                    if later(turn):
                        pe.wait_ge(act_a.sem, act_a(turn - 1, f"out{c}"))
                    for k in range(KT):
                        mm = nc.tensor.matmul(p_o[0:n, c * 512:(c + 1) * 512], mT[:, k, 0:n], w[:, k, c * 512:(c + 1) * 512],
                                              start=(k == 0), stop=(k == KT - 1))
                    mm.then_inc(pe_a.sem, pe_a.did(f"out{c}"))

                def turn_h(turn):
                    grp, n, at, tile = group_of(turn)
                    pe.wait_ge(dve_b.sem, dve_b(turn, "h2"))
                    if later(turn):
                        pe.wait_ge(act_h.sem, act_h(turn - 1, "hT"))
                    for k in range(KT):
                        tr = nc.tensor.transpose(p_h[:, k, 0:n], h[0:n, k * P:(k + 1) * P], g.ident[0:n, 0:n])
                    tr.then_inc(pe_b.sem, pe_b.did("hT"))

                def route(turn):
                    grp, n, at, tile = group_of(turn)
                    pe.wait_ge(act_h.sem, act_h(turn, "hT"))
                    if later(turn):
                        pe.wait_ge(dve_l.sem, dve_l(turn - 1, "logits"))
                    for k in range(KT):
                        mm = nc.tensor.matmul(p_r[0:n, 0:R], hT[:, k, 0:n], wr[:, k, :], start=(k == 0), stop=(k == KT - 1))
                    mm.then_inc(pe_b.sem, pe_b.did("router"))

                def body(turn):
                    if there(turn):
                        turn_merged(turn)
                    if there(turn - 2):
                        turn_h(turn - 2)
                    if there(turn):
                        project(turn, 0)
                    if there(turn - 2):
                        route(turn - 2)
                    if there(turn):
                        project(turn, 1)

                turns(pe, body)

            @block.scalar
            def _(act):
                def take_merged(turn):
                    grp, n, at, tile = group_of(turn)
                    act.wait_ge(pe_a.sem, pe_a(turn, "mT"))
                    if later(turn):
                        act.wait_ge(pe_a.sem, pe_a(turn - 1, "out1"))
                    nc.scalar.copy(mT[:, :, 0:n], p_m[:, :, 0:n]).then_inc(act_a.sem, act_a.did("mT"))

                def take_out(turn, c):
                    grp, n, at, tile = group_of(turn)
                    act.wait_ge(pe_a.sem, pe_a(turn, f"out{c}"))
                    if later(turn):
                        act.wait_ge(dve_b.sem, dve_b(turn - 1, "post"))
                    nc.scalar.copy(osb[0:n, c * 512:(c + 1) * 512], p_o[0:n, c * 512:(c + 1) * 512]).then_inc(act_a.sem, act_a.did(f"out{c}"))

                def squares(turn):
                    grp, n, at, tile = group_of(turn)
                    act.wait_ge(act_a.sem, act_a(turn, "out1"))
                    if later(turn):
                        act.wait_ge(dve_b.sem, dve_b(turn - 1, "h1"))
                        act.wait_ge(act_b.sem, act_b(turn - 1, "sq2"))
                    nc.scalar.activation(junk[0:n], osb[0:n], ACT.Square, accum_out=ss[0:n, 0:1]).then_inc(act_b.sem, act_b.did("sq"))
                    act.wait_ge(dve_b.sem, dve_b(turn, "x2"))
                    act.wait_ge(act_b.sem, act_b(turn, "sq"))
                    nc.scalar.activation(junk[0:n], x2[0:n], ACT.Square, accum_out=ss[0:n, 1:2]).then_inc(act_b.sem, act_b.did("sq2"))
                    act.dma_start(g.x2_d[at, :], x2[0:n]).then_inc(s_x2, 16)

                def take_h(turn):
                    grp, n, at, tile = group_of(turn)
                    act.wait_ge(pe_b.sem, pe_b(turn, "hT"))
                    if later(turn):
                        act.wait_ge(pe_b.sem, pe_b(turn - 1, "router"))
                        act.wait_ge(act_h.sem, act_h(turn - 1, "hT"))
                    nc.scalar.copy(hT[:, :, 0:n], p_h[:, :, 0:n]).then_inc(act_h.sem, act_h.did("hT"))
                    act.dma_start(g.h2_d[at, :], h[0:n]).then_inc(s_h2, 16)

                def body(turn):
                    if there(turn):
                        take_merged(turn)
                    if there(turn - 2):
                        take_h(turn - 2)
                    if there(turn - 1):
                        squares(turn - 1)
                    if there(turn):
                        for c in range(HALVES):
                            take_out(turn, c)

                turns(act, body)
                act.wait_ge(s_x2, T17 * 16)
                act.wait_ge(s_h2, T17 * 16)

            @block.vector
            def _(dve):
                V = nc.vector
                link = Steps(s_link, dve, 5)
                link.begin(0)
                dve.wait_ge(s_rows, 160)
                for a in range(2):
                    link.link(V.tensor_tensor(post[a][:], post[a][:], gains[:, 0, :], ALU.mult))
                    link.link(V.scalar_tensor_tensor(out=scale[a][:], in0=scale[a][:], scalar=1.0, in1=gains[:, 1, :], op0=ALU.add, op1=ALU.mult))
                link.link(V.memset(g.logits[:], 0.0))

                def chain(turn):
                    grp, n, at, tile = group_of(turn)

                    def did(name):
                        return dve_b.sem, dve_b.did(name)

                    def after(name, t=turn):
                        dve.wait_ge(dve_b.sem, dve_b(t, name))

                    dve.wait_ge(act_b.sem, act_b(turn, "sq"))
                    if later(turn):
                        dve.wait_ge(pool_b.sem, pool_b(turn - 1, "r2"))
                    V.tensor_scalar(sn[0:n, 0:1], ss[0:n, 0:1], 1.0 / D, EPS, ALU.mult, ALU.add).then_inc(*did("s1"))
                    dve.wait_ge(pool_b.sem, pool_b(turn, "r"))
                    V.scalar_tensor_tensor(out=po[0:n], in0=osb[0:n], scalar=r[0:n, 0:1], in1=post[grp][0:n], op0=ALU.mult, op1=ALU.mult).then_inc(*did("post"))
                    after("post")
                    dve.wait_ge(s_x, (turn + 1) * 16)
                    if later(turn):
                        dve.wait_ge(s_x2, turn * 16)
                    V.tensor_tensor(x2[0:n], po[0:n], x[0:n], ALU.add).then_inc(*did("x2"))
                    dve.wait_ge(act_b.sem, act_b(turn, "sq2"))
                    V.tensor_scalar(sn[0:n, 1:2], ss[0:n, 1:2], 1.0 / D, EPS, ALU.mult, ALU.add).then_inc(*did("s2"))
                    dve.wait_ge(pool_b.sem, pool_b(turn, "r2"))
                    V.scalar_tensor_tensor(out=hn[0:n], in0=x2[0:n], scalar=r[0:n, 1:2], in1=scale[grp][0:n], op0=ALU.mult, op1=ALU.mult).then_inc(*did("h1"))
                    after("h1")
                    if later(turn):
                        dve.wait_ge(s_h2, turn * 16)
                        dve.wait_ge(pe_b.sem, pe_b(turn - 1, "hT"))
                    V.tensor_tensor(h[0:n], hn[0:n], shift[grp][0:n], ALU.add).then_inc(*did("h2"))

                def take_logits(turn):
                    grp, n, at, tile = group_of(turn)
                    dve.wait_ge(pe_b.sem, pe_b(turn, "router"))
                    V.tensor_tensor(g.logits[0:n, bass.ds(tile, 1), :].rearrange("p a c -> p (a c)"), p_r[0:n, 0:R], br[0:n], ALU.add).then_inc(dve_l.sem, dve_l.did("logits"))

                chain(0)
                chain(1)
                take_logits(0)
                with dve.Fori(2, g.TILES + 1) as turn:
                    chain(turn)
                    take_logits(turn - 1)
                take_logits(g.TILES)

            @block.gpsimd
            def _(pool):
                def body(turn):
                    grp, n, at, tile = group_of(turn)
                    pool.wait_ge(dve_b.sem, dve_b(turn, "s1"))
                    if later(turn):
                        pool.wait_ge(dve_b.sem, dve_b(turn - 1, "h1"))
                    nc.gpsimd.tensor_tensor(r[0:n, 0:1], sn[0:n, 0:1], g.half[0:n, 0:1], ALU.pow).then_inc(pool_b.sem, pool_b.did("r"))
                    pool.wait_ge(dve_b.sem, dve_b(turn, "s2"))
                    nc.gpsimd.tensor_tensor(r[0:n, 1:2], sn[0:n, 1:2], g.half[0:n, 0:1], ALU.pow).then_inc(pool_b.sem, pool_b.did("r2"))
                    if not later(turn):
                        pool.wait_ge(pool_b.sem, pool_b(turn, "r2"))

                body(0)
                with pool.Fori(1, g.TILES + 1) as turn:
                    body(turn)


def routing(nc, g):
    T17, E, GE, NEW = g.T17, g.EXPERTS, g.GROUPS_E, g.NEW
    PER = E // GE
    BIG = 1e30
    FAR = 1e6
    MOST = g.TOK // P + 1
    s_dve, s_act, s_pool, s_pe = (g.sem("r_" + n) for n in ("dve", "act", "pool", "pe"))
    s_fill, s_sc = g.sem("r_fill"), g.sem("r_sc")
    with ExitStack() as life:
        def t(name, shape, dt=F32):
            return g.sb("r_" + name, shape, dt, at=life)

        iota_g, iota_e, iota_b = t("ig", [P, GE]), t("ie", [P, E]), t("ib", [P, MOST])
        token = t("token", [P, T17], I32)
        fill = t("fill", [P, g.COLS], I32)
        valid = t("valid", [P, T17])
        gmax, gi, sg, pg = t("gmax", [P, T17]), t("gi", [P, T17]), t("sg", [P, T17]), t("pg", [P, T17])
        dg, eg, cg, ohg = (t(n, [P, T17, GE]) for n in ("dg", "eg", "cg", "ohg"))
        le, c1, c2, eq = (t(n, [P, T17, E]) for n in ("le", "c1", "c2", "eq"))
        oh = [t(f"oh{i}", [P, T17, E]) for i in range(2)]
        m1, m2, e1, e2, dm, em, den = (t(n, [P, T17]) for n in ("m1", "m2", "e1", "e2", "dm", "em", "den"))
        chosen = t("chosen", [P, T17, E])
        before = t("before", [P, T17 + 1, E])
        counts, blocks, ends, starts = (t(n, [P, E]) for n in ("counts", "blocks", "ends", "starts"))
        over = t("over", [P, E, MOST])
        place = t("place", [P, T17, E])
        sel = t("sel", [P, T17, E])
        destf = t("destf", [P, 2, T17])
        tab, tab2 = t("tab", [P, 2, T17], U32), t("tab2", [P, 2, T17], U32)
        p_rank = g.psum("r_rank", [P, 512], at=life)
        p_rank2 = g.psum("r_rank2", [P, 512], at=life)
        p_cnt = g.psum("r_cnt", [P, 512], at=life)

        def over_last(a, n):
            return a.unsqueeze(2).to_broadcast([P, a.shape[1], n])

        def over_tiles(a):
            return a.unsqueeze(1).to_broadcast([P, T17, a.shape[1]])

        mark = {}
        with nc.Block() as block:
            @block.sync
            def _(sp):
                load_expert(g, sp, 0, 0)
                load_expert(g, sp, 1, 1)

            @block.vector
            def _(dve):
                V = nc.vector
                link = Steps(s_dve, dve, 10 ** 6)
                link.begin(0)
                L = link.link
                dve.wait_ge(s_pool, 6)
                lg = g.logits[:, :, 0:GE]
                L(V.tensor_reduce(gmax[:], lg, AX, ALU.max))
                L(V.tensor_tensor(dg[:], lg, over_last(gmax[:], GE), ALU.subtract))
                mark['group'] = link.k
                L(V.tensor_scalar(cg[:], dg[:], 0.0, -FAR, ALU.is_equal, ALU.mult))
                L(V.tensor_tensor(cg[:], cg[:], over_tiles(iota_g[:]), ALU.add))
                L(V.tensor_reduce(gi[:], cg[:], AX, ALU.min))
                L(V.tensor_tensor(ohg[:], cg[:], over_last(gi[:], GE), ALU.is_equal))
                L(V.tensor_scalar(cg[:], ohg[:], -1.0, BIG, ALU.add, ALU.mult))
                L(V.tensor_tensor(le[:].rearrange("p t (g e) -> p t g e", g=GE), g.logits[:, :, GE:].rearrange("p t (g e) -> p t g e", g=GE),
                                  cg[:].unsqueeze(3).to_broadcast([P, T17, GE, PER]), ALU.add))
                for i, (top, idx) in enumerate(((m1, e1), (m2, e2))):
                    L(V.tensor_reduce(top[:], le[:], AX, ALU.max))
                    L(V.tensor_tensor(eq[:], le[:], over_last(top[:], E), ALU.is_equal))
                    L(V.tensor_scalar(c1[:], eq[:], -FAR, None, ALU.mult))
                    L(V.tensor_tensor(c1[:], c1[:], over_tiles(iota_e[:]), ALU.add))
                    L(V.tensor_reduce(idx[:], c1[:], AX, ALU.min))
                    L(V.tensor_tensor(oh[i][:], c1[:], over_last(idx[:], E), ALU.is_equal))
                    if i == 0:
                        L(V.scalar_tensor_tensor(out=le[:].rearrange("p t e -> p (t e)"), in0=oh[0][:].rearrange("p t e -> p (t e)"), scalar=-2 * BIG,
                                                 in1=le[:].rearrange("p t e -> p (t e)"), op0=ALU.mult, op1=ALU.add))
                L(V.tensor_tensor(dm[:], m2[:], m1[:], ALU.subtract))
                mark['pair'] = link.k
                L(V.tensor_tensor(chosen[:], oh[0][:], oh[1][:], ALU.add))
                L(V.tensor_tensor(chosen[:], chosen[:], over_last(valid[:], E), ALU.mult))
                L(V.memset(before[:, 0, :], 0.0))
                for tile in range(T17):
                    L(V.tensor_tensor(before[:, tile + 1, :], before[:, tile, :], chosen[:, tile, :], ALU.add))
                mark['chosen'] = link.k
                dve.wait_ge(s_act, 2)
                L(V.tensor_reduce(sg[:], eg[:], AX, ALU.add))
                L(V.reciprocal(pg[:], sg[:]))
                L(V.tensor_scalar(den[:], em[:], 1.0, None, ALU.add))
                L(V.reciprocal(den[:], den[:]))
                L(V.tensor_tensor(g.weight[:, 0, :], den[:], pg[:], ALU.mult))
                L(V.tensor_tensor(g.weight[:, 1, :], g.weight[:, 0, :], em[:], ALU.mult))
                dve.wait_ge(s_pe, 1)
                L(V.tensor_copy(counts[:], p_cnt[:, 0:E]))
                L(V.tensor_tensor(over[:], over_last(counts[:], MOST), iota_b[:].unsqueeze(1).to_broadcast([P, E, MOST]), ALU.is_gt))
                L(V.tensor_reduce(blocks[:], over[:], AX, ALU.add))
                L(V.tensor_scalar(blocks[:], blocks[:], 1.0, None, ALU.max))
                L(V.tensor_tensor_scan(ends[:], g.ones[:, 0:E], blocks[:], 0.0, ALU.mult, ALU.add))
                L(V.tensor_tensor(starts[:], ends[:], blocks[:], ALU.subtract))
                L(V.memset(g.bounds[:], 0.0))
                L(V.tensor_copy(g.bounds[:, 1:E + 1], ends[0:1, :]))
                L(V.tensor_scalar(starts[:], starts[:], float(P), -1.0, ALU.mult, ALU.add))
                L(V.tensor_tensor(place[:, 0:16, :], p_rank[:].rearrange("p (t e) -> p t e", e=E), starts[:].unsqueeze(1).to_broadcast([P, 16, E]), ALU.add))
                L(V.tensor_tensor(place[:, 16, :], p_rank2[:, 0:E], starts[:], ALU.add))
                for i in range(2):
                    L(V.tensor_tensor(sel[:], oh[i][:], place[:], ALU.mult))
                    L(V.tensor_reduce(destf[:, i, :], sel[:], AX, ALU.add))
                L(V.tensor_copy(g.dest[:], destf[:]))
                L(V.tensor_single_scalar(tab[:], g.dest[:], P - 1, ALU.bitwise_and))
                L(V.tensor_single_scalar(tab2[:], g.dest[:], 7, ALU.logical_shift_right))
                L(V.tensor_scalar(tab[:], tab[:], float(g.COLS), None, ALU.mult))
                L(V.tensor_tensor(g.slot[:], tab[:], tab2[:], ALU.add))
                mark['places'] = link.k

            @block.gpsimd
            def _(pool):
                G = nc.gpsimd
                G.iota(iota_g[:], pattern=[[1, GE]], base=0, channel_multiplier=0, allow_small_or_imprecise_dtypes=True).then_inc(s_pool, 1)
                G.iota(iota_e[:], pattern=[[1, E]], base=0, channel_multiplier=0, allow_small_or_imprecise_dtypes=True).then_inc(s_pool, 1)
                G.iota(iota_b[:], pattern=[[P, MOST]], base=0, channel_multiplier=0, allow_small_or_imprecise_dtypes=True).then_inc(s_pool, 1)
                G.iota(token[:], pattern=[[P, T17]], base=0, channel_multiplier=1).then_inc(s_pool, 1)
                G.iota(fill[:], pattern=[[0, g.COLS]], base=g.TOK, channel_multiplier=0).then_inc(s_pool, 1)
                G.affine_select(out=valid[:], in_=g.ones[:, 0:T17], compare_op=ALU.is_gt, fill=0.0, base=g.TOK,
                                pattern=[[-P, T17]], channel_multiplier=-1).then_inc(s_pool, 1)
                pool.wait_ge(s_pool, 6)
                pool.dma_start(g.token_d, fill[:]).then_inc(s_fill, 16)
                pool.wait_ge(s_fill, 16)
                pool.wait_ge(s_dve, mark['places'])
                table = g.token_d.rearrange("p (b o) -> (p b) o", o=1)
                for tile in range(T17):
                    n = NEW if tile == g.TILES else P
                    for i in range(2):
                        G.indirect_dma_start(out=table, out_offset=bass.IndirectOffsetOnAxis(ap=g.slot[0:n, i, tile:tile + 1], axis=0),
                                             in_=token[0:n, tile:tile + 1], in_offset=None).then_inc(s_sc, 16)
                pool.wait_ge(s_sc, 32 * T17)

            @block.scalar
            def _(act):
                act.wait_ge(s_dve, mark['group'])
                nc.scalar.activation(eg[:], dg[:], ACT.Exp).then_inc(s_act, 1)
                act.wait_ge(s_dve, mark['pair'])
                nc.scalar.activation(em[:], dm[:], ACT.Exp).then_inc(s_act, 1)

            @block.tensor
            def _(pe):
                pe.wait_ge(s_dve, mark['chosen'])
                for out, a, b in ((p_rank, 0, 16), (p_rank2, 16, T17)):
                    n = (b - a) * E
                    nc.tensor.matmul(out[:, 0:n], g.upto[:], chosen[:, a:b, :].rearrange("p t e -> p (t e)"), start=True, stop=False)
                    nc.tensor.matmul(out[:, 0:n], g.ones[:], before[:, a:b, :].rearrange("p t e -> p (t e)"), start=False, stop=True)
                nc.tensor.matmul(p_cnt[:, 0:E], g.ones[:], before[:, T17, :], start=True, stop=True).then_inc(s_pe, 1)


def load_expert(g, sp, e, buf):
    wg, wu, wd = g.expert_w
    s_wg, s_wd = g.s_expert
    for w, src in ((wg, "w_gate"), (wu, "w_up")):
        sp.dma_start(w[:, buf], g.ins[src][0, bass.ds(e, 1)].rearrange("a (k p) f -> p (a k) f", p=P)).then_inc(s_wg[buf], 16)
    sp.dma_start(wd[:, buf], g.ins["w_down"][0, bass.ds(e, 1)].rearrange("a (k p) d -> p (a k) d", p=P)).then_inc(s_wd[buf], 16)


def experts(nc, g):
    D, KT, E = g.D, g.KT, g.EXPERTS
    F = g.ins["w_gate"].shape[3]
    FT = F // P
    s_wg, s_wd = g.s_expert
    s_tab, s_stored = g.sem("e_tab"), g.sem("e_stored")
    s_idx, s_started, s_x, s_y = g.sem("e_idx"), g.sem("e_started"), g.sem("e_x"), g.sem("e_y")
    s_xt, s_gate, s_up, s_ht, s_down = [g.sem("e_xt0"), g.sem("e_xt1")], *(g.sem("e_" + n) for n in ("gate", "up", "ht", "down"))
    s_silu, s_h, s_hTs, s_xe0, s_xe1, s_ye0, s_ye1 = (g.sem("e_" + n) for n in ("silu", "h", "hTs", "xe0", "xe1", "ye0", "ye1"))
    HALF = KT // 2
    with ExitStack() as life:
        wg, wu, wd = g.expert_w
        table = g.sb("e_table", [P, g.COLS], I32, at=life)
        idx = g.sb("e_idx_", [P, 1], U32, at=life)
        x = g.sb("e_x_", [P, D], at=life)
        xT = g.sb("e_xT", [P, KT, P], at=life)
        sg = g.sb("e_sg", [P, F], at=life)
        h = g.sb("e_h_", [P, F], at=life)
        hT = g.sb("e_hT", [P, FT, P], at=life)
        y = g.sb("e_y_", [P, D], at=life)
        p_x = [g.psum(f"e_px{i}", [P, HALF, P], at=life) for i in range(2)]
        p_g = g.psum("e_pg", [P, F], at=life)
        p_u = g.psum("e_pu", [P, F], at=life)
        p_h = g.psum("e_ph", [P, FT, P], at=life)
        p_y = [g.psum(f"e_py{i}", [P, D // 2], at=life) for i in range(2)]

        def bound(eng, e):
            return eng.value_load(g.bounds[0:1, bass.ds(e, 1)], min_val=0, max_val=g.BLOCKS)

        def blocks_of(eng, e, body):
            first, last = bound(eng, e), bound(eng, e + 1)
            with eng.Fori(first, last) as b:
                body(b)

        with nc.Block() as block:
            @block.sync
            def _(sp):
                sp.dma_start(table[:], g.token_d).then_inc(s_tab, 16)

                with sp.Fori(1, E // 2) as pair:
                    for buf in range(2):
                        sp.wait_ge(s_down, bound(sp, pair * 2 + buf - 1))
                        load_expert(g, sp, pair * 2 + buf, buf)

            @block.gpsimd
            def _(pool):
                with pool.Fori(0, bound(pool, E) + 1) as b:
                    pool.wait_ge(s_idx, b + 1)
                    pool.sem_inc(s_started, 1)
                    nc.gpsimd.indirect_dma_start(out=x[:], out_offset=None, in_=g.h2_d,
                                                 in_offset=bass.IndirectOffsetOnAxis(ap=idx[:], axis=0)).then_inc(s_x, 16)

            @block.tensor
            def _(pe):
                def turn_rows(b, half):
                    if half == 0:
                        pe.wait_ge(s_x, b * 16 + 16)
                    for k in range(half * HALF, (half + 1) * HALF):
                        tr = nc.tensor.transpose(p_x[half][:, k % HALF, :], x[:, k * P:(k + 1) * P], g.ident[:])
                    tr.then_inc(s_xt[half], 1)

                turn_rows(0, 0)
                turn_rows(0, 1)

                def multiply(pair, buf, b):
                    pe.wait_ge(s_wg[buf], pair * 32 + 32)
                    pe.wait_ge(s_xe0, b + 1)
                    pe.wait_ge(s_xe1, b + 1)
                    for out, w, done in ((p_g, wg, s_gate), (p_u, wu, s_up)):
                        for k in range(KT):
                            mm = nc.tensor.matmul(out[:], xT[:, k, :], w[:, buf, k, :], start=(k == 0), stop=(k == KT - 1))
                        mm.then_inc(done, 1)
                    turn_rows(b + 1, 0)
                    pe.wait_ge(s_h, b + 1)
                    for f in range(FT):
                        tr = nc.tensor.transpose(p_h[:, f, :], h[:, f * P:(f + 1) * P], g.ident[:])
                    tr.then_inc(s_ht, 1)
                    turn_rows(b + 1, 1)
                    pe.wait_ge(s_wd[buf], pair * 16 + 16)
                    pe.wait_ge(s_hTs, b + 1)
                    for c in range(2):
                        for f in range(FT):
                            mm = nc.tensor.matmul(p_y[c][:], hT[:, f, :], wd[:, buf, f, c * (D // 2):(c + 1) * (D // 2)],
                                                  start=(f == 0), stop=(f == FT - 1))
                    mm.then_inc(s_down, 1)

                with pe.Fori(0, E // 2) as pair:
                    for buf in range(2):
                        blocks_of(pe, pair * 2 + buf, lambda b: multiply(pair, buf, b))

            @block.scalar
            def _(act):
                def take_x(b):
                    act.wait_ge(s_xt[0], b + 1)
                    nc.scalar.copy(xT[:, 0:HALF, :], p_x[0][:]).then_inc(s_xe0, 1)

                take_x(0)

                def body(b):
                    act.wait_ge(s_gate, b + 1)
                    nc.scalar.activation(sg[:], p_g[:], ACT.Silu).then_inc(s_silu, 1)
                    act.wait_ge(s_up, b + 1)
                    take_x(b + 1)
                    act.wait_ge(s_ht, b + 1)
                    nc.scalar.copy(hT[:], p_h[:]).then_inc(s_hTs, 1)
                    if not isinstance(b, int):
                        act.wait_ge(s_y, b * 16)
                    act.wait_ge(s_down, b + 1)
                    nc.scalar.copy(y[:, 0:D // 2], p_y[0][:]).then_inc(s_ye0, 1)
                    act.wait_ge(s_ye0, b + 1)
                    act.wait_ge(s_ye1, b + 1)
                    act.dma_start(g.y_d[bass.ds(b * P, P), :], y[:]).then_inc(s_y, 16)

                body(0)
                with act.Fori(1, bound(act, E)) as b:
                    body(b)
                act.wait_ge(s_y, bound(act, E) * 16)
                act.sem_inc(s_stored, 1)

            @block.vector
            def _(dve):
                def take_x(b):
                    dve.wait_ge(s_xt[1], b + 1)
                    nc.vector.tensor_copy(xT[:, HALF:, :], p_x[1][:]).then_inc(s_xe1, 1)

                def name_rows(b):
                    nc.vector.tensor_scalar(idx[:], table[:, bass.ds(b, 1)], 0.0, None, ALU.add).then_inc(s_idx, 1)

                dve.wait_ge(s_tab, 16)
                name_rows(0)
                take_x(0)
                dve.wait_ge(s_idx, 1)
                name_rows(1)

                def body(b):
                    dve.wait_ge(s_silu, b + 1)
                    dve.wait_ge(s_up, b + 1)
                    nc.vector.tensor_tensor(h[:], sg[:], p_u[:], ALU.mult).then_inc(s_h, 1)
                    take_x(b + 1)
                    dve.wait_ge(s_idx, b + 2)
                    name_rows(b + 2)
                    if not isinstance(b, int):
                        dve.wait_ge(s_y, b * 16)
                    dve.wait_ge(s_down, b + 1)
                    nc.vector.tensor_copy(y[:, D // 2:], p_y[1][:]).then_inc(s_ye1, 1)

                body(0)
                with dve.Fori(1, bound(dve, E)) as b:
                    body(b)


def combine(nc, g):
    D, NEW, LAST = g.D, g.NEW, g.TILES
    GT = 5
    s_rows, s_idx, s_started, s_link = (g.sem("o_" + n) for n in ("rows", "idx", "started", "link"))
    s_y = [[g.sem(f"o_y{b}{i}") for i in range(2)] for b in range(2)]
    s_x2, s_out = [g.sem(f"o_x2{b}") for b in range(2)], [g.sem(f"o_out{b}") for b in range(2)]
    by_sum = g.lines["dve_a"].next_stage(g.T17, ["w0", "w1"])
    by_norm = g.lines["dve_b"].next_stage(g.T17, ["mean", "gated", "out"])
    s_sq, s_r = g.sem("o_sq"), g.sem("o_r")
    with ExitStack() as life:
        def pair(name, shape, dt=F32):
            return [g.sb(f"o_{name}{b}", shape, dt, at=life) for b in range(2)]

        post = pair("post", [P, D])
        gain = g.sb("o_gain", [P, D], at=life)
        idx = pair("idx", [P, 2], U32)
        rows = pair("rows", [P, 2, D])
        t1, x2, out, ss = pair("t1", [P, D]), pair("x2_", [P, D]), pair("out_", [P, D]), pair("ss", [P, 1])
        t0, junk, gated = (g.sb("o_" + n, [P, D], at=life) for n in ("t0", "junk", "gated"))
        sn, r = (g.sb("o_" + n, [P, 1], at=life) for n in ("sn", "rr"))

        def shape(turn):
            first = isinstance(turn, int) and turn == 0
            return (NEW if first else P), (g.TILES if first else turn - 1), \
                (slice(g.SEQ, g.TOK) if first else bass.ds((turn - 1) * P, P))

        def turns(eng, body):
            for turn in range(3):
                body(turn, turn % 2, turn // 2)
            with eng.Fori(1, (LAST - 2) // 2) as p:
                body(2 * p + 1, 1, p)
                body(2 * p + 2, 0, p + 1)
            for turn in range(LAST - 1, LAST + 1):
                body(turn, turn % 2, turn // 2)

        def there(turn):
            return not isinstance(turn, int) or 0 <= turn <= LAST

        def reg(value):
            return not isinstance(value, int) or value > 0

        with nc.Block() as block:
            @block.sync
            def _(sp):
                for a in range(2):
                    sp.dma_start(post[a][:], g.mod_d[a, GT * D:(GT + 1) * D].partition_broadcast(P)).then_inc(s_rows, 16)
                sp.dma_start(gain[:], g.ins["g_post_ffn"][0].partition_broadcast(P)).then_inc(s_rows, 16)

                def body(turn, b, use):
                    n, tile, at = shape(turn)
                    if reg(use):
                        sp.wait_ge(by_norm.sem, by_norm(turn - 2, "out"))
                    sp.dma_start(x2[b][0:n], g.x2_d[at, :]).then_inc(s_x2[b], 16)

                turns(sp, body)

            @block.gpsimd
            def _(pool):
                def gather(turn, b, use):
                    n, tile, at = shape(turn)
                    if reg(use):
                        pool.wait_ge(by_sum.sem, by_sum(turn - 2, "w1"))
                    pool.wait_ge(s_idx, turn + 1)
                    pool.sem_inc(s_started, 1)
                    for i in range(2):
                        nc.gpsimd.indirect_dma_start(out=rows[b][0:n, i, :], out_offset=None, in_=g.y_d,
                                                     in_offset=bass.IndirectOffsetOnAxis(ap=idx[b][0:n, i:i + 1], axis=0)).then_inc(s_y[b][i], 16)

                gather(0, 0, 0)
                gather(1, 1, 0)

                def body(turn, b, use):
                    n, tile, at = shape(turn)
                    if there(turn + 2):
                        gather(turn + 2, b, use + 1)
                    pool.wait_ge(by_norm.sem, by_norm(turn, "mean"))
                    nc.gpsimd.tensor_tensor(r[0:n], sn[0:n], g.half[0:n, 0:1], ALU.pow).then_inc(s_r, 1)
                    if isinstance(turn, int) and turn == 0:
                        pool.wait_ge(s_r, 1)

                turns(pool, body)

            @block.scalar
            def _(act):
                def store(turn, b):
                    n, tile, at = shape(turn)
                    act.wait_ge(by_norm.sem, by_norm(turn, "out"))
                    dst = g.outs["y_sample"] if isinstance(turn, int) and turn == 0 else g.outs["y_prompt"][at, :]
                    act.dma_start(dst, out[b][0:n]).then_inc(s_out[b], 16)

                def body(turn, b, use):
                    n, tile, at = shape(turn)
                    act.wait_ge(by_sum.sem, by_sum(turn, "w1"))
                    if reg(use):
                        act.wait_ge(by_norm.sem, by_norm(turn - 2, "mean"))
                    if reg(turn):
                        act.wait_ge(s_sq, turn)
                    nc.scalar.activation(junk[0:n], t1[b][0:n], ACT.Square, accum_out=ss[b][0:n]).then_inc(s_sq, 1)
                    if reg(turn):
                        store(turn - 1, 1 - b)

                turns(act, body)
                store(LAST, LAST % 2)
                act.wait_ge(s_out[0], (LAST // 2 + 1) * 16)
                act.wait_ge(s_out[1], (LAST // 2) * 16)

            @block.vector
            def _(dve):
                V = nc.vector
                link = Steps(s_link, dve, 2)
                link.begin(0)

                def name_rows(turn, b):
                    n, tile, at = shape(turn)
                    V.tensor_scalar(idx[b][:], g.dest[:, :, bass.ds(tile, 1)].rearrange("p i a -> p (i a)"), 0.0, None, ALU.add).then_inc(s_idx, 1)

                def norm(turn, b, use):
                    n, tile, at = shape(turn)
                    grp = 1 if isinstance(turn, int) and turn == 0 else 0
                    dve.wait_ge(s_sq, turn + 1)
                    V.tensor_scalar(sn[0:n], ss[b][0:n], 1.0 / D, EPS, ALU.mult, ALU.add).then_inc(by_norm.sem, by_norm.did("mean"))
                    dve.wait_ge(s_r, turn + 1)
                    if reg(turn):
                        dve.wait_ge(by_norm.sem, by_norm(turn - 1, "out"))
                    V.scalar_tensor_tensor(out=gated[0:n], in0=t1[b][0:n], scalar=r[0:n, 0:1], in1=post[grp][0:n],
                                           op0=ALU.mult, op1=ALU.mult).then_inc(by_norm.sem, by_norm.did("gated"))
                    dve.wait_ge(by_norm.sem, by_norm(turn, "gated"))
                    dve.wait_ge(s_x2[b], (use + 1) * 16)
                    if reg(use):
                        dve.wait_ge(s_out[b], use * 16)
                    V.tensor_tensor(out[b][0:n], gated[0:n], x2[b][0:n], ALU.add).then_inc(by_norm.sem, by_norm.did("out"))

                def body(turn, b, use):
                    n, tile, at = shape(turn)
                    if reg(turn):
                        dve.wait_ge(by_sum.sem, by_sum(turn - 1, "w1"))
                    dve.wait_ge(s_y[b][0], (use + 1) * 16)
                    V.tensor_scalar(t0[0:n], rows[b][0:n, 0, :], g.weight[0:n, 0, bass.ds(tile, 1)], None, ALU.mult).then_inc(by_sum.sem, by_sum.did("w0"))
                    dve.wait_ge(s_y[b][1], (use + 1) * 16)
                    dve.wait_ge(by_sum.sem, by_sum(turn, "w0"))
                    V.scalar_tensor_tensor(out=t1[b][0:n], in0=rows[b][0:n, 1, :], scalar=g.weight[0:n, 1, bass.ds(tile, 1)], in1=t0[0:n],
                                           op0=ALU.mult, op1=ALU.add).then_inc(by_sum.sem, by_sum.did("w1"))
                    if there(turn + 2):
                        name_rows(turn + 2, b)
                    if reg(turn):
                        norm(turn - 1, 1 - b, use if b else use - 1)

                name_rows(0, 0)
                name_rows(1, 1)
                dve.wait_ge(s_rows, 48)
                for a in range(2):
                    link.link(V.tensor_tensor(post[a][:], post[a][:], gain[:], ALU.mult))
                turns(dve, body)
                norm(LAST, LAST % 2, LAST // 2)


_OUTS = [("y_prompt", (1, 2048, 1024)), ("y_sample", (1, 32, 1024)),
         ("k_prompt", (1, 1, 2048, 8, 64)), ("v_prompt", (1, 1, 2048, 8, 64)),
         ("delta_prompt", (1, 1, 4, 128, 128)), ("conv_prompt", (1, 1, 3, 1536)),
         ("k_sample", (1, 1, 32, 8, 64)), ("v_sample", (1, 1, 32, 8, 64)),
         ("delta_sample", (1, 1, 4, 128, 128)), ("conv_sample", (1, 1, 3, 1536))]


def _flat(name, ap):
    if name[0] == "y":
        return ap.rearrange("a t d -> (a t) d")
    if name[0] in "kv":
        return ap.rearrange("l b t h d -> (l b t) (h d)")
    if name[0] == "d":
        return ap.rearrange("l b h k v -> (l b h) k v")
    return ap.rearrange("l b t c -> (l b t) c")


def kernel(**inputs):
    import numpy as _np
    import concourse.bacc as _bacc
    from concourse import mybir as _mybir
    from concourse.bass_utils import run_bass_kernel_spmd as _run

    nc = _bacc.Bacc("TRN2", target_bir_lowering=False, num_devices=1)
    arrays, ins, outs = {}, {}, {}
    for name, value in inputs.items():
        a = _np.ascontiguousarray(value)
        arrays[f"in_{name}"] = a
        ins[name] = nc.dram_tensor(f"in_{name}", a.shape, _mybir.dt.from_np(a.dtype), kind="ExternalInput").ap()
    for name, shape in _OUTS:
        outs[name] = _flat(name, nc.dram_tensor(f"out_{name}", shape, _mybir.dt.float32, kind="ExternalOutput").ap())
    build(nc, ins, outs)
    r = _run(nc, [arrays], core_ids=[0])
    return tuple(r.results[0][f"out_{name}"] for name, _ in _OUTS)
```
